# Optimizing a Trainium2 kernel written in Bass

```python
import math
import jax, jax.numpy as jnp
from jax import lax
import numpy as np

D_MODEL = 1024
BATCH = 1
SEQ = 256
DEPTH = 2
DEC_BATCH = 8
DEC_SEQ = 8
PAST_LEN = 256
PAGE_SIZE = 128

N_A = (DEPTH + 1) // 2
N_C = DEPTH // 2
D_A = D_MODEL // 2
H_A = 4
DH_A = D_A // H_A
MLSTM_CHUNK = 64
D_B = D_MODEL // 2
CONV_GROUPS = 8
CONV_W = 3
A_SPLITS = (D_A, 2 * D_A, 3 * D_A, 4 * D_A, 4 * D_A + H_A, 4 * D_A + 2 * H_A,
            4 * D_A + 2 * H_A + D_B, 4 * D_A + 2 * H_A + 2 * D_B)
A_COLS = 4 * D_A + 2 * H_A + 3 * D_B
H_C = 8
DH_C = D_MODEL // (2 * H_C)
D_C = 2 * H_C * DH_C
Q_BLOCK = 128
ROPE_THETA = 10000.0
N_MEM = 256
H_M = 4
DH_M = D_MODEL // H_M
N_GROUPS = 4
E_PER_GROUP = 8
TOP_K_IN_GROUP = 2
D_FF_EXPERT = D_MODEL // 4
EPS = 1e-6

kernel_name = "hybrid_mlstm_shortconv_diffattn_hmoe_step"

def rms_norm(x, g):
    xf = x.astype(jnp.float32)
    y = xf * lax.rsqrt(jnp.mean(xf * xf, axis=-1, keepdims=True) + EPS)
    return (y * g.astype(jnp.float32)).astype(x.dtype)

def rope(x, pos):
    half = x.shape[-1] // 2
    inv_freq = jnp.exp(-math.log(ROPE_THETA) * jnp.arange(half, dtype=jnp.float32) / half)
    ang = pos.astype(jnp.float32)[:, None] * inv_freq[None, :]
    bshape = (1, pos.shape[0]) + (1,) * (x.ndim - 3) + (half,)
    cos = jnp.cos(ang).reshape(bshape)
    sin = jnp.sin(ang).reshape(bshape)
    xf = x.astype(jnp.float32)
    x1, x2 = xf[..., :half], xf[..., half:]
    return jnp.concatenate([x1 * cos - x2 * sin, x2 * cos + x1 * sin], axis=-1).astype(x.dtype)

def mlstm_chunk(state, q, k, v, ig, lf):
    c0, n0, m0 = state
    L = q.shape[2]
    b = jnp.cumsum(lf, axis=-1)
    causal = jnp.tril(jnp.ones((L, L), dtype=bool))
    log_d = jnp.where(causal, b[..., :, None] - b[..., None, :] + ig[..., None, :], -jnp.inf)
    log_inter = b + m0[..., None]
    m_t = jnp.maximum(log_inter, jnp.max(log_d, axis=-1))
    d = jnp.exp(log_d - m_t[..., None])
    inter = jnp.exp(log_inter - m_t)
    s = jnp.einsum('bhtd,bhsd->bhts', q, k) * d
    num = jnp.einsum('bhts,bhsd->bhtd', s, v) + inter[..., None] * jnp.einsum('bhvk,bhtk->bhtv', c0, q)
    den = jnp.sum(s, axis=-1) + inter * jnp.einsum('bhk,bhtk->bht', n0, q)
    h = num / jnp.maximum(jnp.abs(den), jnp.exp(-m_t))[..., None]
    m_new = m_t[..., -1]
    w_last = d[..., -1, :]
    decay = inter[..., -1]
    c_new = decay[..., None, None] * c0 + jnp.einsum('bhsv,bhsk->bhvk', v * w_last[..., None], k)
    n_new = decay[..., None] * n0 + jnp.einsum('bhs,bhsk->bhk', w_last, k)
    return (c_new, n_new, m_new), h

def mlstm_conv_mixer(xn, w_in, gate_b, head_g, conv_w, w_out, state, conv_buf):
    f32 = jnp.float32
    B, T, _ = xn.shape
    z = xn @ w_in
    q, k, v, o, ig, fg, gb, gc, hb = jnp.split(z, A_SPLITS, axis=-1)

    def heads(t):
        return t.reshape(B, T, H_A, DH_A).transpose(0, 2, 1, 3).astype(f32)

    qh, kh, vh = heads(q), heads(k) * (DH_A ** -0.5), heads(v)
    gate_b = gate_b.astype(f32)
    igh = (ig.astype(f32) + gate_b[0]).transpose(0, 2, 1)
    lfh = jax.nn.log_sigmoid(fg.astype(f32) + gate_b[1]).transpose(0, 2, 1)
    if state is None:
        nc = T // MLSTM_CHUNK

        def chunks(t):
            return jnp.moveaxis(t.reshape(t.shape[:2] + (nc, MLSTM_CHUNK) + t.shape[3:]), 2, 0)

        state0 = (jnp.zeros((B, H_A, DH_A, DH_A), f32), jnp.zeros((B, H_A, DH_A), f32), jnp.zeros((B, H_A), f32))
        new_state, hs = lax.scan(lambda st, inp: mlstm_chunk(st, *inp), state0,
                                 (chunks(qh), chunks(kh), chunks(vh), chunks(igh), chunks(lfh)))
        h = jnp.moveaxis(hs, 0, 2).reshape(B, H_A, T, DH_A)
    else:
        st = (state[0].astype(f32), state[1].astype(f32), state[2].astype(f32))
        new_state, h = mlstm_chunk(st, qh, kh, vh, igh, lfh)
    h = h.transpose(0, 2, 1, 3)
    h = h * lax.rsqrt(jnp.mean(h * h, axis=-1, keepdims=True) + EPS) * head_g.astype(f32).reshape(H_A, DH_A)
    y_a = (jax.nn.sigmoid(o.astype(f32)) * h.reshape(B, T, D_A)).astype(xn.dtype)
    u = gc * hb
    prefix = jnp.zeros((B, CONV_W - 1, D_B), u.dtype) if conv_buf is None else conv_buf.astype(u.dtype)
    up = jnp.concatenate([prefix, u], axis=1)
    conv = up[:, 0:T] * conv_w[0]
    for j in range(1, CONV_W):
        conv = conv + up[:, j:j + T] * conv_w[j]
    y_b = gb * conv
    new_buf = up[:, -(CONV_W - 1):]
    y = jnp.concatenate([y_a, y_b], axis=-1) @ w_out
    return y, new_state, new_buf

def diff_softmax_mix(q, k, v, mask, lam, scale):
    s = jnp.einsum('bqhmd,bkhmd->bhmqk', q, k).astype(jnp.float32) * scale
    s = jnp.where(mask, s, -jnp.inf)
    p = jax.nn.softmax(s, axis=-1)
    a = p[:, :, 0] - lam * p[:, :, 1]
    return jnp.einsum('bhqk,bkhe->bqhe', a.astype(v.dtype), v)

def diff_attention(xn, w_qkv, lam_vecs, subln_g, w_out, layer_idx, past):
    B, T, _ = xn.shape
    q, k, v = jnp.split(xn @ w_qkv, 3, axis=-1)
    q = q.reshape(B, T, H_C, 2, DH_C)
    k = k.reshape(B, T, H_C, 2, DH_C)
    v = v.reshape(B, T, H_C, 2 * DH_C)
    offset = 0 if past is None else PAST_LEN
    pos = offset + jnp.arange(T)
    q = rope(q, pos)
    k = rope(k, pos)
    lam_init = 0.8 - 0.6 * math.exp(-0.3 * layer_idx)
    lv = lam_vecs.astype(jnp.float32)
    lam = jnp.exp(jnp.sum(lv[0] * lv[1])) - jnp.exp(jnp.sum(lv[2] * lv[3])) + lam_init
    scale = DH_C ** -0.5
    if past is None:
        nb = T // Q_BLOCK
        qb = jnp.moveaxis(q.reshape(B, nb, Q_BLOCK, H_C, 2, DH_C), 1, 0)
        k_pos = jnp.arange(T)

        def one_block(args):
            qi, bi = args
            q_pos = bi * Q_BLOCK + jnp.arange(Q_BLOCK)
            return diff_softmax_mix(qi, k, v, k_pos[None, :] <= q_pos[:, None], lam, scale)

        o = lax.map(one_block, (qb, jnp.arange(nb)))
        o = jnp.moveaxis(o, 0, 1).reshape(B, T, H_C, 2 * DH_C)
    else:
        k_past, v_past = past
        k_all = jnp.concatenate([k_past.astype(k.dtype), k], axis=1)
        v_all = jnp.concatenate([v_past.astype(v.dtype), v], axis=1)
        k_pos = jnp.arange(k_all.shape[1])
        mask = k_pos[None, :] <= pos[:, None]
        o = diff_softmax_mix(q, k_all, v_all, mask, lam, scale)
    o = rms_norm(o, subln_g) * (1.0 - lam_init)
    y = o.reshape(B, T, D_C) @ w_out
    return y, k, v

def mem_attention(xn, mem_k, mem_v, w_q, w_o):
    B, T, _ = xn.shape
    q = (xn @ w_q).reshape(B, T, H_M, DH_M)
    s = jnp.einsum('bqhd,bmhd->bhqm', q, mem_k).astype(jnp.float32) * (DH_M ** -0.5)
    p = jax.nn.softmax(s, axis=-1)
    o = jnp.einsum('bhqm,bmhd->bqhd', p.astype(mem_v.dtype), mem_v)
    return o.reshape(B, T, D_MODEL) @ w_o

def hier_moe(xn, w_rg, b_rg, w_re, b_re, w_gate, w_up, w_down):
    f32 = jnp.float32
    B, T, D = xn.shape
    x = xn.reshape(B * T, D)
    g_logits = (x @ w_rg).astype(f32) + b_rg.astype(f32)
    g_prob = jax.nn.softmax(g_logits, axis=-1)
    g_sel = jnp.argmax(g_logits, axis=-1)
    g_w = jnp.take_along_axis(g_prob, g_sel[:, None], axis=-1)
    e_logits = ((x @ w_re).astype(f32) + b_re.astype(f32)).reshape(-1, N_GROUPS, E_PER_GROUP)
    e_logits = jnp.take_along_axis(e_logits, g_sel[:, None, None], axis=1)[:, 0]
    e_prob = jax.nn.softmax(e_logits, axis=-1)
    top_v, top_i = lax.top_k(e_prob, TOP_K_IN_GROUP)
    top_v = top_v / jnp.sum(top_v, axis=-1, keepdims=True)
    e_w = jnp.sum(jax.nn.one_hot(top_i, E_PER_GROUP, dtype=f32) * top_v[..., None], axis=1)
    gate = jax.nn.one_hot(g_sel, N_GROUPS, dtype=f32)[:, :, None] * (g_w * e_w)[:, None, :]
    y = jnp.zeros_like(x)
    for g in range(N_GROUPS):
        h = jax.nn.silu(jnp.einsum('nd,edf->nef', x, w_gate[g])) * jnp.einsum('nd,edf->nef', x, w_up[g])
        y = y + jnp.einsum('nef,efd->nd', h * gate[:, g, :, None].astype(h.dtype), w_down[g])
    return y.reshape(B, T, D)

def trunk(x, mem_k, mem_v, st_c, st_n, st_m, st_conv, cache_k, cache_v, page_table, p):
    is_prompt = st_c is None
    out_c, out_n, out_m, out_conv, out_k, out_v = [], [], [], [], [], []
    ia = 0
    ic = 0
    for layer in range(DEPTH):
        h = rms_norm(x, p['norm_mix_g'][layer])
        if layer % 2 == 0:
            state = None if is_prompt else (st_c[ia], st_n[ia], st_m[ia])
            buf = None if is_prompt else st_conv[ia]
            y, (c_new, n_new, m_new), buf_new = mlstm_conv_mixer(
                h, p['w_in_a'][ia], p['gate_b_a'][ia], p['head_norm_g_a'][ia], p['conv_w_b'][ia],
                p['w_out_a'][ia], state, buf)
            out_c.append(c_new.astype(x.dtype))
            out_n.append(n_new.astype(x.dtype))
            out_m.append(m_new.astype(x.dtype))
            out_conv.append(buf_new)
            ia += 1
        else:
            if is_prompt:
                past = None
            else:
                nb, npg = page_table.shape
                k_past = cache_k[ic, page_table].reshape(nb, npg * PAGE_SIZE, H_C, 2, DH_C)
                v_past = cache_v[ic, page_table].reshape(nb, npg * PAGE_SIZE, H_C, 2 * DH_C)
                past = (k_past, v_past)
            y, k_new, v_new = diff_attention(h, p['w_qkv_c'][ic], p['lambda_c'][ic], p['subln_g_c'][ic],
                                             p['w_out_c'][ic], layer, past)
            out_k.append(k_new)
            out_v.append(v_new)
            ic += 1
        x = x + y
        x = x + mem_attention(rms_norm(x, p['norm_mem_g'][layer]), mem_k[layer], mem_v[layer],
                              p['w_mem_q'][layer], p['w_mem_o'][layer])
        x = x + hier_moe(rms_norm(x, p['norm_ffn_g'][layer]), p['w_router_g'][layer], p['b_router_g'][layer],
                         p['w_router_e'][layer], p['b_router_e'][layer], p['w_exp_gate'][layer],
                         p['w_exp_up'][layer], p['w_exp_down'][layer])
    y = rms_norm(x, p['final_norm_g'])
    return y, (jnp.stack(out_c), jnp.stack(out_n), jnp.stack(out_m), jnp.stack(out_conv),
               jnp.stack(out_k), jnp.stack(out_v))

def setup_inputs(seed: int = 0) -> dict:
    key = jax.random.key(seed)
    keys = list(jax.random.split(key, 48))

    def nrm(shape, scale=1.0):
        return scale * jax.random.normal(keys.pop(), shape, jnp.float32)

    n_pages = PAST_LEN // PAGE_SIZE
    n_pool = (DEC_BATCH * n_pages * 5 + 3) // 4
    perm = jax.random.permutation(keys.pop(), n_pool)
    page_table = perm[:DEC_BATCH * n_pages].reshape(DEC_BATCH, n_pages).astype(jnp.int32)
    gate_b_a = jnp.stack([nrm((N_A, H_A), 0.1),
                          jnp.broadcast_to(jnp.linspace(3.0, 6.0, H_A), (N_A, H_A)) + nrm((N_A, H_A), 0.1)], axis=1)
    sd = D_MODEL ** -0.5
    return {
        "x_prompt": nrm((BATCH, SEQ, D_MODEL)),
        "x_sample": nrm((DEC_BATCH, DEC_SEQ, D_MODEL)),
        "state_mlstm_C": nrm((N_A, DEC_BATCH, H_A, DH_A, DH_A), 0.1),
        "state_mlstm_n": nrm((N_A, DEC_BATCH, H_A, DH_A)),
        "state_mlstm_m": nrm((N_A, DEC_BATCH, H_A)),
        "state_conv": nrm((N_A, DEC_BATCH, CONV_W - 1, D_B)),
        "cache_k": nrm((N_C, n_pool, PAGE_SIZE, H_C, 2, DH_C)),
        "cache_v": nrm((N_C, n_pool, PAGE_SIZE, H_C, 2 * DH_C)),
        "page_table": page_table,
        "cache_mem_k": nrm((DEPTH, DEC_BATCH, N_MEM, H_M, DH_M)),
        "cache_mem_v": nrm((DEPTH, DEC_BATCH, N_MEM, H_M, DH_M)),
        "mem_prompt": nrm((BATCH, N_MEM, D_MODEL)),
        "norm_mix_g": 1.0 + nrm((DEPTH, D_MODEL), 0.02),
        "norm_mem_g": 1.0 + nrm((DEPTH, D_MODEL), 0.02),
        "norm_ffn_g": 1.0 + nrm((DEPTH, D_MODEL), 0.02),
        "final_norm_g": 1.0 + nrm((D_MODEL,), 0.02),
        "w_in_a": nrm((N_A, D_MODEL, A_COLS), sd),
        "gate_b_a": gate_b_a,
        "head_norm_g_a": 1.0 + nrm((N_A, D_A), 0.02),
        "conv_w_b": nrm((N_A, CONV_W, D_B), CONV_W ** -0.5),
        "w_out_a": nrm((N_A, D_A + D_B, D_MODEL), (D_A + D_B) ** -0.5),
        "w_qkv_c": nrm((N_C, D_MODEL, 3 * D_C), sd),
        "lambda_c": nrm((N_C, 4, DH_C), 0.1),
        "subln_g_c": 1.0 + nrm((N_C, 2 * DH_C), 0.02),
        "w_out_c": nrm((N_C, D_C, D_MODEL), D_C ** -0.5),
        "w_mem_q": nrm((DEPTH, D_MODEL, D_MODEL), sd),
        "w_mem_k": nrm((DEPTH, D_MODEL, D_MODEL), sd),
        "w_mem_v": nrm((DEPTH, D_MODEL, D_MODEL), sd),
        "w_mem_o": nrm((DEPTH, D_MODEL, D_MODEL), sd),
        "w_router_g": nrm((DEPTH, D_MODEL, N_GROUPS), sd),
        "b_router_g": nrm((DEPTH, N_GROUPS), 0.01),
        "w_router_e": nrm((DEPTH, D_MODEL, N_GROUPS * E_PER_GROUP), sd),
        "b_router_e": nrm((DEPTH, N_GROUPS * E_PER_GROUP), 0.01),
        "w_exp_gate": nrm((DEPTH, N_GROUPS, E_PER_GROUP, D_MODEL, D_FF_EXPERT), sd),
        "w_exp_up": nrm((DEPTH, N_GROUPS, E_PER_GROUP, D_MODEL, D_FF_EXPERT), sd),
        "w_exp_down": nrm((DEPTH, N_GROUPS, E_PER_GROUP, D_FF_EXPERT, D_MODEL), D_FF_EXPERT ** -0.5),
    }

def reference(x_prompt, x_sample, state_mlstm_C, state_mlstm_n, state_mlstm_m, state_conv,
              cache_k, cache_v, page_table, cache_mem_k, cache_mem_v, mem_prompt,
              norm_mix_g, norm_mem_g, norm_ffn_g, final_norm_g,
              w_in_a, gate_b_a, head_norm_g_a, conv_w_b, w_out_a,
              w_qkv_c, lambda_c, subln_g_c, w_out_c,
              w_mem_q, w_mem_k, w_mem_v, w_mem_o,
              w_router_g, b_router_g, w_router_e, b_router_e,
              w_exp_gate, w_exp_up, w_exp_down):
    p = dict(norm_mix_g=norm_mix_g, norm_mem_g=norm_mem_g, norm_ffn_g=norm_ffn_g, final_norm_g=final_norm_g,
             w_in_a=w_in_a, gate_b_a=gate_b_a, head_norm_g_a=head_norm_g_a, conv_w_b=conv_w_b, w_out_a=w_out_a,
             w_qkv_c=w_qkv_c, lambda_c=lambda_c, subln_g_c=subln_g_c, w_out_c=w_out_c,
             w_mem_q=w_mem_q, w_mem_o=w_mem_o,
             w_router_g=w_router_g, b_router_g=b_router_g, w_router_e=w_router_e, b_router_e=b_router_e,
             w_exp_gate=w_exp_gate, w_exp_up=w_exp_up, w_exp_down=w_exp_down)
    bp = mem_prompt.shape[0]
    p_mem_k = jnp.einsum('bmd,lde->lbme', mem_prompt, w_mem_k).reshape(DEPTH, bp, N_MEM, H_M, DH_M)
    p_mem_v = jnp.einsum('bmd,lde->lbme', mem_prompt, w_mem_v).reshape(DEPTH, bp, N_MEM, H_M, DH_M)
    y_prompt, (p_c, p_n, p_m, p_conv, p_k, p_v) = trunk(
        x_prompt, p_mem_k, p_mem_v, None, None, None, None, None, None, None, p)
    y_sample, (s_c, s_n, s_m, s_conv, s_k, s_v) = trunk(
        x_sample, cache_mem_k, cache_mem_v, state_mlstm_C, state_mlstm_n, state_mlstm_m, state_conv,
        cache_k, cache_v, page_table, p)
    return (y_prompt, y_sample, p_c, p_n, p_m, p_conv, p_k, p_v, p_mem_k, p_mem_v,
            s_c, s_n, s_m, s_conv, s_k, s_v)


_drawn_inputs = setup_inputs


def setup_inputs(seed=0):
    import zlib

    import numpy as np

    out = dict(_drawn_inputs(seed))
    spreads = {}
    factors = {'norm_mem_g': 4.261, 'final_norm_g': 7.642, 'subln_g_c': 2.883, 'b_router_g': 6.63}
    for name, (base, spread) in spreads.items():
        noise = np.random.default_rng([zlib.crc32(name.encode()), seed]).standard_normal(out[name].shape)
        drawn = base * np.exp(spread * noise) if base else spread * noise
        out[name] = __import__('jax').numpy.asarray(drawn.astype(out[name].dtype))
    for name, factor in factors.items():
        out[name] = (out[name] * factor).astype(out[name].dtype)
    return out
```

```python
import math

import numpy as np

D = 1024
KD = D // 128
NP, NB, NI = 256, 8, 8
NS = NB * NI
T = NP + NS
HA, HC, HM = 4, 8, 4
PAST, PAGE = 256, 128
NG, EPG = 4, 8
NE = NG * EPG
EPS = 1e-6
WSCALE = 64.0
BIG = 1e30
TILES = ((0, 128), (128, 128), (256, 64))

CONST = {}
_at = 0
for _n, _w in (("ident", 128), ("rot", 128), ("fold_pair", 64), ("fold_heads", 64), ("m_tri", 128), ("m_samp", 64),
               ("m_pair", 64), ("m_new", 512), ("cos", T), ("sin", T), ("seg", T), ("segneg", T), ("rank_g", 4),
               ("rank_e", 8), ("map_pair", 1), ("map_heads", 1)):
    CONST[_n] = (_at, _w)
    _at += _w
NCONST = _at


def constants():
    f = np.float32
    c = np.zeros((128, NCONST), f)

    def put(name, a):
        at, w = CONST[name]
        c[:a.shape[0], at:at + w] = a

    p = np.arange(128)
    put("ident", np.eye(128, dtype=f))
    rot = np.zeros((128, 128), f)
    for m in range(128):
        if m % 64 < 32:
            rot[m + 32, m] = -1
        else:
            rot[m - 32, m] = 1
    put("rot", rot)
    put("fold_pair", (p[:, None] % 64 == np.arange(64)[None]).astype(f))
    h, t = p // 16, p % 8
    j = np.arange(64)
    put("fold_heads", ((h[:, None] == j[None] // 8) & (t[:, None] == j[None] % 8)).astype(f))
    neg = f(-BIG)
    put("m_tri", np.where(p[:, None] > p[None], neg, f(0)))
    put("m_samp", np.where((j[:, None] // 8 == j[None] // 8) & (j[:, None] <= j[None]), f(0), neg))
    put("m_pair", np.where(j[None] > p[:, None] % 64, neg, f(0)))
    b = np.arange(8)
    new = np.where((b[None, :, None] == j[None, None] // 8) & (j[None, None] % 8 <= t[:, None, None]), f(0), neg)
    put("m_new", new.reshape(128, 512).astype(f))
    pos = np.concatenate([np.arange(NP), np.tile(PAST + np.arange(NI), NB)]).astype(f)
    inv = np.exp(f(-math.log(10000.0)) * np.arange(32, dtype=f) / f(32)).astype(f)
    ang = (pos[None] * inv[p % 32][:, None]).astype(f)
    put("cos", np.cos(ang).astype(f))
    put("sin", np.sin(ang).astype(f))
    seg = np.ones((4, T), f)
    seg[:, 0] = 0
    seg[:, NP::NI] = 0
    put("seg", seg)
    put("segneg", (seg - 1) * f(BIG))
    put("rank_g", np.tile(8 - np.arange(4, dtype=f), (128, 1)))
    put("rank_e", np.tile(16 - np.arange(8, dtype=f), (128, 1)))
    put("map_pair", (p[:, None] // 64).astype(f))
    put("map_heads", (p[:, None] // 8 % 2).astype(f))
    return c


VEC = dict(mix=0, mem=16, ffn=32, final=48, head=56, subln=60, conv=61)
NVEC = 73

STREAM = [("memk0", 4), ("memv0", 4), ("memk1", 4), ("memv1", 4), ("in_a", 8), ("in_b", 6), ("out_a", 4),
          ("memq0", 4), ("memo0", 4), ("moe0", 96), ("qkv", 12), ("out_c", 4), ("memq1", 4), ("memo1", 4),
          ("moe1", 96)]
UNIT = {}
_at = 0
for _n, _w in STREAM:
    UNIT[_n] = (_at, _w)
    _at += _w
NUNITS = _at


def build(nc, a, o):
    import concourse.bass as bass
    from concourse import mybir
    from contextlib import ExitStack

    F32, F16, BF16, I32 = mybir.dt.float32, mybir.dt.float16, mybir.dt.bfloat16, mybir.dt.int32
    ALU, ACT, AX = mybir.AluOpType, mybir.ActivationFunctionType, mybir.AxisListType
    ds = bass.ds
    ctx = ExitStack()
    ctx.enter_context(nc.allow_non_contiguous_dma("small vectors and strided outputs"))

    def sb(name, shape, dt=F32):
        return ctx.enter_context(nc.sbuf_tensor(name, shape, dt))

    def sem(name):
        return ctx.enter_context(nc.semaphore(name))

    cst = sb("cst", [128, NCONST])
    maskb = sb("maskb", [128, 768], BF16)
    identb = sb("identb", [128, 128], BF16)
    ones = sb("ones", [128, 128])
    epsc = sb("epsc", [128, 2])
    vecs = sb("vecs", [NVEC, 128])
    vec = sb("vec", [128, NVEC])
    xT = sb("xT", [128, KD, T])
    xn = sb("xn", [128, KD, T])
    xh = sb("xh", [128, KD, T], F16)
    xl = sb("xl", [128, KD, T], F16)
    stg = sb("stg", [128, 2, 2048])
    wh = sb("wh", [128, 2, 2048], F16)
    wl = sb("wl", [128, 2, 2048], F16)
    memkT = sb("memkT", [128, 2, KD, 256])
    memv = sb("memv", [128, 2, 2, 1024])
    rstd = sb("rstd", [128, 2, T])
    brt = sb("brt", [128, 2, 36])
    lamv = sb("lamv", [128, 256])
    lams = sb("lams", [128, 8])
    gbias = sb("gbias", [36, 1])
    wgate = sb("wgate", [128, KD, 36])
    wrt = sb("wrt", [128, 2, KD, 36])
    ptab = sb("ptab", [1, 16], I32)
    NAR = (nc.sbuf_bytes_remaining - 2048) // 4 if isinstance(nc.sbuf_bytes_remaining, int) else 22000
    arena = sb("arena", [128, NAR])
    ps = ctx.enter_context(nc.psum_tensor("ps", [128, 8, 512], F32))

    def const(name, rows=128):
        at, w = CONST[name]
        return cst[0:rows, at:at + w]

    ident = const("ident")
    m0 = CONST["m_tri"][0]

    def mask(name, rows=128):
        at, w = CONST[name]
        return maskb[0:rows, at - m0:at - m0 + w]

    def area(start):
        pos = [start]

        def take(*shape, dt=F32):
            n = int(np.prod(shape))
            words = n if dt == F32 else (n + 1) // 2
            v = arena[:, pos[0]:pos[0] + words]
            pos[0] += words
            assert pos[0] <= NAR, (pos[0], NAR)
            if dt != F32:
                v = v.bitcast(dt)
            if len(shape) == 1:
                return v
            names = " ".join("abcd"[:len(shape)])
            return v.rearrange(f"p ({names}) -> p {names}", **{"abcd"[i]: shape[i] for i in range(1, len(shape))})
        return take

    take = area(0)
    x_nat = take(3, 1024)
    mem_nat = take(2, 1024)
    mvT = take(KD, 256)
    mk_out = take(2, 1024)
    take = area(0)
    z = take(28, T)
    zq, zk, zv, zo = z[:, 0:4], z[:, 4:8], z[:, 8:12], z[:, 12:16]
    zgb, zgc, zhb = z[:, 16:20], z[:, 20:24], z[:, 24:28]
    ktok = take(3, 512)
    vtok = take(3, 512)
    dmat = take(4, 448)
    smat = take(448)
    ei = take(4, 384)
    c0 = take(2, 8, 128)
    c0T = take(8, 128)
    vw = take(8, 128)
    vwp = take(2, 128)
    cp_out = take(4, 128)
    u_p = take(4, NP + 2)
    u_s = take(4, NB, NI + 2)
    qi = take(NS)
    qn = take(NS)
    den = take(2, T)
    n0 = take(128)
    n0T = take(32)
    nT = take(36)
    nout = take(128)
    acol = take(12)
    cvt = take(4, 2)
    cvs = take(4, 16)
    m0row = take(8)
    rowsp = z[:, 20:28].rearrange("p a b -> p (a b)")
    r_out = rowsp[0:4, 0:1024]
    cout = rowsp[:, 1024:1536]
    mrow = rowsp[:, 1536:1536 + T]
    cnat = dmat.rearrange("p a b -> p (a b)")[:, 0:512]
    hsq, hstd = z[:, 0:4], z[:, 4:8]
    grow = c0T.rearrange("p a b -> p (a b)")
    g_ig = vw.rearrange("p a b -> p (a b)")[0:4, 0:T]
    g_f = grow[:, 0:T]
    g_t = grow[:, T:2 * T]
    g_lf = vw.rearrange("p a b -> p (a b)")[0:4, T:2 * T]
    g_b = vw.rearrange("p a b -> p (a b)")[0:4, 2 * T:3 * T]
    take = area(0)
    zc = take(24, T)
    vtok3 = take(3, 1024)
    kpg = take(2, 2, 1024)
    vpg = take(2, 2, 1024)
    kTb = take(KD, 256)
    qpadf = take(1152)
    qpad = qpadf[:, 0:1024].rearrange("p (a b) -> p a b", a=8)
    aTp = take(2, 512)
    aTf = aTp.rearrange("p a b -> p (a b)")
    pb, fr, aTb = aTf[:, 0:T], aTf[:, T:T + 64], aTf[:, 384:576].rearrange("p (a b) -> p a b", a=3)
    sst = take(4, 8)
    ktok3 = kpg.rearrange("p a b c -> p (a b c)")[:, 0:3072].rearrange("p (t c) -> p t c", t=3)
    pp = zc[:, 16:24].rearrange("p a b -> p (a b)")[:, 0:2048].rearrange("p (a b) -> p a b", a=8)
    frp = zc[:, 16:24].rearrange("p a b -> p (a b)")[:, 2048:2560]
    take = area(0)
    gbc = take(NE, T)
    e_t = take(2, T)
    r_t = take(2, T)
    a_t = take(2, T)
    b_t = take(2, T)
    cg = take(2, 2, T)
    hh = take(4, T, dt=F16)
    hl = take(4, T, dt=F16)
    gT = take(T)
    lg = take(3, 36)
    rt = take(24, 3, 8)
    gate = take(3, NE)
    take = area(NAR - 2560)
    sq = take(KD, T)

    names = """const_in tab_in vec_in small_in x_in mem_in gate_in
        cst_ready vec_ps vec_ev tr_ps tr_ev
        w_hi w_lo w_used w_ev in_hi in_lo
        sq_ready sum_ready std_ready xn_ready
        gate_ps gneg_ready gln_ready rows_ready acol_ps acol_ev kscaled
        bc_ps d_ready ei_ready s_ps s_ready ct_ps ct_ev q_ready vw_ready num_ps h_ready cn_ps c_ready
        nt_ps nt_ev n_ready hsq_ready hsum_ready hstd_ready osig_ready y_ready conv_ps conv_ev u_ready cv_ready
        cvo_ps cvo_ev c_pool dve_chain act_chain pool_chain pool_loop dve_loop act_loop
        rot_ps rot_cos rot_done lam_arg lam_exp lam_ready
        psc_ps pmax_ready pexp_ready pfr_ready pat_ps pat_ev ppv_ps ppv_ev
        kt_ps kt_ev qp_tile qp_ready bsc_ps bmax_ready bexp_ready bfr_ready bat_ps bat_ev bpv_ps bpv_ev
        osq_ready osum_ready ostd_ready on_ready
        lg_ps lg_ready gexp_ready gsel_ready rexp_ready gate_ready gt_ps gt_ev gbc_ps gbc_ev
        mexp_ready mb_ready mc_ready mhh_ready mhl_ready
        out_mem out_p out_c out_y final_ready""".split()
    S = {n: sem(n) for n in names}
    w_load = [sem("w_load0"), sem("w_load1")]
    c0_in = [sem("c0_in0"), sem("c0_in1")]
    c_out = [sem("c_out0"), sem("c_out1")]
    kv_in = [sem("kv_in0"), sem("kv_in1")]

    class Chain:

        def __init__(self, eng, name, loop):
            self.eng, self.sem, self.n = eng, S[name], 0
            self.lsem, self.base, self.per, self.i, self.k = S[loop], 0, 0, None, 0

        def __call__(self, ins):
            if self.i is None:
                self.n += 1
                ins.then_inc(self.sem, 1)
                self.eng.wait_ge(self.sem, self.n)
            else:
                self.k += 1
                ins.then_inc(self.lsem, 1)
                self.eng.wait_ge(self.lsem, self.i * self.per + (self.base + self.k))

        def enter(self, i, per):
            self.i, self.per, self.k = i, per, 0

        def leave(self, rounds):
            assert self.k == self.per, (self.k, self.per)
            self.base += rounds * self.per
            self.i = None

    block = ctx.enter_context(nc.Block())

    def cols(w, j0, n=256):
        return w.rearrange("(k p) n -> p k n", p=128)[:, :, ds(j0, n)]

    a_cols = a["w_in_a"][0]
    MATRIX = {"memk0": lambda j: cols(a["w_mem_k"][0], j * 256), "memv0": lambda j: cols(a["w_mem_v"][0], j * 256),
              "memk1": lambda j: cols(a["w_mem_k"][1], j * 256), "memv1": lambda j: cols(a["w_mem_v"][1], j * 256),
              "in_a": lambda j: cols(a_cols, j * 256), "in_b": lambda j: cols(a_cols, j * 256 + 2056),
              "out_a": lambda j: cols(a["w_out_a"][0], j * 256),
              "memq0": lambda j: cols(a["w_mem_q"][0], j * 256), "memo0": lambda j: cols(a["w_mem_o"][0], j * 256),
              "qkv": lambda j: cols(a["w_qkv_c"][0], j * 256), "out_c": lambda j: cols(a["w_out_c"][0], j * 256),
              "memq1": lambda j: cols(a["w_mem_q"][1], j * 256), "memo1": lambda j: cols(a["w_mem_o"][1], j * 256)}
    w_gate_f = a["w_exp_gate"].rearrange("l g e (k p) f -> (l g e) p k f", p=128)
    w_up_f = a["w_exp_up"].rearrange("l g e (k p) f -> (l g e) p k f", p=128)
    w_down_f = a["w_exp_down"].rearrange("l g e (k p) d -> (l g e k) p d", p=128)

    def stage8(s):
        return stg[:, s].rearrange("p (k n) -> p k n", k=KD)

    @block.sync
    def _(sp):
        def load(u, s, dst, src, first=False):
            if not first:
                sp.wait_ge(S["w_lo"], u - 1)
            sp.dma_start(dst, src).then_inc(w_load[s], 16)

        def load_expert(u, e):
            load(u, 0, stage8(0), w_gate_f[e, :, :, :] if isinstance(e, int) else
                 w_gate_f[ds(e, 1), :, :, :].rearrange("a p k f -> p (a k) f"))
            load(u + 1, 1, stage8(1), w_up_f[e, :, :, :] if isinstance(e, int) else
                 w_up_f[ds(e, 1), :, :, :].rearrange("a p k f -> p (a k) f"))

        def load_down(u, row):
            for s in range(2):
                load(u + s, s, stg[:, s].rearrange("p (k n) -> p k n", k=4),
                     w_down_f[ds(row, 4), :, 512 * s:512 * s + 512].rearrange("k p n -> p k n"))

        for name, n in STREAM:
            u0 = UNIT[name][0]
            if name.startswith("moe"):
                layer = int(name[-1])
                load_expert(u0, NE * layer)
                load_expert(u0 + 2, NE * layer + 1)
                with sp.Fori(1, NE // 2) as i:
                    u = i * 6 + (u0 - 2)
                    load_expert(u, i * 2 + NE * layer)
                    load_down(u + 2, i * 4 + (NE * 2 * layer - 4))
                    load_expert(u + 4, i * 2 + (NE * layer + 1))
                load_down(u0 + n - 2, NE * 2 * layer + 2 * NE - 4)
            else:
                start = 0
                if u0 == 0:
                    for s in range(2):
                        load(s, s, stage8(s), MATRIX[name](s), first=True)
                    start = 1
                with sp.Fori(start, n // 2) as i:
                    for s in range(2):
                        load(i * 2 + (u0 + s), s, stage8(s), MATRIX[name](i * 2 + s))

    def split_hi(act, u, s):
        act.wait_ge(w_load[s], (u - s) * 8 + 16)
        nc.scalar.mul(wh[:, s], stg[:, s], WSCALE).then_inc(S["w_hi"], 1)

    def split_lo(dve, u, s):
        dve.wait_ge(S["w_hi"], u + 1)
        nc.vector.scalar_tensor_tensor(wl[:, s], stg[:, s], WSCALE, wh[:, s], ALU.mult,
                                       ALU.subtract).then_inc(S["w_lo"], 1)

    def mm3(out, s, kk, c0_, hi, lo, start, stop, width=256):
        at = kk * width + c0_
        nc.tensor.matmul(out, wh[:, s, at:at + 128], hi, start=start, stop=False)
        nc.tensor.matmul(out, wh[:, s, at:at + 128], lo, start=False, stop=False)
        return nc.tensor.matmul(out, wl[:, s, at:at + 128], hi, start=False, stop=stop)

    def gemm_pe(pe, name, g, n=T):
        u0, units = UNIT[name]
        pe.wait_ge(S["in_lo"], g + 1)

        def unit(u, s):
            pe.wait_ge(S["w_lo"], u + 1)
            pe.wait_ge(S["w_ev"], u - 1)
            for j in range(2):
                for k in range(KD):
                    last = mm3(ps[:, 2 * s + j, 0:n], s, k, 128 * j, xh[:, k, 0:n], xl[:, k, 0:n], k == 0,
                               k == KD - 1)
            last.then_inc(S["w_used"], 1)

        start = 0
        if u0 == 0:
            for s in range(2):
                pe.wait_ge(S["w_lo"], s + 1)
                for j in range(2):
                    for k in range(KD):
                        last = mm3(ps[:, 2 * s + j, 0:n], s, k, 128 * j, xh[:, k, 0:n], xl[:, k, 0:n], k == 0,
                                   k == KD - 1)
                last.then_inc(S["w_used"], 1)
            start = 1
        with pe.Fori(start, units // 2) as i:
            for s in range(2):
                unit(i * 2 + (u0 + s), s)

    def gemm_copy_act(act, name, dst, n=T):
        u0, units = UNIT[name]
        with act.Fori(0, units // 2) as i:
            for s in range(2):
                act.wait_ge(S["w_used"], i * 2 + (u0 + s + 1))
                nc.scalar.mul(dst[:, ds(i * 4 + 2 * s, 2), :], ps[:, 2 * s:2 * s + 2, 0:n],
                              1 / WSCALE).then_inc(S["w_ev"], 1)
                split_hi(act, i * 2 + (u0 + s + 2), s)

    def gemm_split_act(act, name):
        u0, units = UNIT[name]
        with act.Fori(0, units // 2) as i:
            for s in range(2):
                act.wait_ge(S["w_used"], i * 2 + (u0 + s + 1))
                split_hi(act, i * 2 + (u0 + s + 2), s)

    def gemm_split_dve(dve, name):
        u0, units = UNIT[name]
        with dve.Fori(0, units // 2) as i:
            for s in range(2):
                dve.wait_ge(S["w_used"], i * 2 + (u0 + s + 1))
                split_lo(dve, i * 2 + (u0 + s + 2), s)

    def gemm_add_dve(dve, name):
        u0, units = UNIT[name]
        with dve.Fori(0, units // 2) as i:
            for s in range(2):
                dve.wait_ge(S["w_used"], i * 2 + (u0 + s + 1))
                at = ds(i * 4 + 2 * s, 2)
                nc.vector.scalar_tensor_tensor(xT[:, at, :], ps[:, 2 * s:2 * s + 2, 0:T], 1 / WSCALE, xT[:, at, :],
                                               ALU.mult, ALU.add).then_inc(S["w_ev"], 1)
                split_lo(dve, i * 2 + (u0 + s + 2), s)

    def input_act(act, src, n=T):
        nc.scalar.copy(xh[:, :, 0:n], src).then_inc(S["in_hi"], 1)

    def input_dve(dve, g, src, n=T):
        dve.wait_ge(S["in_hi"], g + 1)
        nc.vector.tensor_sub(xl[:, :, 0:n], src, xh[:, :, 0:n]).then_inc(S["in_lo"], 1)

    def tr_pe(pe, g, srcs, n):
        if g >= 4:
            pe.wait_ge(S["tr_ev"], g - 3)
        for i, src in enumerate(srcs):
            m = src.shape[-1]
            last = nc.tensor.transpose(ps[0:m, 4 + g % 4, 128 * i:128 * i + n], src, ident[0:n, 0:n])
        last.then_inc(S["tr_ps"], 1)

    def tr_dve(dve, g, dst, m, n, cnt=4):
        dve.wait_ge(S["tr_ps"], g + 1)
        src = ps[0:m, 4 + g % 4, :].rearrange("p (a b) -> p a b", a=4)[:, 0:cnt, 0:n]
        nc.vector.tensor_copy(dst, src).then_inc(S["tr_ev"], 1)

    G_X, G_MEM, G_MKV, G_ML, G_DA, G_Y = 0, 6, 10, 26, 32, 44

    NVROW = {0: VEC["mix"], 1: VEC["mem"], 2: VEC["ffn"], 3: VEC["mix"] + 8, 4: VEC["mem"] + 8, 5: VEC["ffn"] + 8,
             6: VEC["final"]}

    def norm_act(act, n):
        nc.scalar.activation(sq[:], xT[:], ACT.Square).then_inc(S["sq_ready"], 1)
        act.wait_ge(S["sum_ready"], n + 1)
        nc.scalar.activation(rstd[:, 0, :], ps[:, 4, 0:T], ACT.Sqrt, bias=epsc[:, 0:1],
                             scale=1.0 / D).then_inc(S["std_ready"], 1)

    def norm_pe(pe, n):
        pe.wait_ge(S["sq_ready"], n + 1)
        for k in range(KD):
            last = nc.tensor.matmul(ps[:, 4, 0:T], ones[:], sq[:, k, :], start=(k == 0), stop=(k == KD - 1))
        last.then_inc(S["sum_ready"], 1)

    def norm_dve(dve, link, n):
        dve.wait_ge(S["std_ready"], n + 1)
        link(nc.vector.reciprocal(rstd[:, 1, :], rstd[:, 0, :]))
        for k in range(KD):
            v = NVROW[n] + k
            last = nc.vector.scalar_tensor_tensor(xn[:, k, :], xT[:, k, :], vec[:, v:v + 1], rstd[:, 1, :], ALU.mult,
                                                  ALU.mult)
        last.then_inc(S["xn_ready"], 1)
        dve.wait_ge(S["xn_ready"], n + 1)

    NPOOL = a["cache_k"].shape[1]
    SMALL = 16 * 3
    NVIN = 16 * (7 + 2 + 8 + 1)
    DGROUPS = ((0, 128, 0, 256), (1, 128, 256, 128), (2, 64, 384, 64))

    def mlstm_pool(pool, link):
        for h in range(2):
            pool.dma_start(c0[:, h], a["state_mlstm_C"][0, :, h].rearrange("b v k -> v b k")).then_inc(c0_in[h], 16)
        pool.dma_start(n0[0:32, :], a["state_mlstm_n"][0].rearrange("b h k -> (b h) k")).then_inc(S["small_in"], 16)
        pool.dma_start(m0row[0:4, :], a["state_mlstm_m"][0].rearrange("b h -> h b")).then_inc(S["small_in"], 16)
        pool.dma_start(cnat[0:16, :], a["state_conv"][0].rearrange("b w d -> (b w) d")).then_inc(S["small_in"], 16)

    def mlstm_pool_out(pool, link):
        pool.wait_ge(S["cvo_ev"], 1)
        pool.dma_start(o["p_conv"][0, 0], cout[0:2, :]).then_inc(S["out_c"], 16)
        pool.dma_start(o["s_conv"][0].rearrange("b w d -> (b w) d"), cout[32:48, :]).then_inc(S["out_c"], 16)
        pool.wait_ge(S["rows_ready"], 1)
        pool.dma_start(o["p_m"][0].rearrange("b h -> h b"), mrow[0:4, NP - 1:NP]).then_inc(S["out_c"], 16)
        pool.dma_start(o["s_m"][0].rearrange("b h -> h b"), mrow[0:4, NP + NI - 1::NI]).then_inc(S["out_c"], 16)
        for h in range(HA):
            pool.wait_ge(S["c_ready"], h + 1)
            pool.dma_start(o["s_C"][0, :, h].rearrange("b v k -> v b k"), c0[:, h % 2]).then_inc(c_out[h % 2], 16)
            pool.dma_start(o["p_C"][0, 0, h], cp_out[:, h, :]).then_inc(S["out_c"], 16)
            if h + 2 < HA:
                pool.wait_ge(c_out[h % 2], 16)
                pool.dma_start(c0[:, h % 2], a["state_mlstm_C"][0, :, h + 2].rearrange("b v k -> v b k")
                               ).then_inc(c0_in[h % 2], 16)
        pool.wait_ge(S["n_ready"], 1)
        pool.dma_start(o["s_n"][0].rearrange("b h k -> (b h) k"), nout[0:32, :]).then_inc(S["out_c"], 16)
        pool.dma_start(o["p_n"][0, 0], nout[32:36, :]).then_inc(S["out_c"], 16)

    def mlstm_pe(pe):
        pe.wait_ge(S["gate_in"], 32)
        pe.wait_ge(S["cst_ready"], 1)
        for k in range(KD):
            last = nc.tensor.matmul(ps[0:36, 5, 0:T], wgate[:, k, :], xn[:, k, :], start=(k == 0),
                                    stop=(k == KD - 1))
        last.then_inc(S["gate_ps"], 1)
        gemm_pe(pe, "in_a", 1)
        gemm_pe(pe, "in_b", 1)
        pe.wait_ge(S["small_in"], SMALL)
        for c in range(4):
            nc.tensor.transpose(ps[:, 6, 16 * c:16 * c + 16], cnat[0:16, 128 * c:128 * c + 128], ident[0:16, 0:16])
        nc.tensor.transpose(ps[:, 6, 64:96], n0[0:32, :], ident[0:32, 0:32]).then_inc(S["conv_ps"], 1)
        pe.wait_ge(S["kscaled"], 1)
        pe.wait_ge(S["gneg_ready"], 1)
        pe.wait_ge(S["conv_ev"], 1)
        g = G_ML
        for src in (zk, zv):
            for t0, n in TILES:
                tr_pe(pe, g, [src[:, i, t0:t0 + n] for i in range(4)], 128)
                g += 1
        pe.wait_ge(S["rows_ready"], 1)
        pe.wait_ge(S["tr_ev"], G_ML + 6)
        for i, (t0, n) in enumerate(TILES):
            last = nc.tensor.transpose(ps[0:n, 3, 4 * i:4 * i + 4], r_out[:, 704 + t0:704 + t0 + n], ident[0:4, 0:4])
        last.then_inc(S["acol_ps"], 1)
        pe.wait_ge(S["u_ready"], 2)
        for c in range(4):
            nc.tensor.transpose(ps[0:2, 1, 128 * c:128 * c + 128], cvt[:, c, :], ident)
        for c in range(4):
            last = nc.tensor.transpose(ps[0:16, 2, 128 * c:128 * c + 128], cvs[:, c, :], ident)
        last.then_inc(S["cvo_ps"], 1)
        pe.wait_ge(S["cvo_ev"], 1)
        pe.wait_ge(S["acol_ev"], 1)
        for h in range(HA):
            if h:
                pe.wait_ge(S["ei_ready"], h)
            sel = ident[0:4, h:h + 1].to_broadcast([4, 128])
            for (tile, n, c, w) in DGROUPS:
                t0 = T - 64 if tile == 2 else 128 * tile
                mname, mw = ("m_samp", 64) if tile == 2 else ("m_tri", 128)
                nc.tensor.matmul(ps[0:n, 4, c:c + w], sel[:, 0:n], r_out[:, t0:t0 + w], start=True, stop=False)
                nc.tensor.matmul(ps[0:n, 4, c:c + mw], identb[0:n, 0:n], mask(mname, n), start=False, stop=True)
            nc.tensor.matmul(ps[:, 5, 0:384], sel, r_out[:, 320:704], start=True, stop=True).then_inc(S["bc_ps"], 1)
            if h:
                pe.wait_ge(S["s_ready"], h)
            for (tile, n, c, w) in DGROUPS:
                t0 = T - 64 if tile == 2 else 128 * tile
                last = nc.tensor.matmul(ps[0:n, 6, c:c + w], zk[:, h, t0:t0 + n], zq[:, h, t0:t0 + w], start=True,
                                        stop=True)
            last.then_inc(S["s_ps"], 1)
            pe.wait_ge(c0_in[h % 2], 16 * (h // 2 + 1))
            if h:
                pe.wait_ge(S["c_ready"], h)
            for b in range(NB):
                last = nc.tensor.transpose(ps[:, 1 + b // 4, 128 * (b % 4):128 * (b % 4) + 128], c0[:, h % 2, b, :],
                                           ident)
            last.then_inc(S["ct_ps"], 1)
            pe.wait_ge(S["s_ready"], h + 1)
            pe.wait_ge(S["ct_ev"], h + 1)
            pe.wait_ge(S["q_ready"], h + 1)
            if h:
                pe.wait_ge(S["h_ready"], h)
            for bank, left in ((7, None), (0, ones)):
                first = True
                for (tile, n, c, w) in DGROUPS:
                    t0 = T - 64 if tile == 2 else 128 * tile
                    lhs = vtok[0:n, tile, 128 * h:128 * h + 128] if left is None else ones[0:n, :]
                    nc.tensor.matmul(ps[:, bank, t0:t0 + w], lhs, smat[0:n, c:c + w], start=first, stop=False,
                                     skip_group_check=True)
                    first = False
                if left is None:
                    for b in range(NB):
                        last = nc.tensor.matmul(ps[:, bank, NP + NI * b:NP + NI * b + NI], c0T[:, b, :],
                                                qi[:, NI * b:NI * b + NI], start=False, stop=(b == NB - 1),
                                                skip_group_check=True)
                else:
                    last = nc.tensor.matmul(ps[:, bank, NP:T], ones[:], qn[:], start=False, stop=True,
                                            skip_group_check=True)
            last.then_inc(S["num_ps"], 1)
            pe.wait_ge(S["vw_ready"], h + 1)
            kt = ktok[:, :, 128 * h:128 * h + 128]
            for b in range(NB):
                nc.tensor.matmul(ps[:, 1 + b // 4, 128 * (b % 4):128 * (b % 4) + 128], vw[0:64, b, :],
                                 kt[0:64, 2, :], start=True, stop=True)
            for i in range(2):
                nc.tensor.matmul(ps[:, 3, 0:128], vwp[:, i, :], kt[:, i, :], start=(i == 0), stop=(i == 1))
            nc.tensor.matmul(ps[:, 3, 128:136], kt[0:64, 2, :], dmat[0:64, h, 384 + NI - 1:448:NI], start=True,
                             stop=True)
            for i in range(2):
                last = nc.tensor.matmul(ps[:, 3, 136:137], kt[:, i, :], dmat[:, h, 255 + 128 * i:256 + 128 * i],
                                        start=(i == 0), stop=(i == 1))
            last.then_inc(S["cn_ps"], 1)
        pe.wait_ge(S["c_ready"], HA)
        nc.tensor.transpose(ps[0:36, 3, 0:128], nT[:], ident).then_inc(S["nt_ps"], 1)
        pe.wait_ge(S["hsq_ready"], 1)
        pe.wait_ge(S["h_ready"], HA)
        pe.wait_ge(S["s_ready"], HA)
        for h in range(HA):
            last = nc.tensor.matmul(ps[:, 4 + h, 0:T], ones[:], hsq[:, h, :], start=True, stop=True)
        last.then_inc(S["hsum_ready"], 1)

    def mlstm_act(act, link):
        act.wait_ge(S["gneg_ready"], 1)
        link(nc.scalar.activation(g_t[32:36, :], g_t[32:36, :], ACT.Exp))
        nc.scalar.activation(g_t[32:36, :], g_t[32:36, :], ACT.Ln, bias=epsc[32:36, 1:2]).then_inc(S["gln_ready"], 1)
        for h in range(HA):
            act.wait_ge(S["bc_ps"], h + 1)
            if h == 0:
                act.wait_ge(S["acol_ev"], 1)
            for (tile, n, c, w) in DGROUPS:
                last = nc.scalar.activation(dmat[0:n, h, c:c + w], ps[0:n, 4, c:c + w], ACT.Exp,
                                            bias=acol[0:n, 4 * tile + h:4 * tile + h + 1])
            last.then_inc(S["d_ready"], 1)
            nc.scalar.activation(ei[:, h, :], ps[:, 5, 0:384], ACT.Exp).then_inc(S["ei_ready"], 1)
            act.wait_ge(S["ct_ps"], h + 1)
            if h:
                act.wait_ge(S["num_ps"], h)
            nc.scalar.copy(c0T.rearrange("p (a b) c -> p a (b c)", a=2), ps[:, 1:3, :]).then_inc(S["ct_ev"], 1)
        act.wait_ge(S["h_ready"], HA)
        nc.scalar.activation(hsq, xn[:, 0:4, :], ACT.Square).then_inc(S["hsq_ready"], 1)
        nc.scalar.activation(zo[:], zo[:], ACT.Exp, scale=-1.0).then_inc(S["osig_ready"], 1)
        act.wait_ge(S["hsum_ready"], 1)
        nc.scalar.activation(hstd, ps[:, 4:8, 0:T], ACT.Sqrt, bias=epsc[:, 0:1],
                             scale=1.0 / 128).then_inc(S["hstd_ready"], 1)

    def mlstm_dve(dve, link):
        dve.wait_ge(S["w_ev"], UNIT["out_a"][0])
        nc.vector.tensor_scalar(zk[:], zk[:], 128 ** -0.5, None, ALU.mult).then_inc(S["kscaled"], 1)
        dve.wait_ge(S["conv_ps"], 1)
        nc.vector.tensor_copy(u_s[:, :, :, 0:2], ps[:, 6, 0:64].rearrange("p (c b w) -> p c b w", c=4, w=2))
        link(nc.vector.tensor_copy(n0T[:], ps[:, 6, 64:96]))
        nc.vector.memset(u_p[:, :, 0:2], 0.0).then_inc(S["conv_ev"], 1)
        dve.wait_ge(S["conv_ev"], 1)
        nc.vector.tensor_tensor(u_p[:, :, 2:], zgc[:, :, 0:NP], zhb[:, :, 0:NP], ALU.mult)
        for c in range(4):
            last = nc.vector.tensor_tensor(u_s[:, c, :, 2:], zgc[:, c, NP:T].rearrange("p (b i) -> p b i", b=NB),
                                           zhb[:, c, NP:T].rearrange("p (b i) -> p b i", b=NB), ALU.mult)
        link(last)
        nc.vector.tensor_copy(cvt[:], u_p[:, :, NP:NP + 2]).then_inc(S["u_ready"], 1)
        nc.vector.tensor_copy(cvs.rearrange("p c (b w) -> p c b w", w=2), u_s[:, :, :, NI:NI + 2]
                              ).then_inc(S["u_ready"], 1)
        for j in range(3):
            for c in range(4):
                v = VEC["conv"] + 4 * j + c
                for (dst, src) in ((xn[:, 4 + c, 0:NP], u_p[:, c, j:j + NP]),
                                   (xn[:, 4 + c, NP:T].rearrange("p (b i) -> p b i", b=NB), u_s[:, c, :, j:j + NI])):
                    if j == 0:
                        last = nc.vector.tensor_scalar(dst, src, vec[:, v:v + 1], None, ALU.mult)
                    else:
                        last = nc.vector.scalar_tensor_tensor(dst, src, vec[:, v:v + 1], dst, ALU.mult, ALU.add)
            link(last)
        link(nc.vector.tensor_tensor(xn[:, 4:8, :], xn[:, 4:8, :], zgb[:], ALU.mult))
        dve.wait_ge(S["gate_ps"], 1)
        nc.vector.tensor_scalar(g_ig, ps[0:4, 5, 0:T], gbias[0:4, :], None, ALU.add)
        link(nc.vector.tensor_scalar(g_f[32:36, :], ps[32:36, 5, 0:T], gbias[32:36, :], None, ALU.add))
        nc.vector.scalar_tensor_tensor(g_t[32:36, :], g_f[32:36, :], -1.0, g_f[32:36, :], ALU.mult, ALU.min
                                       ).then_inc(S["gneg_ready"], 1)
        for i, (t0, n) in enumerate(TILES):
            tr_dve(dve, G_ML + i, ktok[0:n, i, :].rearrange("p (a b) -> p a b", a=4), n, 128)
        for i, (t0, n) in enumerate(TILES):
            tr_dve(dve, G_ML + 3 + i, vtok[0:n, i, :].rearrange("p (a b) -> p a b", a=4), n, 128)
        dve.wait_ge(S["gln_ready"], 1)
        link(nc.vector.scalar_tensor_tensor(g_lf, g_f[32:36, :], 0.0, g_t[32:36, :], ALU.min, ALU.subtract))
        link(nc.vector.tensor_tensor_scan(g_b, const("seg", 4), g_lf, 0.0, ALU.mult, ALU.add))
        ar = r_out[:, 704:1024]
        link(nc.vector.tensor_tensor(ar, g_ig, g_b, ALU.subtract))
        link(nc.vector.tensor_copy(g_lf, ar))
        nc.vector.tensor_scalar(g_lf[:, 0:1], ar[:, 0:1], 0.0, None, ALU.max)
        link(nc.vector.tensor_tensor(g_lf[:, NP::NI], ar[:, NP::NI], m0row[0:4, :], ALU.max))
        link(nc.vector.tensor_tensor_scan(g_ig, const("segneg", 4), g_lf, 0.0, ALU.add, ALU.max))
        link(nc.vector.tensor_tensor(mrow[0:4, :], g_b, g_ig, ALU.add))
        nc.vector.tensor_scalar(r_out[:, 0:320], g_ig, -1.0, None, ALU.mult)
        nc.vector.tensor_scalar(r_out[:, 320:640], mrow[0:4, :], -1.0, None, ALU.mult)
        nc.vector.tensor_tensor(r_out[:, 640:704].rearrange("p (b i) -> p b i", b=NB),
                                m0row[0:4, :].unsqueeze(2).to_broadcast([4, NB, NI]),
                                g_ig[:, NP:T].rearrange("p (b i) -> p b i", b=NB), ALU.subtract
                                ).then_inc(S["rows_ready"], 1)
        dve.wait_ge(S["acol_ps"], 1)
        nc.vector.tensor_copy(acol[:, 0:8], ps[:, 3, 0:8])
        nc.vector.tensor_copy(acol[0:64, 8:12], ps[0:64, 3, 8:12]).then_inc(S["acol_ev"], 1)
        dve.wait_ge(S["cvo_ps"], 1)
        link(nc.vector.tensor_copy(cout[0:2, :], ps[0:2, 1, :]))
        nc.vector.tensor_copy(cout[32:48, :], ps[0:16, 2, :]).then_inc(S["cvo_ev"], 1)
        dve.wait_ge(S["cvo_ev"], 1)
        for h in range(HA):
            dve.wait_ge(S["s_ps"], h + 1)
            dve.wait_ge(S["d_ready"], h + 1)
            if h:
                dve.wait_ge(S["num_ps"], h)
            for (tile, n, c, w) in DGROUPS:
                last = nc.vector.tensor_tensor(smat[0:n, c:c + w], ps[0:n, 6, c:c + w], dmat[0:n, h, c:c + w],
                                               ALU.mult)
            last.then_inc(S["s_ready"], 1)
            dve.wait_ge(S["ei_ready"], h + 1)
            link(nc.vector.tensor_tensor(qi[:], zq[:, h, NP:T], ei[:, h, 320:384], ALU.mult))
            nc.vector.tensor_tensor(qn.rearrange("p (b i) -> p b i", b=NB), qi.rearrange("p (b i) -> p b i", b=NB),
                                    n0T[:, h::HA].unsqueeze(2).to_broadcast([128, NB, NI]), ALU.mult
                                    ).then_inc(S["q_ready"], 1)
            if h:
                dve.wait_ge(S["cn_ps"], h)
            hs = slice(128 * h, 128 * h + 128)
            nc.vector.tensor_tensor(vw[0:64], vtok[0:64, 2, hs].unsqueeze(1).to_broadcast([64, NB, 128]),
                                    dmat[0:64, h, 384 + NI - 1:448:NI].unsqueeze(2).to_broadcast([64, NB, 128]),
                                    ALU.mult)
            for i in range(2):
                last = nc.vector.tensor_scalar(vwp[:, i, :], vtok[:, i, hs], dmat[:, h, 255 + 128 * i:256 + 128 * i],
                                               None, ALU.mult)
            last.then_inc(S["vw_ready"], 1)
            dve.wait_ge(S["num_ps"], h + 1)
            link(nc.vector.scalar_tensor_tensor(den[:, 0, :], ps[:, 0, 0:T], -1.0, ei[:, h, 0:T], ALU.mult, ALU.max))
            link(nc.vector.tensor_tensor(den[:, 0, :], ps[:, 0, 0:T], den[:, 0, :], ALU.max))
            link(nc.vector.reciprocal(den[:, 1, :], den[:, 0, :]))
            nc.vector.tensor_tensor(xn[:, h, :], ps[:, 7, 0:T], den[:, 1, :], ALU.mult).then_inc(S["h_ready"], 1)
            dve.wait_ge(S["cn_ps"], h + 1)
            dec = ei[:, h, 320 + NI - 1:384:NI]
            link(nc.vector.tensor_tensor(c0[:, h % 2], c0[:, h % 2], dec.unsqueeze(2).to_broadcast([128, NB, 128]),
                                         ALU.mult))
            nc.vector.tensor_tensor(c0[:, h % 2].rearrange("p (a b) c -> p a (b c)", a=2), ps[:, 1:3, :],
                                    c0[:, h % 2].rearrange("p (a b) c -> p a (b c)", a=2), ALU.add)
            nc.vector.tensor_copy(cp_out[:, h, :], ps[:, 3, 0:128])
            nc.vector.tensor_copy(nT[:, 32 + h:33 + h], ps[:, 3, 136:137])
            link(nc.vector.tensor_tensor(nT[:, h:32:HA], n0T[:, h::HA], dec, ALU.mult))
            nc.vector.tensor_tensor(nT[:, h:32:HA], nT[:, h:32:HA], ps[:, 3, 128:136], ALU.add
                                    ).then_inc(S["c_ready"], 1)
        dve.wait_ge(S["nt_ps"], 1)
        nc.vector.tensor_copy(nout[0:36, :], ps[0:36, 3, 0:128]).then_inc(S["n_ready"], 1)
        dve.wait_ge(S["osig_ready"], 1)
        link(nc.vector.tensor_scalar(zo[:], zo[:], 1.0, None, ALU.add))
        link(nc.vector.reciprocal(zo[:], zo[:]))
        dve.wait_ge(S["hstd_ready"], 1)
        link(nc.vector.reciprocal(hsq, hstd))
        link(nc.vector.tensor_tensor(xn[:, 0:4, :], xn[:, 0:4, :], hsq, ALU.mult))
        for h in range(HA):
            v = VEC["head"] + h
            last = nc.vector.scalar_tensor_tensor(xn[:, h, :], xn[:, h, :], vec[:, v:v + 1], zo[:, h, :], ALU.mult,
                                                  ALU.mult)
        last.then_inc(S["y_ready"], 1)
        dve.wait_ge(S["y_ready"], 1)


    ATT = {"m0": dict(tile0=0, batch0=0, kv0=0, dma=32, layer=0), "d": dict(tile0=2, batch0=8, kv0=128, dma=64, layer=1),
           "m1": dict(tile0=6, batch0=16, kv0=384, dma=32, layer=1)}
    for _k, _c in ATT.items():
        diff = _k == "d"
        _c.update(diff=diff, nt=4 if diff else 2, nq=64 if diff else 128, nh=8 if diff else 4,
                  rows=128 if diff else 32, width=T if diff else 256, c=64 if diff else 32,
                  scale=64 ** -0.5 if diff else 256 ** -0.5)
    psf = ps.rearrange("p b k -> p (b k)")
    qdiag = qpadf[:, 0:1152].rearrange("p (h x) -> p h x", x=144)
    qmem = qpadf[:, 0:288].rearrange("p (h x) -> p h x", x=72)[:, :, 0:64].rearrange("p h (c y) -> p h c y", y=32)

    def head_of(c, blk):
        return blk if c["diff"] else blk // 2

    def prompt_pe(pe, kind):
        c = ATT[kind]
        nh, nq = c["nh"], c["nq"]
        for t in range(c["nt"]):
            n = c["tile0"] + t
            nk = 64 * (t + 1) if c["diff"] else 256
            if c["diff"]:
                pe.wait_ge(S["qp_tile"], t + 1)
            if n:
                pe.wait_ge(S["pexp_ready"], n)
            for h in range(nh):
                out = psf[:, 2048 + 256 * h:2048 + 256 * h + nk]
                if c["diff"]:
                    nc.tensor.matmul(out, qpad[:, h, :], zc[:, 8 + h, 0:nk], start=True, stop=False,
                                     skip_group_check=True)
                    last = nc.tensor.matmul(out[:, 64 * t:nk], identb[:], mask("m_pair"), start=False, stop=True,
                                            skip_group_check=True)
                else:
                    for dc in range(2):
                        last = nc.tensor.matmul(out, zc[:, 2 * h + dc, 128 * t:128 * t + 128],
                                                memkT[:, c["layer"], 2 * h + dc, :], start=(dc == 0), stop=(dc == 1))
            last.then_inc(S["psc_ps"], 1)
            pe.wait_ge(S["pfr_ready"], n + 1)
            kts = [(kt, min(128, nk - 128 * kt)) for kt in range((nk + 127) // 128)]
            for kt, m in kts:
                for h in range(nh):
                    last = nc.tensor.matmul(ps[0:m, kt, nq * h:nq * h + nq], pp[:, h, 128 * kt:128 * kt + m],
                                            frp[:, nq * h:nq * h + nq], start=True, stop=True)
            last.then_inc(S["pat_ps"], 1)
            pe.wait_ge(S["pat_ev"], n + 1)
            if n:
                pe.wait_ge(S["ppv_ev"], n)
            for blk in range(8):
                h = head_of(c, blk)
                at = 1024 + nq * blk
                for kt, m in kts:
                    v = vtok3[0:m, kt, 128 * blk:128 * blk + 128] if c["diff"] else \
                        memv[0:m, c["layer"], kt, 128 * blk:128 * blk + 128]
                    last = nc.tensor.matmul(psf[:, at:at + nq], v, aTp[0:m, kt, nq * h:nq * h + nq], start=(kt == 0),
                                            stop=(kt == kts[-1][0]))
            last.then_inc(S["ppv_ps"], 1)

    def prompt_act(act, kind):
        c = ATT[kind]
        for t in range(c["nt"]):
            n = c["tile0"] + t
            nk = 64 * (t + 1) if c["diff"] else 256
            act.wait_ge(S["pmax_ready"], n + 1)
            if n:
                act.wait_ge(S["pat_ps"], n)
            for h in range(c["nh"]):
                last = nc.scalar.activation(pp[:, h, 0:nk], psf[:, 2048 + 256 * h:2048 + 256 * h + nk], ACT.Exp,
                                            bias=sst[:, 0, h:h + 1], scale=c["scale"], accum_out=sst[:, 1, h:h + 1])
            last.then_inc(S["pexp_ready"], 1)
            act.wait_ge(S["pat_ps"], n + 1)
            if n:
                act.wait_ge(S["ppv_ps"], n)
            for kt in range((nk + 127) // 128):
                m = min(128, nk - 128 * kt)
                last = nc.scalar.copy(aTp[0:m, kt, :], ps[0:m, kt, :])
            last.then_inc(S["pat_ev"], 1)

    def prompt_dve(dve, link, kind):
        c = ATT[kind]
        nh, nq = c["nh"], c["nq"]
        if c["diff"]:
            link(nc.vector.memset(qpadf[:], 0.0))
        for t in range(c["nt"]):
            n = c["tile0"] + t
            nk = 64 * (t + 1) if c["diff"] else 256
            if c["diff"]:
                if t:
                    dve.wait_ge(S["psc_ps"], n)
                for m in range(2):
                    r = slice(64 * m, 64 * m + 64)
                    last = nc.vector.tensor_copy(qpad[r, :, 64 * m:64 * m + 64], zc[r, 0:8, 64 * t:64 * t + 64])
                last.then_inc(S["qp_tile"], 1)
            dve.wait_ge(S["psc_ps"], n + 1)
            sc = psf[:, 2048:2048 + 256 * nh].rearrange("p (h k) -> p h k", h=nh)[:, :, 0:nk]
            link(nc.vector.reduce_max(sst[:, 2, 0:nh], sc, AX.X))
            nc.vector.tensor_scalar(sst[:, 0, 0:nh], sst[:, 2, 0:nh], -c["scale"], None, ALU.mult
                                    ).then_inc(S["pmax_ready"], 1)
            dve.wait_ge(S["pexp_ready"], n + 1)
            link(nc.vector.reciprocal(sst[:, 3, 0:nh], sst[:, 1, 0:nh]))
            if c["diff"]:
                link(nc.vector.tensor_scalar(sst[:, 3, 0:nh], sst[:, 3, 0:nh], lams[:, 5:6], None, ALU.mult))
            fold = const("fold_pair") if c["diff"] else ident
            nc.vector.tensor_tensor(frp.rearrange("p (h q) -> p h q", h=nh),
                                    fold.unsqueeze(1).to_broadcast([128, nh, nq]),
                                    sst[:, 3, 0:nh].unsqueeze(2).to_broadcast([128, nh, nq]), ALU.mult
                                    ).then_inc(S["pfr_ready"], 1)
            dve.wait_ge(S["ppv_ps"], n + 1)
            nc.vector.tensor_copy(xn[:, :, nq * t:nq * t + nq],
                                  psf[:, 1024:1024 + 8 * nq].rearrange("p (b q) -> p b q", b=8)
                                  ).then_inc(S["ppv_ev"], 1)

    def batch_pool(pool, link, kind):
        c = ATT[kind]

        def load(b, s):
            if c["diff"]:
                for p in range(2):
                    page = pool.value_load(ptab[0:1, ds(b * 2 + p, 1)] if not isinstance(b, int) else
                                           ptab[0:1, 2 * b + p:2 * b + p + 1], min_val=0, max_val=NPOOL - 1)
                    for cache, dst in ((a["cache_k"], kpg), (a["cache_v"], vpg)):
                        v = cache[0].rearrange("g t h m d -> g t (h m d)") if len(cache.shape) == 6 else \
                            cache[0].rearrange("g t h d -> g t (h d)")
                        pool.dma_start(dst[:, s, p, :], v[ds(page, 1), :, :].rearrange("g t d -> (g t) d")
                                       ).then_inc(kv_in[s], 16)
            else:
                for cache, dst in ((a["cache_mem_k"], kpg), (a["cache_mem_v"], vpg)):
                    v = cache[c["layer"]].rearrange("b (t p) h d -> b p t (h d)", p=128)
                    src = v[b] if isinstance(b, int) else v[ds(b, 1)].rearrange("g p t d -> (g p) t d")
                    pool.dma_start(dst[:, s], src).then_inc(kv_in[s], 16)

        for s in range(2):
            load(s, s)
        with pool.Fori(1, NB // 2) as i:
            for s in range(2):
                pool.wait_ge(S["bpv_ps"], i * 2 + (c["batch0"] + s - 1))
                load(i * 2 + s, s)

    def batch_pe(pe, kind):
        c = ATT[kind]
        R, C, b0 = c["rows"], c["c"], c["batch0"]

        def step(i, s, first):
            n = i * 2 + (b0 + s)
            b = i * 2 + s
            pe.wait_ge(kv_in[s], i * c["dma"] + (c["kv0"] + c["dma"]))
            if not first:
                pe.wait_ge(S["kt_ev"], n * 4)
            for p in range(2):
                for half in range(2):
                    for j in range(4):
                        at = 512 * half + 128 * j
                        last = nc.tensor.transpose(ps[:, 4 + 2 * p + half, 128 * j:128 * j + 128],
                                                   kpg[:, s, p, at:at + 128], ident)
                    last.then_inc(S["kt_ps"], 1)
            pe.wait_ge(S["qp_ready"], n + 1)
            pe.wait_ge(S["kt_ev"], n * 4 + 4)
            if not first:
                pe.wait_ge(S["bexp_ready"], n)
            for blk in range(8):
                last = nc.tensor.matmul(ps[0:R, 0, 0:256], qpadf[:, R * blk:R * blk + R], kTb[:, blk, :],
                                        start=(blk == 0), stop=(blk == 7), skip_group_check=True)
            if c["diff"]:
                nc.tensor.matmul(ps[:, 0, 256:T], identb[:], mask("m_new")[:, ds(b * 64, 64)] if
                                 not isinstance(b, int) else mask("m_new")[:, 64 * b:64 * b + 64], start=True,
                                 stop=False, skip_group_check=True)
                for blk in range(8):
                    last = nc.tensor.matmul(ps[:, 0, 256:T], qpadf[:, R * blk:R * blk + R], zc[:, 8 + blk, NP:T],
                                            start=False, stop=(blk == 7), skip_group_check=True)
            last.then_inc(S["bsc_ps"], 1)
            pe.wait_ge(S["bfr_ready"], n + 1)
            for kt in range(2):
                last = nc.tensor.matmul(ps[:, 1, 64 * kt:64 * kt + C], pb[0:R, 128 * kt:128 * kt + 128],
                                        fr[0:R, 0:C], start=True, stop=True)
            if c["diff"]:
                last = nc.tensor.matmul(ps[0:64, 1, 128:192], pb[:, 256:T], fr, start=True, stop=True)
            last.then_inc(S["bat_ps"], 1)
            pe.wait_ge(S["bat_ev"], n + 1)
            if not first:
                pe.wait_ge(S["bpv_ev"], n)
            for blk in range(8):
                q = 8 * head_of(c, blk)
                for kt in range(2):
                    last = nc.tensor.matmul(ps[:, 2, 8 * blk:8 * blk + 8], vpg[:, s, kt, 128 * blk:128 * blk + 128],
                                            aTb[:, kt, q:q + 8], start=(kt == 0), stop=(kt == 1 and not c["diff"]),
                                            skip_group_check=True)
                if c["diff"]:
                    last = nc.tensor.matmul(ps[:, 2, 8 * blk:8 * blk + 8], vtok3[0:64, 2, 128 * blk:128 * blk + 128],
                                            aTb[0:64, 2, q:q + 8], start=False, stop=True, skip_group_check=True)
            last.then_inc(S["bpv_ps"], 1)

        if kind == "m0":
            step(0, 0, True)
            step(0, 1, False)
            start = 1
        else:
            start = 0
        with pe.Fori(start, NB // 2) as i:
            for s in range(2):
                step(i, s, False)

    def batch_act(act, kind):
        c = ATT[kind]
        R, C, b0, W = c["rows"], c["c"], c["batch0"], c["width"]
        with act.Fori(0, NB // 2) as i:
            for s in range(2):
                n = i * 2 + (b0 + s)
                act.wait_ge(S["bmax_ready"], n + 1)
                nc.scalar.activation(pb[0:R, 0:W], ps[0:R, 0, 0:W], ACT.Exp, bias=sst[0:R, 0, 0:1],
                                     scale=c["scale"], accum_out=sst[0:R, 1, 0:1]).then_inc(S["bexp_ready"], 1)
                act.wait_ge(S["bat_ps"], n + 1)
                if c["diff"]:
                    nc.scalar.copy(aTb[0:64, 2, :], ps[0:64, 1, 128:192])
                nc.scalar.copy(aTb[:, 0:2, 0:C], ps[:, 1, 0:128].rearrange("p (t c) -> p t c", t=2)[:, :, 0:C]
                               ).then_inc(S["bat_ev"], 1)

    def batch_dve(dve, link, kind):
        c = ATT[kind]
        R, C, b0, W = c["rows"], c["c"], c["batch0"], c["width"]
        dve.wait_ge(S["ppv_ps"], c["tile0"] + c["nt"])
        link(nc.vector.memset(qpadf[:], 0.0))
        rounds = NB // 2
        with dve.Fori(0, rounds) as i:
            link.enter(i, 6 if c["diff"] else 4)
            for s in range(2):
                n = i * 2 + (b0 + s)
                at = ds(i * 16 + (NP + 8 * s), 8)
                if not (kind == "m0" and s == 0):
                    dve.wait_ge(S["bsc_ps"], n)
                if c["diff"]:
                    for m in range(2):
                        r = slice(64 * m, 64 * m + 64)
                        last = nc.vector.tensor_copy(qdiag[r, :, 8 * m:8 * m + 8], zc[r, 0:8, at])
                else:
                    last = nc.vector.tensor_copy(qmem[:, :, :, 0:8],
                                                 zc[:, 0:8, at].rearrange("p (h c) t -> p h c t", h=4))
                last.then_inc(S["qp_ready"], 1)
                for p in range(2):
                    for half in range(2):
                        dve.wait_ge(S["kt_ps"], n * 4 + (2 * p + half + 1))
                        nc.vector.tensor_copy(kTb[:, 4 * half:4 * half + 4, 128 * p:128 * p + 128],
                                              ps[:, 4 + 2 * p + half, :].rearrange("p (a b) -> p a b", a=4)
                                              ).then_inc(S["kt_ev"], 1)
                dve.wait_ge(S["bsc_ps"], n + 1)
                link(nc.vector.reduce_max(sst[0:R, 2, 0:1], ps[0:R, 0, 0:W], AX.X))
                nc.vector.tensor_scalar(sst[0:R, 0, 0:1], sst[0:R, 2, 0:1], -c["scale"], None, ALU.mult
                                        ).then_inc(S["bmax_ready"], 1)
                dve.wait_ge(S["bexp_ready"], n + 1)
                link(nc.vector.reciprocal(sst[0:R, 3, 0:1], sst[0:R, 1, 0:1]))
                if c["diff"]:
                    link(nc.vector.tensor_tensor(sst[:, 3, 0:1], sst[:, 3, 0:1], lams[:, 6:7], ALU.mult))
                fold = const("fold_heads") if c["diff"] else ident[0:32, 0:32]
                nc.vector.tensor_scalar(fr[0:R, 0:C], fold, sst[0:R, 3, 0:1], None, ALU.mult
                                        ).then_inc(S["bfr_ready"], 1)
                dve.wait_ge(S["bpv_ps"], n + 1)
                nc.vector.tensor_copy(xn[:, :, at], ps[:, 2, 0:64].rearrange("p (b q) -> p b q", b=8)
                                      ).then_inc(S["bpv_ev"], 1)
        link.leave(rounds)

    def rope_pe(pe):
        pe.wait_ge(S["w_ev"], UNIT["out_c"][0])
        for blk in range(16):
            if blk >= 4:
                pe.wait_ge(S["rot_done"], blk - 3)
            nc.tensor.matmul(ps[:, blk % 4, 0:T], const("rot"), zc[:, blk, :], start=True, stop=True
                             ).then_inc(S["rot_ps"], 1)
        g = G_DA
        for src in (8, 16):
            for t0, n in TILES:
                for half in range(2):
                    if src == 8:
                        pe.wait_ge(S["rot_done"], 16)
                    tr_pe(pe, g, [zc[:, src + 4 * half + j, t0:t0 + n] for j in range(4)], 128)
                    g += 1

    def rope_pool(pool, link):
        for blk in range(16):
            pool.wait_ge(S["rot_ps"], blk + 1)
            nc.gpsimd.tensor_tensor(zc[:, blk, :], zc[:, blk, :], const("cos"), ALU.mult
                                    ).then_inc(S["rot_cos"], 1)

    def rope_dve(dve, link):
        for blk in range(16):
            dve.wait_ge(S["rot_ps"], blk + 1)
            link(nc.vector.tensor_tensor(rstd[:, blk % 2, :], ps[:, blk % 4, 0:T], const("sin"), ALU.mult))
            dve.wait_ge(S["rot_cos"], blk + 1)
            nc.vector.tensor_tensor(zc[:, blk, :], zc[:, blk, :], rstd[:, blk % 2, :], ALU.add
                                    ).then_inc(S["rot_done"], 1)
        lv = lamv.rearrange("p (a d) -> p a d", a=4)
        dve.wait_ge(S["rot_done"], 16)
        link(nc.vector.tensor_tensor(rstd[:, 0, 0:128].rearrange("p (a d) -> p a d", a=2), lv[:, 0::2, :],
                                     lv[:, 1::2, :], ALU.mult))
        nc.vector.reduce_sum(lams[:, 0:2], rstd[:, 0, 0:128].rearrange("p (a d) -> p a d", a=2), AX.X
                             ).then_inc(S["lam_arg"], 1)
        dve.wait_ge(S["lam_exp"], 1)
        lam_init = 0.8 - 0.6 * math.exp(-0.3)
        link(nc.vector.tensor_tensor(lams[:, 4:5], lams[:, 3:4], lams[:, 2:3], ALU.subtract))
        link(nc.vector.tensor_scalar(lams[:, 4:5], lams[:, 4:5], -(1.0 + lam_init), None, ALU.add))
        for col, name in ((5, "map_pair"), (6, "map_heads")):
            link(nc.vector.tensor_scalar(lams[:, col:col + 1], const(name), lams[:, 4:5], 1.0, ALU.mult, ALU.add))
        g = G_DA
        for dst in (ktok3, vtok3):
            for i, (t0, n) in enumerate(TILES):
                for half in range(2):
                    tr_dve(dve, g, dst[0:n, i, 512 * half:512 * half + 512].rearrange("p (a b) -> p a b", a=4), n,
                           128)
                    g += 1

    def subln_pe(pe):
        pe.wait_ge(S["osq_ready"], 1)
        pe.wait_ge(S["ppv_ev"], ATT["d"]["tile0"] + 4)
        pe.wait_ge(S["bpv_ev"], ATT["d"]["batch0"] + 8)
        for h in range(HC):
            last = nc.tensor.matmul(ps[:, h, 0:T], ones[:], sq[:, h, :], start=True, stop=True)
        last.then_inc(S["osum_ready"], 1)

    def subln_act(act):
        act.wait_ge(S["bpv_ev"], ATT["d"]["batch0"] + 8)
        nc.scalar.activation(sq[:], xn[:], ACT.Square).then_inc(S["osq_ready"], 1)
        act.wait_ge(S["osum_ready"], 1)
        nc.scalar.activation(sq[:], ps[:, :, 0:T], ACT.Sqrt, bias=epsc[:, 0:1], scale=1.0 / 128
                             ).then_inc(S["ostd_ready"], 1)

    def subln_dve(dve, link):
        lam_init = 0.8 - 0.6 * math.exp(-0.3)
        v = VEC["subln"]
        link(nc.vector.tensor_scalar(lams[:, 7:8], vec[:, v:v + 1], 1.0 - lam_init, None, ALU.mult))
        dve.wait_ge(S["ostd_ready"], 1)
        link(nc.vector.reciprocal(sq[:], sq[:]))
        nc.vector.scalar_tensor_tensor(xn[:], xn[:], lams[:, 7:8], sq[:], ALU.mult, ALU.mult
                                       ).then_inc(S["on_ready"], 1)
        dve.wait_ge(S["on_ready"], 1)

    def route_pe(pe, l):
        for i, (t0, n) in enumerate(TILES):
            for k in range(KD):
                last = nc.tensor.matmul(ps[0:n, 5, 36 * i:36 * i + 36], xn[:, k, t0:t0 + n], wrt[:, l, k, :],
                                        start=(k == 0), stop=(k == KD - 1))
        last.then_inc(S["lg_ps"], 1)
        pe.wait_ge(S["gate_ready"], l + 1)
        for i, (t0, n) in enumerate(TILES):
            last = nc.tensor.transpose(ps[0:32, 6, t0:t0 + n], gate[0:n, i, :], ident[0:n, 0:n])
        last.then_inc(S["gt_ps"], 1)
        pe.wait_ge(S["gt_ev"], l + 1)
        for e in range(NE):
            n = NE * l + e
            if e >= 4:
                pe.wait_ge(S["gbc_ev"], n - 3)
            nc.tensor.matmul(ps[:, 4 + e % 4, 0:T], ident[0:32, e:e + 1].to_broadcast([32, 128]), gT[0:32, :],
                             start=True, stop=True).then_inc(S["gbc_ps"], 1)

    def route_act(act, l):
        act.wait_ge(S["gsel_ready"], l + 1)
        nc.scalar.activation(rt[:, 4, :, 0:4], rt[:, 3, :, 0:4], ACT.Exp).then_inc(S["gexp_ready"], 1)
        act.wait_ge(S["rexp_ready"], 2 * l + 1)
        nc.scalar.activation(rt[:, 15, :, 0:1], rt[:, 14, :, 0:1], ACT.Exp).then_inc(S["rexp_ready"], 1)
        for e in range(NE):
            act.wait_ge(S["gbc_ps"], NE * l + e + 1)
            nc.scalar.copy(gbc[:, e, :], ps[:, 4 + e % 4, 0:T]).then_inc(S["gbc_ev"], 1)

    def route_dve(dve, link, l):
        V = nc.vector

        def bc(x, w):
            return x.to_broadcast([128, 3, w])

        link(V.memset(lg[:, 2, :], 0.0))
        dve.wait_ge(S["lg_ps"], l + 1)
        V.tensor_tensor(lg[:, 0:2, :], ps[:, 5, 0:72].rearrange("p (t n) -> p t n", t=2),
                        brt[:, l, :].unsqueeze(1).to_broadcast([128, 2, 36]), ALU.add)
        link(V.tensor_tensor(lg[0:64, 2, :], ps[0:64, 5, 72:108], brt[0:64, l, :], ALU.add))
        gl, el = lg[:, :, 0:4], lg[:, :, 4:36].rearrange("p t (g e) -> p t g e", g=4)

        def first_max(x, w, rank, at, oh):
            link(V.reduce_max(rt[:, at, :, 0:1], x, AX.X))
            link(V.tensor_tensor(rt[:, at + 1, :, 0:w], x, bc(rt[:, at, :, 0:1], w), ALU.is_equal))
            link(V.tensor_tensor(rt[:, at + 1, :, 0:w], rt[:, at + 1, :, 0:w],
                                 const(rank).unsqueeze(1).to_broadcast([128, 3, w]), ALU.mult))
            link(V.reduce_max(rt[:, at, :, 1:2], rt[:, at + 1, :, 0:w], AX.X))
            link(V.tensor_tensor(oh, rt[:, at + 1, :, 0:w], bc(rt[:, at, :, 1:2], w), ALU.is_equal))

        ohg = rt[:, 2, :, 0:4]
        first_max(gl, 4, "rank_g", 0, ohg)
        V.tensor_tensor(rt[:, 3, :, 0:4], gl, bc(rt[:, 0, :, 0:1], 4), ALU.subtract).then_inc(S["gsel_ready"], 1)
        prod = rt[:, 16:20].rearrange("p a t e -> p (a t e)").rearrange("p (t g e) -> p t g e", t=3, g=4)
        link(V.tensor_tensor(prod, el, ohg.unsqueeze(3).to_broadcast([128, 3, 4, 8]), ALU.mult))
        es, oh1, es2, oh2 = rt[:, 5], rt[:, 8], rt[:, 9], rt[:, 12]
        link(V.tensor_tensor(es, prod[:, :, 0, :], prod[:, :, 1, :], ALU.add))
        link(V.tensor_tensor(es, es, prod[:, :, 2, :], ALU.add))
        link(V.tensor_tensor(es, es, prod[:, :, 3, :], ALU.add))
        first_max(es, 8, "rank_e", 6, oh1)
        link(V.tensor_scalar(es2, oh1, -BIG, None, ALU.mult))
        link(V.tensor_tensor(es2, es2, es, ALU.add))
        first_max(es2, 8, "rank_e", 10, oh2)
        V.tensor_tensor(rt[:, 14, :, 0:1], rt[:, 10, :, 0:1], rt[:, 6, :, 0:1], ALU.subtract
                        ).then_inc(S["rexp_ready"], 1)
        dve.wait_ge(S["gexp_ready"], l + 1)
        link(V.reduce_sum(rt[:, 13, :, 0:1], rt[:, 4, :, 0:4], AX.X))
        dve.wait_ge(S["rexp_ready"], 2 * l + 2)
        link(V.tensor_scalar(rt[:, 13, :, 1:2], rt[:, 15, :, 0:1], 1.0, None, ALU.add))
        link(V.tensor_tensor(rt[:, 13, :, 2:3], rt[:, 13, :, 0:1], rt[:, 13, :, 1:2], ALU.mult))
        link(V.reciprocal(rt[:, 13, :, 3:4], rt[:, 13, :, 2:3]))
        link(V.tensor_tensor(oh2, oh2, bc(rt[:, 15, :, 0:1], 8), ALU.mult))
        link(V.tensor_tensor(oh1, oh1, oh2, ALU.add))
        link(V.tensor_tensor(oh1, oh1, bc(rt[:, 13, :, 3:4], 8), ALU.mult))
        for i in range(3):
            last = V.tensor_tensor(gate[:, i, :].rearrange("p (g e) -> p g e", g=4),
                                   ohg[:, i, :].unsqueeze(2).to_broadcast([128, 4, 8]),
                                   oh1[:, i, :].unsqueeze(1).to_broadcast([128, 4, 8]), ALU.mult)
        last.then_inc(S["gate_ready"], 1)
        dve.wait_ge(S["gt_ps"], l + 1)
        V.tensor_copy(gT[0:32, :], ps[0:32, 6, 0:T]).then_inc(S["gt_ev"], 1)

    def moe_pe(pe, l):
        u0 = UNIT[f"moe{l}"][0]
        pe.wait_ge(S["in_lo"], (6, 11)[l])

        def up(u, s, bank):
            pe.wait_ge(S["w_lo"], u + 1)
            for j in range(2):
                for k in range(KD):
                    last = mm3(ps[:, bank + j, 0:T], s, k, 128 * j, xh[:, k, :], xl[:, k, :], k == 0, k == KD - 1)
            last.then_inc(S["w_used"], 1)

        def down(u, s, bank):
            pe.wait_ge(S["w_lo"], u + 1)
            for j in range(4):
                for k in range(4):
                    last = mm3(ps[:, bank + j, 0:T], s, k, 128 * j, hh[:, k, :], hl[:, k, :], k == 0, k == 3, 512)
            last.then_inc(S["w_used"], 1)

        pe.wait_ge(S["w_ev"], u0)
        up(u0, 0, 0)
        up(u0 + 1, 1, 2)
        pe.wait_ge(S["gbc_ev"], NE * (l + 1))
        up(u0 + 2, 0, 4)
        up(u0 + 3, 1, 6)
        with pe.Fori(1, NE // 2) as i:
            u = i * 6 + (u0 - 2)
            pe.wait_ge(S["w_ev"], u - 2)
            up(u, 0, 0)
            up(u + 1, 1, 2)
            pe.wait_ge(S["w_ev"], u)
            pe.wait_ge(S["mhl_ready"], i * 2 + NE * l)
            down(u + 2, 0, 4)
            pe.wait_ge(S["w_ev"], u + 2)
            down(u + 3, 1, 0)
            pe.wait_ge(S["w_ev"], u + 3)
            up(u + 4, 0, 4)
            up(u + 5, 1, 6)
        u = u0 + 94
        pe.wait_ge(S["w_ev"], u)
        pe.wait_ge(S["mhl_ready"], NE * (l + 1))
        down(u, 0, 4)
        down(u + 1, 1, 0)

    def moe_act(act, l, last_layer):
        u0 = UNIT[f"moe{l}"][0]

        def hi(u, s):
            act.wait_ge(S["w_used"], u + 1)
            split_hi(act, u + 2, s)

        def sig(u, bank, prev):
            if prev is not None:
                act.wait_ge(S["w_ev"], prev + 1)
            nc.scalar.activation(e_t, ps[:, bank:bank + 2, 0:T], ACT.Exp, scale=-1.0 / WSCALE
                                 ).then_inc(S["mexp_ready"], 1)

        def hid(n, j):
            act.wait_ge(S["mc_ready"], n + 1)
            nc.scalar.copy(hh[:, 2 * j:2 * j + 2, :], cg[:, j]).then_inc(S["mhh_ready"], 1)

        n0_ = NE * l
        hi(u0, 0)
        sig(u0, 0, None)
        hi(u0 + 1, 1)
        hid(n0_, 0)
        hi(u0 + 2, 0)
        sig(u0 + 2, 4, u0 + 1)
        hi(u0 + 3, 1)
        hid(n0_ + 1, 1)
        with act.Fori(1, NE // 2) as i:
            u = i * 6 + (u0 - 2)
            n = i * 2 + n0_
            hi(u, 0)
            sig(u, 0, u - 1)
            hi(u + 1, 1)
            hi(u + 2, 0)
            hi(u + 3, 1)
            hid(n, 0)
            hi(u + 4, 0)
            sig(u + 4, 4, u + 1)
            hi(u + 5, 1)
            hid(n + 1, 1)
        if not last_layer:
            hi(u0 + 94, 0)
            hi(u0 + 95, 1)

    def moe_pool(pool, link, l):
        def gated(u, n, e, j):
            pool.wait_ge(S["w_ev"], u + 1)
            if not isinstance(n, int) or n >= 2:
                pool.wait_ge(S["mhl_ready"], n - 1)
            for c in range(2):
                g = gbc[:, e, :] if isinstance(e, int) else gbc[:, ds(e, 1), :].rearrange("p a t -> p (a t)")
                last = nc.gpsimd.tensor_tensor(cg[:, j, c, :], b_t[:, c, :], g, ALU.mult)
            last.then_inc(S["mc_ready"], 1)

        u0 = UNIT[f"moe{l}"][0]
        pool.wait_ge(S["gbc_ev"], NE * (l + 1))
        gated(u0 + 1, NE * l, 0, 0)
        gated(u0 + 3, NE * l + 1, 1, 1)
        with pool.Fori(1, NE // 2) as i:
            u = i * 6 + (u0 - 2)
            gated(u + 1, i * 2 + NE * l, i * 2, 0)
            gated(u + 5, i * 2 + (NE * l + 1), i * 2 + 1, 1)

    def moe_dve(dve, link, l, last_layer):
        u0 = UNIT[f"moe{l}"][0]

        def lo(u, s):
            dve.wait_ge(S["w_used"], u + 1)
            split_lo(dve, u + 2, s)

        def act_fn(u, n, bank, nfirst=False):
            dve.wait_ge(S["mexp_ready"], n + 1)
            link(nc.vector.tensor_scalar(r_t, e_t, 1.0, None, ALU.add))
            link(nc.vector.reciprocal(r_t, r_t))
            nc.vector.scalar_tensor_tensor(a_t, ps[:, bank:bank + 2, 0:T], 1 / WSCALE, r_t, ALU.mult, ALU.mult
                                           ).then_inc(S["w_ev"], 1)
            dve.wait_ge(S["w_ev"], u + 1)
            if not nfirst:
                dve.wait_ge(S["mc_ready"], n)
            nc.vector.scalar_tensor_tensor(b_t, ps[:, bank + 2:bank + 4, 0:T], 1 / WSCALE, a_t, ALU.mult, ALU.mult
                                           ).then_inc(S["w_ev"], 1)

        def low(n, j):
            dve.wait_ge(S["mhh_ready"], n + 1)
            nc.vector.tensor_tensor(hl[:, 2 * j:2 * j + 2, :], cg[:, j], hh[:, 2 * j:2 * j + 2, :], ALU.subtract
                                    ).then_inc(S["mhl_ready"], 1)

        def add(half, bank):
            x = xT[:, 4 * half:4 * half + 4, :]
            nc.vector.scalar_tensor_tensor(x, ps[:, bank:bank + 4, 0:T], 1 / WSCALE, x, ALU.mult, ALU.add
                                           ).then_inc(S["w_ev"], 1)

        n0_ = NE * l
        lo(u0, 0)
        lo(u0 + 1, 1)
        act_fn(u0, n0_, 0, nfirst=(l == 0))
        low(n0_, 0)
        lo(u0 + 2, 0)
        lo(u0 + 3, 1)
        act_fn(u0 + 2, n0_ + 1, 4)
        low(n0_ + 1, 1)
        with dve.Fori(1, NE // 2) as i:
            link.enter(i - 1, 4)
            u = i * 6 + (u0 - 2)
            n = i * 2 + n0_
            lo(u, 0)
            lo(u + 1, 1)
            act_fn(u, n, 0)
            lo(u + 2, 0)
            add(0, 4)
            lo(u + 3, 1)
            add(1, 0)
            low(n, 0)
            lo(u + 4, 0)
            lo(u + 5, 1)
            act_fn(u + 4, n + 1, 4)
            low(n + 1, 1)
        link.leave(NE // 2 - 1)
        if last_layer:
            dve.wait_ge(S["w_used"], u0 + 95)
            add(0, 4)
            dve.wait_ge(S["w_used"], u0 + 96)
            add(1, 0)
        else:
            lo(u0 + 94, 0)
            add(0, 4)
            lo(u0 + 95, 1)
            add(1, 0)
        dve.wait_ge(S["w_ev"], u0 + 96)

    def pe_memory(pe, l):
        n = 1 + 3 * l
        norm_pe(pe, n)
        gemm_pe(pe, f"memq{l}", (3, 8)[l])
        pe.wait_ge(S["w_ev"], sum(UNIT[f"memq{l}"]))
        prompt_pe(pe, f"m{l}")
        batch_pe(pe, f"m{l}")
        pe.wait_ge(S["bpv_ev"], ATT[f"m{l}"]["batch0"] + 8)
        gemm_pe(pe, f"memo{l}", (4, 9)[l])
        norm_pe(pe, n + 1)
        pe.wait_ge(S["xn_ready"], n + 2)
        route_pe(pe, l)
        moe_pe(pe, l)

    def pe_rest(pe):
        pe.wait_ge(S["vec_in"], NVIN)
        pe_memory(pe, 0)
        norm_pe(pe, 3)
        gemm_pe(pe, "qkv", 6)
        rope_pe(pe)
        pe.wait_ge(S["tr_ev"], G_Y)
        prompt_pe(pe, "d")
        batch_pe(pe, "d")
        subln_pe(pe)
        pe.wait_ge(S["ostd_ready"], 1)
        gemm_pe(pe, "out_c", 7)
        pe_memory(pe, 1)
        norm_pe(pe, 6)
        pe.wait_ge(S["xn_ready"], 7)
        g = G_Y
        for i, (t0, n) in enumerate(TILES):
            for half in range(2):
                tr_pe(pe, g, [xn[:, 4 * half + j, t0:t0 + n] for j in range(4)], 128)
                g += 1

    def act_memory(act, link, l):
        n = 1 + 3 * l
        norm_act(act, n)
        act.wait_ge(S["xn_ready"], n + 1)
        input_act(act, xn[:])
        gemm_copy_act(act, f"memq{l}", z[:, 0:8])
        prompt_act(act, f"m{l}")
        batch_act(act, f"m{l}")
        act.wait_ge(S["bpv_ev"], ATT[f"m{l}"]["batch0"] + 8)
        input_act(act, xn[:])
        gemm_split_act(act, f"memo{l}")
        act.wait_ge(S["w_ev"], sum(UNIT[f"memo{l}"]))
        norm_act(act, n + 1)
        act.wait_ge(S["xn_ready"], n + 2)
        input_act(act, xn[:])
        route_act(act, l)
        moe_act(act, l, l == 1)

    def act_rest(act, link):
        act.wait_ge(S["w_ev"], sum(UNIT["out_a"]))
        act.wait_ge(S["out_c"], 16 * 10)
        act.wait_ge(c_out[0], 32)
        act.wait_ge(c_out[1], 32)
        act_memory(act, link, 0)
        act.wait_ge(S["w_ev"], sum(UNIT["moe0"]))
        norm_act(act, 3)
        act.wait_ge(S["xn_ready"], 4)
        input_act(act, xn[:])
        gemm_copy_act(act, "qkv", zc[:])
        act.wait_ge(S["lam_arg"], 1)
        nc.scalar.activation(lams[:, 2:4], lams[:, 0:2], ACT.Exp).then_inc(S["lam_exp"], 1)
        prompt_act(act, "d")
        batch_act(act, "d")
        subln_act(act)
        act.wait_ge(S["on_ready"], 1)
        input_act(act, xn[:])
        gemm_split_act(act, "out_c")
        act.wait_ge(S["w_ev"], sum(UNIT["out_c"]))
        act_memory(act, link, 1)
        act.wait_ge(S["w_ev"], sum(UNIT["moe1"]))
        norm_act(act, 6)

    def dve_memory(dve, link, l):
        n = 1 + 3 * l
        norm_dve(dve, link, n)
        input_dve(dve, (3, 8)[l], xn[:])
        gemm_split_dve(dve, f"memq{l}")
        dve.wait_ge(S["w_ev"], sum(UNIT[f"memq{l}"]))
        prompt_dve(dve, link, f"m{l}")
        batch_dve(dve, link, f"m{l}")
        dve.wait_ge(S["bpv_ev"], ATT[f"m{l}"]["batch0"] + 8)
        input_dve(dve, (4, 9)[l], xn[:])
        gemm_add_dve(dve, f"memo{l}")
        norm_dve(dve, link, n + 1)
        input_dve(dve, (5, 10)[l], xn[:])
        route_dve(dve, link, l)
        moe_dve(dve, link, l, l == 1)

    def dve_rest(dve, link):
        dve_memory(dve, link, 0)
        norm_dve(dve, link, 3)
        input_dve(dve, 6, xn[:])
        gemm_split_dve(dve, "qkv")
        rope_dve(dve, link)
        prompt_dve(dve, link, "d")
        batch_dve(dve, link, "d")
        subln_dve(dve, link)
        input_dve(dve, 7, xn[:])
        gemm_add_dve(dve, "out_c")
        dve_memory(dve, link, 1)
        norm_dve(dve, link, 6)
        g = G_Y
        for i, (t0, n) in enumerate(TILES):
            for half in range(2):
                tr_dve(dve, g, x_nat[0:n, i, 512 * half:512 * half + 512].rearrange("p (a b) -> p a b", a=4), n, 128)
                g += 1

    def pool_rest(pool, link):
        pool.wait_ge(S["out_c"], 16 * 10)
        pool.wait_ge(c_out[0], 32)
        pool.wait_ge(c_out[1], 32)
        pool.wait_ge(S["in_lo"], 3)
        batch_pool(pool, link, "m0")
        moe_pool(pool, link, 0)
        rope_pool(pool, link)
        pool.wait_ge(S["tr_ev"], G_Y)
        pool.dma_start(o["p_k"][0, 0].rearrange("(t p) h m d -> p t (h m d)", p=128), ktok3[:, 0:2, :]
                       ).then_inc(S["out_p"], 16)
        pool.dma_start(o["s_k"][0].rearrange("b i h m d -> (b i) (h m d)"), ktok3[0:64, 2, :]).then_inc(S["out_p"], 16)
        pool.dma_start(o["p_v"][0, 0].rearrange("(t p) h d -> p t (h d)", p=128), vtok3[:, 0:2, :]
                       ).then_inc(S["out_p"], 16)
        pool.dma_start(o["s_v"][0].rearrange("b i h d -> (b i) (h d)"), vtok3[0:64, 2, :]).then_inc(S["out_p"], 16)
        pool.wait_ge(S["out_p"], 64)
        batch_pool(pool, link, "d")
        pool.wait_ge(S["in_lo"], 8)
        batch_pool(pool, link, "m1")
        moe_pool(pool, link, 1)
        pool.wait_ge(S["tr_ev"], G_Y + 6)
        pool.dma_start(o["y_prompt"][0].rearrange("(t p) d -> p t d", p=128), x_nat[:, 0:2, :]).then_inc(S["out_y"], 16)
        pool.dma_start(o["y_sample"].rearrange("b i d -> (b i) d"), x_nat[0:64, 2, :]).then_inc(S["out_y"], 16)
        pool.wait_ge(S["out_y"], 32)

    @block.gpsimd
    def _(pool):
        link = Chain(pool, "pool_chain", "pool_loop")
        nc.gpsimd.memset(ones[:], 1.0)
        nc.gpsimd.memset(wgate[:], 0.0)
        nc.gpsimd.memset(epsc[:, 0:1], EPS)
        nc.gpsimd.memset(epsc[:, 1:2], 1.0).then_inc(S["cst_ready"], 1)
        pool.dma_start(cst[:], a["consts"]).then_inc(S["const_in"], 16)
        pool.dma_start(mem_nat, a["mem_prompt"][0].rearrange("(t p) d -> p t d", p=128)).then_inc(S["mem_in"], 16)
        pool.dma_start(x_nat[:, 0:2, :], a["x_prompt"][0].rearrange("(t p) d -> p t d", p=128)
                       ).then_inc(S["x_in"], 16)
        pool.dma_start(x_nat[0:64, 2, :], a["x_sample"].rearrange("b i d -> (b i) d")).then_inc(S["x_in"], 16)
        r = 0
        for name in ("norm_mix_g", "norm_mem_g", "norm_ffn_g"):
            pool.dma_start(vecs[r:r + 16, :], a[name].rearrange("l (k p) -> (l k) p", p=128)
                           ).then_inc(S["vec_in"], 16)
            r += 16
        pool.dma_start(vecs[r:r + 8, :], a["final_norm_g"].rearrange("(k p) -> k p", p=128)
                       ).then_inc(S["vec_in"], 16)
        pool.dma_start(vecs[r + 8:r + 12, :], a["head_norm_g_a"][0].rearrange("(k p) -> k p", p=128)
                       ).then_inc(S["vec_in"], 16)
        pool.dma_start(vecs[r + 12:r + 13, :], a["subln_g_c"]).then_inc(S["vec_in"], 16)
        pool.dma_start(vecs[r + 13:r + 25, :], a["conv_w_b"][0].rearrange("j (k p) -> (j k) p", p=128)
                       ).then_inc(S["vec_in"], 16)
        pool.dma_start(ptab[:], a["page_table"].rearrange("b n -> (b n)").unsqueeze(0)).then_inc(S["tab_in"], 16)
        pool.wait_ge(S["tab_in"], 16)
        pool.wait_ge(S["cst_ready"], 1)
        wg = a["w_in_a"][0].rearrange("(k p) n -> p k n", p=128)
        pool.dma_start(wgate[:, :, 0:4], wg[:, :, 2048:2052]).then_inc(S["gate_in"], 16)
        pool.dma_start(wgate[:, :, 32:36], wg[:, :, 2052:2056]).then_inc(S["gate_in"], 16)
        pool.dma_start(gbias[0:4, :], a["gate_b_a"][0, 0].rearrange("(h o) -> h o", o=1)).then_inc(S["vec_in"], 16)
        pool.dma_start(gbias[32:36, :], a["gate_b_a"][0, 1].rearrange("(h o) -> h o", o=1)
                       ).then_inc(S["vec_in"], 16)
        for l in range(2):
            pool.dma_start(wrt[:, l, :, 0:4], a["w_router_g"][l].rearrange("(k p) n -> p k n", p=128)
                           ).then_inc(S["vec_in"], 16)
            pool.dma_start(wrt[:, l, :, 4:36], a["w_router_e"][l].rearrange("(k p) n -> p k n", p=128)
                           ).then_inc(S["vec_in"], 16)
            pool.dma_start(brt[:, l, 0:4], a["b_router_g"][l].partition_broadcast(128)).then_inc(S["vec_in"], 16)
            pool.dma_start(brt[:, l, 4:36], a["b_router_e"][l].partition_broadcast(128)).then_inc(S["vec_in"], 16)
        pool.dma_start(lamv[:], a["lambda_c"][0].rearrange("a b -> (a b)").partition_broadcast(128)
                       ).then_inc(S["vec_in"], 16)
        for l in range(2):
            pool.wait_ge(S["tr_ev"], G_MKV + 8 * l + 4)
            pool.dma_start(o["p_mem_k"][l, 0].rearrange("(t p) h d -> p t (h d)", p=128), mk_out
                           ).then_inc(S["out_mem"], 16)
            pool.wait_ge(S["tr_ev"], G_MKV + 8 * l + 8)
            pool.dma_start(o["p_mem_v"][l, 0].rearrange("(t p) h d -> p t (h d)", p=128), memv[:, l]
                           ).then_inc(S["out_mem"], 16)
        pool.wait_ge(S["out_mem"], 64)
        pool.wait_ge(S["in_lo"], 2)
        mlstm_pool(pool, link)
        mlstm_pool_out(pool, link)
        pool_rest(pool, link)

    @block.tensor
    def _(pe):
        pe.wait_ge(S["const_in"], 16)
        pe.wait_ge(S["cst_ready"], 1)
        g = G_X
        pe.wait_ge(S["x_in"], 32)
        for i, (t0, n) in enumerate(TILES):
            for half in range(2):
                tr_pe(pe, g, [x_nat[0:n, i, 512 * half + 128 * j:512 * half + 128 * j + 128] for j in range(4)], n)
                g += 1
        pe.wait_ge(S["mem_in"], 16)
        for i in range(2):
            for half in range(2):
                tr_pe(pe, g, [mem_nat[:, i, 512 * half + 128 * j:512 * half + 128 * j + 128] for j in range(4)], 128)
                g += 1
        pe.wait_ge(S["vec_in"], NVIN)
        pe.wait_ge(S["tr_ev"], G_MKV)
        nc.tensor.transpose(ps[:, 4, 0:NVEC], vecs[:], ident[0:NVEC, 0:NVEC]).then_inc(S["vec_ps"], 1)
        pe.wait_ge(S["vec_ev"], 1)
        for l in range(2):
            for kv in range(2):
                name = ("memk", "memv")[kv] + str(l)
                gemm_pe(pe, name, 0, 256)
                pe.wait_ge(S["w_ev"], sum(UNIT[name]))
                src = memkT[:, l] if kv == 0 else mvT
                for i in range(2):
                    for half in range(2):
                        tr_pe(pe, g, [src[:, 4 * half + j, 128 * i:128 * i + 128] for j in range(4)], 128)
                        g += 1
        pe.wait_ge(S["tr_ev"], g)
        norm_pe(pe, 0)
        pe.wait_ge(S["xn_ready"], 1)
        mlstm_pe(pe)
        gemm_pe(pe, "out_a", 2)
        pe_rest(pe)

    @block.scalar
    def _(act):
        link = Chain(act, "act_chain", "act_loop")
        for s in range(2):
            split_hi(act, s, s)
        act.wait_ge(S["tr_ev"], G_MKV)
        input_act(act, sq[:, :, 0:256], 256)
        for l in range(2):
            gemm_copy_act(act, f"memk{l}", memkT[:, l], 256)
            if l:
                act.wait_ge(S["tr_ps"], G_MKV + 8)
            gemm_copy_act(act, f"memv{l}", mvT, 256)
        act.wait_ge(S["in_lo"], 1)
        norm_act(act, 0)
        act.wait_ge(S["xn_ready"], 1)
        input_act(act, xn[:])
        act.wait_ge(S["out_mem"], 64)
        gemm_copy_act(act, "in_a", z[:, 0:16])
        gemm_copy_act(act, "in_b", z[:, 16:28])
        mlstm_act(act, link)
        act.wait_ge(S["y_ready"], 1)
        input_act(act, xn[:])
        gemm_split_act(act, "out_a")
        act_rest(act, link)

    @block.vector
    def _(dve):
        link = Chain(dve, "dve_chain", "dve_loop")
        dve.wait_ge(S["const_in"], 16)
        nc.vector.tensor_copy(maskb[:], cst[:, m0:m0 + 768])
        link(nc.vector.tensor_copy(identb[:], ident))
        for s in range(2):
            split_lo(dve, s, s)
        g = G_X
        for i, (t0, n) in enumerate(TILES):
            for half in range(2):
                tr_dve(dve, g, xT[:, 4 * half:4 * half + 4, t0:t0 + n], 128, n)
                g += 1
        for i in range(2):
            for half in range(2):
                tr_dve(dve, g, sq[:, 4 * half:4 * half + 4, 128 * i:128 * i + 128], 128, 128)
                g += 1
        dve.wait_ge(S["vec_ps"], 1)
        nc.vector.tensor_copy(vec[:], ps[:, 4, 0:NVEC]).then_inc(S["vec_ev"], 1)
        dve.wait_ge(S["tr_ev"], G_MKV)
        input_dve(dve, 0, sq[:, :, 0:256], 256)
        for l in range(2):
            for kv in range(2):
                gemm_split_dve(dve, ("memk", "memv")[kv] + str(l))
                if kv == 0 and l == 1:
                    dve.wait_ge(S["out_mem"], 32)
                for i in range(2):
                    for half in range(2):
                        dst = mk_out if kv == 0 else memv[:, l]
                        tr_dve(dve, g, dst[:, i, 512 * half:512 * half + 512].rearrange("p (a b) -> p a b", a=4),
                               128, 128)
                        g += 1
        norm_dve(dve, link, 0)
        input_dve(dve, 1, xn[:])
        gemm_split_dve(dve, "in_a")
        gemm_split_dve(dve, "in_b")
        mlstm_dve(dve, link)
        input_dve(dve, 2, xn[:])
        gemm_add_dve(dve, "out_a")
        dve_rest(dve, link)



_INS = ['x_prompt', 'x_sample', 'state_mlstm_C', 'state_mlstm_n', 'state_mlstm_m', 'state_conv', 'cache_k', 'cache_v',
        'page_table', 'cache_mem_k', 'cache_mem_v', 'mem_prompt', 'norm_mix_g', 'norm_mem_g', 'norm_ffn_g',
        'final_norm_g', 'w_in_a', 'gate_b_a', 'head_norm_g_a', 'conv_w_b', 'w_out_a', 'w_qkv_c', 'lambda_c',
        'subln_g_c', 'w_out_c', 'w_mem_q', 'w_mem_k', 'w_mem_v', 'w_mem_o', 'w_router_g', 'b_router_g', 'w_router_e',
        'b_router_e', 'w_exp_gate', 'w_exp_up', 'w_exp_down']
_OUTS = [("y_prompt", (1, 256, 1024)), ("y_sample", (8, 8, 1024)), ("p_C", (1, 1, 4, 128, 128)),
         ("p_n", (1, 1, 4, 128)), ("p_m", (1, 1, 4)), ("p_conv", (1, 1, 2, 512)), ("p_k", (1, 1, 256, 8, 2, 64)),
         ("p_v", (1, 1, 256, 8, 128)), ("p_mem_k", (2, 1, 256, 4, 256)), ("p_mem_v", (2, 1, 256, 4, 256)),
         ("s_C", (1, 8, 4, 128, 128)), ("s_n", (1, 8, 4, 128)), ("s_m", (1, 8, 4)), ("s_conv", (1, 8, 2, 512)),
         ("s_k", (1, 8, 8, 8, 2, 64)), ("s_v", (1, 8, 8, 8, 128))]


def kernel(**inputs):
    import concourse.bacc as bacc
    from concourse import mybir
    from concourse.bass_utils import run_bass_kernel_spmd

    nc = bacc.Bacc("TRN2", target_bir_lowering=False, num_devices=1)
    arrays = {f"in_{n}": np.ascontiguousarray(inputs[n]) for n in _INS}
    arrays["in_consts"] = constants()
    a = {n[3:]: nc.dram_tensor(n, v.shape, mybir.dt.from_np(v.dtype), kind="ExternalInput").ap()
         for n, v in arrays.items()}
    o = {n: nc.dram_tensor(f"out_{n}", s, mybir.dt.float32, kind="ExternalOutput").ap() for n, s in _OUTS}
    build(nc, a, o)
    r = run_bass_kernel_spmd(nc, [arrays], core_ids=[0])
    return tuple(r.results[0][f"out_{n}"] for n, _ in _OUTS)
```

```python
import math

import numpy as np

D = 1024
KD = D // 128
NP, NB, NI = 256, 8, 8
NS = NB * NI
T = NP + NS
HA, HC, HM = 4, 8, 4
PAST, PAGE = 256, 128
NG, EPG = 4, 8
NE = NG * EPG
EPS = 1e-6
WSCALE = 64.0
BIG = 1e30
CAP = 64
NSLOT = 2 * T + CAP
SH = NSLOT // 2
TILES = ((0, 128), (128, 128), (256, 64))

CONST = {}
_at = 0
for _n, _w in (("ident", 128), ("rot", 128), ("fold_pair", 64), ("fold_heads", 64), ("m_tri", 128), ("m_samp", 64),
               ("m_pair", 64), ("m_new", 512), ("cos", T), ("sin", T), ("seg", T), ("segneg", T), ("rank_g", 4),
               ("rank_e", 8), ("map_pair", 1), ("map_heads", 1)):
    CONST[_n] = (_at, _w)
    _at += _w
NCONST = _at


def constants():
    f = np.float32
    c = np.zeros((128, NCONST), f)

    def put(name, a):
        at, w = CONST[name]
        c[:a.shape[0], at:at + w] = a

    p = np.arange(128)
    put("ident", np.eye(128, dtype=f))
    rot = np.zeros((128, 128), f)
    for m in range(128):
        if m % 64 < 32:
            rot[m + 32, m] = -1
        else:
            rot[m - 32, m] = 1
    put("rot", rot)
    put("fold_pair", (p[:, None] % 64 == np.arange(64)[None]).astype(f))
    h, t = p // 16, p % 8
    j = np.arange(64)
    put("fold_heads", ((h[:, None] == j[None] // 8) & (t[:, None] == j[None] % 8)).astype(f))
    neg = f(-BIG)
    put("m_tri", np.where(p[:, None] > p[None], neg, f(0)))
    put("m_samp", np.where((j[:, None] // 8 == j[None] // 8) & (j[:, None] <= j[None]), f(0), neg))
    put("m_pair", np.where(j[None] > p[:, None] % 64, neg, f(0)))
    b = np.arange(8)
    new = np.where((b[None, :, None] == j[None, None] // 8) & (j[None, None] % 8 <= t[:, None, None]), f(0), neg)
    put("m_new", new.reshape(128, 512).astype(f))
    pos = np.concatenate([np.arange(NP), np.tile(PAST + np.arange(NI), NB)]).astype(f)
    inv = np.exp(f(-math.log(10000.0)) * np.arange(32, dtype=f) / f(32)).astype(f)
    ang = (pos[None] * inv[p % 32][:, None]).astype(f)
    put("cos", np.cos(ang).astype(f))
    put("sin", np.sin(ang).astype(f))
    seg = np.ones((4, T), f)
    seg[:, 0] = 0
    seg[:, NP::NI] = 0
    put("seg", seg)
    put("segneg", (seg - 1) * f(BIG))
    put("rank_g", np.tile(8 - np.arange(4, dtype=f), (128, 1)))
    put("rank_e", np.tile(16 - np.arange(8, dtype=f), (128, 1)))
    put("map_pair", (p[:, None] // 64).astype(f))
    put("map_heads", (p[:, None] // 8 % 2).astype(f))
    return c


VEC = dict(mix=0, mem=16, ffn=32, final=48, head=56, subln=60, conv=61)
NVEC = 73

STREAM = [("memk0", 4), ("memv0", 4), ("memk1", 4), ("memv1", 4), ("in_a", 8), ("in_b", 6), ("out_a", 4),
          ("memq0", 4), ("memo0", 4), ("moe0", 96), ("qkv", 12), ("out_c", 4), ("memq1", 4), ("memo1", 4),
          ("moe1", 96)]
UNIT = {}
_at = 0
for _n, _w in STREAM:
    UNIT[_n] = (_at, _w)
    _at += _w
NUNITS = _at


def slot_constants():
    c = np.zeros((128, NSLOT + 128), np.float32)
    c[:, :NSLOT] = np.arange(NSLOT)
    c[:, NSLOT:] = np.arange(128)[:, None] < np.arange(128)[None]
    return c


def build(nc, a, o):
    import concourse.bass as bass
    from concourse import mybir
    from contextlib import ExitStack

    F32, F16, BF16, I32 = mybir.dt.float32, mybir.dt.float16, mybir.dt.bfloat16, mybir.dt.int32
    ALU, ACT, AX = mybir.AluOpType, mybir.ActivationFunctionType, mybir.AxisListType
    ds = bass.ds
    ctx = ExitStack()
    ctx.enter_context(nc.allow_non_contiguous_dma("small vectors and strided outputs"))

    def sb(name, shape, dt=F32):
        return ctx.enter_context(nc.sbuf_tensor(name, shape, dt))

    def sem(name):
        return ctx.enter_context(nc.semaphore(name))

    cst = sb("cst", [128, NCONST])
    maskb = sb("maskb", [128, 768], BF16)
    identb = sb("identb", [128, 128], BF16)
    ones = sb("ones", [128, 128])
    epsc = sb("epsc", [128, 2])
    vecs = sb("vecs", [NVEC, 128])
    vec = sb("vec", [128, NVEC])
    xT = sb("xT", [128, KD, T])
    xn = sb("xn", [128, KD, T])
    xh = sb("xh", [128, KD, T], F16)
    xl = sb("xl", [128, KD, T], F16)
    stg = sb("stg", [128, 2, 2048])
    wh = sb("wh", [128, 2, 2048], F16)
    wl = sb("wl", [128, 2, 2048], F16)
    memkT = sb("memkT", [128, 2, KD, 256])
    memv = sb("memv", [128, 2, 2, 1024])
    rstd = sb("rstd", [128, 2, T])
    brt = sb("brt", [128, 2, 36])
    lamv = sb("lamv", [128, 256])
    lams = sb("lams", [128, 8])
    gbias = sb("gbias", [36, 1])
    wgate = sb("wgate", [128, KD, 36])
    wrt = sb("wrt", [128, 2, KD, 36])
    roff = sb("roff", [1, NE + 1], I32)
    ptab = sb("ptab", [1, 16], I32)
    NAR = (nc.sbuf_bytes_remaining - 2048) // 4 if isinstance(nc.sbuf_bytes_remaining, int) else 22000
    arena = sb("arena", [128, NAR])
    ps = ctx.enter_context(nc.psum_tensor("ps", [128, 8, 512], F32))

    def const(name, rows=128):
        at, w = CONST[name]
        return cst[0:rows, at:at + w]

    ident = const("ident")
    m0 = CONST["m_tri"][0]

    def mask(name, rows=128):
        at, w = CONST[name]
        return maskb[0:rows, at - m0:at - m0 + w]

    def area(start):
        pos = [start]

        def take(*shape, dt=F32):
            n = int(np.prod(shape))
            words = n if dt == F32 else (n + 1) // 2
            v = arena[:, pos[0]:pos[0] + words]
            pos[0] += words
            assert pos[0] <= NAR, (pos[0], NAR)
            if dt != F32:
                v = v.bitcast(dt)
            if len(shape) == 1:
                return v
            names = " ".join("abcd"[:len(shape)])
            return v.rearrange(f"p ({names}) -> p {names}", **{"abcd"[i]: shape[i] for i in range(1, len(shape))})
        return take

    take = area(0)
    x_nat = take(3, 1024)
    mem_nat = take(2, 1024)
    mvT = take(KD, 256)
    mk_out = take(2, 1024)
    take = area(0)
    z = take(28, T)
    zq, zk, zv, zo = z[:, 0:4], z[:, 4:8], z[:, 8:12], z[:, 12:16]
    zgb, zgc, zhb = z[:, 16:20], z[:, 20:24], z[:, 24:28]
    ktok = take(3, 512)
    vtok = take(3, 512)
    dmat = take(4, 448)
    smat = take(448)
    ei = take(4, 384)
    c0 = take(2, 8, 128)
    c0T = take(8, 128)
    vw = take(8, 128)
    vwp = take(2, 128)
    cp_out = take(4, 128)
    u_p = take(4, NP + 2)
    u_s = take(4, NB, NI + 2)
    qi = take(NS)
    qn = take(NS)
    den = take(2, T)
    n0 = take(128)
    n0T = take(32)
    nT = take(36)
    nout = take(128)
    acol = take(12)
    cvt = take(4, 2)
    cvs = take(4, 16)
    m0row = take(8)
    rowsp = z[:, 20:28].rearrange("p a b -> p (a b)")
    r_out = rowsp[0:4, 0:1024]
    cout = rowsp[:, 1024:1536]
    mrow = rowsp[:, 1536:1536 + T]
    cnat = dmat.rearrange("p a b -> p (a b)")[:, 0:512]
    hsq, hstd = z[:, 0:4], z[:, 4:8]
    grow = c0T.rearrange("p a b -> p (a b)")
    g_ig = vw.rearrange("p a b -> p (a b)")[0:4, 0:T]
    g_f = grow[:, 0:T]
    g_t = grow[:, T:2 * T]
    g_lf = vw.rearrange("p a b -> p (a b)")[0:4, T:2 * T]
    g_b = vw.rearrange("p a b -> p (a b)")[0:4, 2 * T:3 * T]
    take = area(0)
    zc = take(24, T)
    vtok3 = take(3, 1024)
    kpg = take(2, 2, 1024)
    vpg = take(2, 2, 1024)
    kTb = take(KD, 256)
    qpadf = take(1152)
    qpad = qpadf[:, 0:1024].rearrange("p (a b) -> p a b", a=8)
    aTp = take(2, 512)
    aTf = aTp.rearrange("p a b -> p (a b)")
    pb, fr, aTb = aTf[:, 0:T], aTf[:, T:T + 64], aTf[:, 384:576].rearrange("p (a b) -> p a b", a=3)
    sst = take(4, 8)
    ktok3 = kpg.rearrange("p a b c -> p (a b c)")[:, 0:3072].rearrange("p (t c) -> p t c", t=3)
    pp = zc[:, 16:24].rearrange("p a b -> p (a b)")[:, 0:2048].rearrange("p (a b) -> p a b", a=8)
    frp = zc[:, 16:24].rearrange("p a b -> p (a b)")[:, 2048:2560]
    take = area(0)
    gbc = take(NE, T)
    take = area(0)
    xgh = take(KD, NSLOT, dt=F16)
    xgl = take(KD, NSLOT, dt=F16)
    yc = take(KD, NSLOT)
    after = area(0)
    ysh = after(5, 1024, dt=F16)
    ysl = after(5, 1024, dt=F16)
    before_yc = area(KD * NSLOT)
    xth = before_yc(3, 1024, dt=F16)
    xtl = before_yc(3, 1024, dt=F16)
    pw = before_yc(3, NSLOT)
    pk = take(3, NSLOT, dt=F16)
    gk = take(5, T, dt=F16)
    gslot = take(NSLOT)
    rc = take(NSLOT + 128)
    iota, before = rc[:, 0:NSLOT], rc[:, NSLOT:NSLOT + 128]
    amat = take(3, NE)
    cnt = take(NE)
    off = take(NE)
    cmax = take(1)
    e_t = take(2, T)
    r_t = take(2, T)
    a_t = take(2, T)
    b_t = take(2, T)
    cg = take(2, 2, T)
    hh = take(4, T, dt=F16)
    hl = take(4, T, dt=F16)
    gT = take(T)
    lg = take(3, 36)
    rt = take(24, 3, 8)
    gate = take(3, NE)
    take = area(NAR - 2560)
    sq = take(KD, T)

    names = """const_in tab_in vec_in small_in x_in mem_in gate_in cst_ready vec_ps vec_ev tr_ps tr_ev w_hi w_lo
        w_used w_ev in_hi in_lo sq_ready sum_ready std_ready xn_ready gate_ps gneg_ready gln_ready rows_ready
        kscaled bc_ps d_ready ei_ready s_ps s_ready ct_ps ct_ev q_ready vw_ready num_ps h_ready cn_ps c_ready
        n_ready hsq_ready hsum_ready hstd_ready osig_ready y_ready u_ready dve_chain act_chain pool_chain
        pool_loop dve_loop act_loop rot_ps rot_cos rot_done lam_arg lam_exp psc_ps pmax_ready pexp_ready
        pfr_ready pat_ps pat_ev ppv_ps ppv_ev kt_ps kt_ev qp_tile qp_ready bsc_ps bmax_ready bexp_ready
        bfr_ready bat_ps bat_ev bpv_ps bpv_ev osq_ready osum_ready ostd_ready on_ready lg_ps gexp_ready
        gsel_ready rexp_ready gate_ready rank_ps off_ready rc_in moe_done out_mem out_p out_c out_y ml_ps
        ml_ev""".split()
    S = {n: sem(n) for n in names}
    ML = [{n: sem(f"moe{l}_{n}") for n in """exp c hh hl chain loop xt_ps xt_hi xt_ev p_ready
           gs_ps gs_ready g_ps g_ev xg_ps xg_hi xg_lo b y ys_ps ys_hi ys_lo z_ps""".split()} for l in range(2)]
    w_load = [sem(f"w_load{n}") for n in range(4)]
    slot_in = [sem("slot_in0"), sem("slot_in1")]
    c_out = [sem("c_out0"), sem("c_out1")]

    class Chain:

        def __init__(self, eng, name, loop):
            self.eng, self.sem, self.n = eng, name, 0
            self.lsem, self.base, self.per, self.i, self.k = loop, 0, 0, None, 0

        def __call__(self, ins):
            if self.i is None:
                self.n += 1
                ins.then_inc(self.sem, 1)
                self.eng.wait_ge(self.sem, self.n)
            else:
                self.k += 1
                ins.then_inc(self.lsem, 1)
                self.eng.wait_ge(self.lsem, self.i * self.per + (self.base + self.k))

        def enter(self, i, per):
            self.i, self.per, self.k = i, per, 0

        def leave(self, rounds):
            assert self.k == self.per, (self.k, self.per)
            self.base += rounds * self.per
            self.i = None

    block = ctx.enter_context(nc.Block())

    def cols(w, j0, n=256):
        return w.rearrange("(k p) n -> p k n", p=128)[:, :, ds(j0, n)]

    a_cols = a["w_in_a"][0]
    MATRIX = {"memk0": lambda j: cols(a["w_mem_k"][0], j * 256), "memv0": lambda j: cols(a["w_mem_v"][0], j * 256),
              "memk1": lambda j: cols(a["w_mem_k"][1], j * 256), "memv1": lambda j: cols(a["w_mem_v"][1], j * 256),
              "in_a": lambda j: cols(a_cols, j * 256), "in_b": lambda j: cols(a_cols, j * 256 + 2056),
              "out_a": lambda j: cols(a["w_out_a"][0], j * 256),
              "memq0": lambda j: cols(a["w_mem_q"][0], j * 256), "memo0": lambda j: cols(a["w_mem_o"][0], j * 256),
              "qkv": lambda j: cols(a["w_qkv_c"][0], j * 256), "out_c": lambda j: cols(a["w_out_c"][0], j * 256),
              "memq1": lambda j: cols(a["w_mem_q"][1], j * 256), "memo1": lambda j: cols(a["w_mem_o"][1], j * 256)}
    w_gate_f = a["w_exp_gate"].rearrange("l g e (k p) f -> (l g e) p k f", p=128)
    w_up_f = a["w_exp_up"].rearrange("l g e (k p) f -> (l g e) p k f", p=128)
    w_down_f = a["w_exp_down"].rearrange("l g e (k p) d -> (l g e k) p d", p=128)

    def stage8(s):
        return stg[:, s].rearrange("p (k n) -> p k n", k=KD)

    @block.sync
    def _(sp):
        def load(u, s, dst, src, first=False):
            kk = dst.shape[1] // 2
            for h in range(2):
                if not first:
                    sp.wait_ge(S["w_lo"], u * 2 + (h - 3))
                sp.dma_start(dst[:, kk * h:kk * h + kk], src[:, kk * h:kk * h + kk]).then_inc(w_load[2 * s + h], 16)

        def load_expert(u, e):
            load(u, 0, stage8(0), w_gate_f[e, :, :, :] if isinstance(e, int) else
                 w_gate_f[ds(e, 1), :, :, :].rearrange("a p k f -> p (a k) f"))
            load(u + 1, 1, stage8(1), w_up_f[e, :, :, :] if isinstance(e, int) else
                 w_up_f[ds(e, 1), :, :, :].rearrange("a p k f -> p (a k) f"))

        def load_down(u, row):
            for s in range(2):
                load(u + s, s, stg[:, s].rearrange("p (k n) -> p k n", k=4),
                     w_down_f[ds(row, 4), :, 512 * s:512 * s + 512].rearrange("k p n -> p k n"))

        for name, n in STREAM:
            u0 = UNIT[name][0]
            if name.startswith("moe"):
                layer = int(name[-1])
                load_expert(u0, NE * layer)
                load_expert(u0 + 2, NE * layer + 1)
                with sp.Fori(1, NE // 2) as i:
                    u = i * 6 + (u0 - 2)
                    load_expert(u, i * 2 + NE * layer)
                    load_down(u + 2, i * 4 + (NE * 2 * layer - 4))
                    load_expert(u + 4, i * 2 + (NE * layer + 1))
                load_down(u0 + n - 2, NE * 2 * layer + 2 * NE - 4)
            else:
                start = 0
                if u0 == 0:
                    for s in range(2):
                        load(s, s, stage8(s), MATRIX[name](s), first=True)
                    start = 1
                with sp.Fori(start, n // 2) as i:
                    for s in range(2):
                        load(i * 2 + (u0 + s), s, stage8(s), MATRIX[name](i * 2 + s))

    def split_hi(act, u, s):
        for h in range(2):
            c = slice(1024 * h, 1024 * h + 1024)
            act.wait_ge(w_load[2 * s + h], (u - s) * 8 + 16)
            nc.scalar.mul(wh[:, s, c], stg[:, s, c], WSCALE).then_inc(S["w_hi"], 1)

    def split_lo(dve, u, s):
        for h in range(2):
            c = slice(1024 * h, 1024 * h + 1024)
            dve.wait_ge(S["w_hi"], u * 2 + (h + 1))
            nc.vector.scalar_tensor_tensor(wl[:, s, c], stg[:, s, c], WSCALE, wh[:, s, c], ALU.mult,
                                           ALU.subtract).then_inc(S["w_lo"], 1)

    def mm3(out, s, kk, c0_, hi, lo, start, stop, width=256):
        at = kk * width + c0_
        nc.tensor.matmul(out, wh[:, s, at:at + 128], hi, start=start, stop=False)
        nc.tensor.matmul(out, wh[:, s, at:at + 128], lo, start=False, stop=False)
        return nc.tensor.matmul(out, wl[:, s, at:at + 128], hi, start=False, stop=stop)

    def gemm_pe(pe, name, g, n=T):
        u0, units = UNIT[name]
        pe.wait_ge(S["in_lo"], g + 1)

        def unit(u, s):
            pe.wait_ge(S["w_lo"], u * 2 + 2)
            pe.wait_ge(S["w_ev"], u - 1)
            for j in range(2):
                for k in range(KD):
                    last = mm3(ps[:, 2 * s + j, 0:n], s, k, 128 * j, xh[:, k, 0:n], xl[:, k, 0:n], k == 0,
                               k == KD - 1)
            last.then_inc(S["w_used"], 1)

        start = 0
        if u0 == 0:
            for s in range(2):
                pe.wait_ge(S["w_lo"], 2 * s + 2)
                for j in range(2):
                    for k in range(KD):
                        last = mm3(ps[:, 2 * s + j, 0:n], s, k, 128 * j, xh[:, k, 0:n], xl[:, k, 0:n], k == 0,
                                   k == KD - 1)
                last.then_inc(S["w_used"], 1)
            start = 1
        with pe.Fori(start, units // 2) as i:
            for s in range(2):
                unit(i * 2 + (u0 + s), s)

    def gemm_copy_act(act, name, dst, n=T):
        u0, units = UNIT[name]
        with act.Fori(0, units // 2) as i:
            for s in range(2):
                act.wait_ge(S["w_used"], i * 2 + (u0 + s + 1))
                nc.scalar.mul(dst[:, ds(i * 4 + 2 * s, 2), :], ps[:, 2 * s:2 * s + 2, 0:n],
                              1 / WSCALE).then_inc(S["w_ev"], 1)
                split_hi(act, i * 2 + (u0 + s + 2), s)

    def gemm_split_act(act, name):
        u0, units = UNIT[name]
        with act.Fori(0, units // 2) as i:
            for s in range(2):
                act.wait_ge(S["w_used"], i * 2 + (u0 + s + 1))
                split_hi(act, i * 2 + (u0 + s + 2), s)

    def gemm_split_dve(dve, name):
        u0, units = UNIT[name]
        with dve.Fori(0, units // 2) as i:
            for s in range(2):
                dve.wait_ge(S["w_used"], i * 2 + (u0 + s + 1))
                split_lo(dve, i * 2 + (u0 + s + 2), s)

    def gemm_add_dve(dve, name):
        u0, units = UNIT[name]
        with dve.Fori(0, units // 2) as i:
            for s in range(2):
                dve.wait_ge(S["w_used"], i * 2 + (u0 + s + 1))
                at = ds(i * 4 + 2 * s, 2)
                nc.vector.scalar_tensor_tensor(xT[:, at, :], ps[:, 2 * s:2 * s + 2, 0:T], 1 / WSCALE, xT[:, at, :],
                                               ALU.mult, ALU.add).then_inc(S["w_ev"], 1)
                split_lo(dve, i * 2 + (u0 + s + 2), s)

    def input_act(act, src, n=T):
        nc.scalar.copy(xh[:, :, 0:n], src).then_inc(S["in_hi"], 1)

    def input_dve(dve, g, src, n=T):
        dve.wait_ge(S["in_hi"], g + 1)
        nc.vector.tensor_sub(xl[:, :, 0:n], src, xh[:, :, 0:n]).then_inc(S["in_lo"], 1)

    def tr_pe(pe, g, srcs, n):
        if g >= 4:
            pe.wait_ge(S["tr_ev"], g - 3)
        for i, src in enumerate(srcs):
            m = src.shape[-1]
            last = nc.tensor.transpose(ps[0:m, 4 + g % 4, 128 * i:128 * i + n], src, ident[0:n, 0:n])
        last.then_inc(S["tr_ps"], 1)

    def tr_dve(dve, g, dst, m, n, cnt=4):
        dve.wait_ge(S["tr_ps"], g + 1)
        src = ps[0:m, 4 + g % 4, :].rearrange("p (a b) -> p a b", a=4)[:, 0:cnt, 0:n]
        nc.vector.tensor_copy(dst, src).then_inc(S["tr_ev"], 1)

    G_X, G_MEM, G_MKV, G_ML, G_DA, G_Y = 0, 6, 10, 26, 32, 44

    NVROW = {0: VEC["mix"], 1: VEC["mem"], 2: VEC["ffn"], 3: VEC["mix"] + 8, 4: VEC["mem"] + 8, 5: VEC["ffn"] + 8,
             6: VEC["final"]}

    def norm_act(act, n):
        nc.scalar.activation(sq[:], xT[:], ACT.Square).then_inc(S["sq_ready"], 1)
        act.wait_ge(S["sum_ready"], n + 1)
        nc.scalar.activation(rstd[:, 0, :], ps[:, 4, 0:T], ACT.Sqrt, bias=epsc[:, 0:1],
                             scale=1.0 / D).then_inc(S["std_ready"], 1)

    def norm_pe(pe, n):
        pe.wait_ge(S["sq_ready"], n + 1)
        for k in range(KD):
            last = nc.tensor.matmul(ps[:, 4, 0:T], ones[:], sq[:, k, :], start=(k == 0), stop=(k == KD - 1))
        last.then_inc(S["sum_ready"], 1)

    def norm_dve(dve, link, n):
        dve.wait_ge(S["std_ready"], n + 1)
        link(nc.vector.reciprocal(rstd[:, 1, :], rstd[:, 0, :]))
        for k in range(KD):
            v = NVROW[n] + k
            last = nc.vector.scalar_tensor_tensor(xn[:, k, :], xT[:, k, :], vec[:, v:v + 1], rstd[:, 1, :], ALU.mult,
                                                  ALU.mult)
        last.then_inc(S["xn_ready"], 1)
        dve.wait_ge(S["xn_ready"], n + 1)

    NPOOL = a["cache_k"].shape[1]
    SMALL = 16 * 3
    NVIN = 16 * (7 + 2 + 8 + 1)
    DGROUPS = ((0, 128, 0, 256), (1, 128, 256, 128), (2, 64, 384, 64))

    def mlstm_pool(pool, link):
        for h in range(2):
            pool.dma_start(c0[:, h], a["state_mlstm_C"][0, :, h].rearrange("b v k -> v b k")).then_inc(slot_in[h], 16)
        pool.dma_start(n0[0:32, :], a["state_mlstm_n"][0].rearrange("b h k -> (b h) k")).then_inc(S["small_in"], 16)
        pool.dma_start(m0row[0:4, :], a["state_mlstm_m"][0].rearrange("b h -> h b")).then_inc(S["small_in"], 16)
        pool.dma_start(cnat[0:16, :], a["state_conv"][0].rearrange("b w d -> (b w) d")).then_inc(S["small_in"], 16)

    def mlstm_pool_out(pool, link):
        pool.wait_ge(S["ml_ev"], 3)
        pool.dma_start(o["p_conv"][0, 0], cout[0:2, :]).then_inc(S["out_c"], 16)
        pool.dma_start(o["s_conv"][0].rearrange("b w d -> (b w) d"), cout[32:48, :]).then_inc(S["out_c"], 16)
        pool.wait_ge(S["rows_ready"], 1)
        pool.dma_start(o["p_m"][0].rearrange("b h -> h b"), mrow[0:4, NP - 1:NP]).then_inc(S["out_c"], 16)
        pool.dma_start(o["s_m"][0].rearrange("b h -> h b"), mrow[0:4, NP + NI - 1::NI]).then_inc(S["out_c"], 16)
        for h in range(HA):
            pool.wait_ge(S["c_ready"], h + 1)
            pool.dma_start(o["s_C"][0, :, h].rearrange("b v k -> v b k"), c0[:, h % 2]).then_inc(c_out[h % 2], 16)
            pool.dma_start(o["p_C"][0, 0, h], cp_out[:, h, :]).then_inc(S["out_c"], 16)
            if h + 2 < HA:
                pool.wait_ge(c_out[h % 2], 16)
                pool.dma_start(c0[:, h % 2], a["state_mlstm_C"][0, :, h + 2].rearrange("b v k -> v b k")
                               ).then_inc(slot_in[h % 2], 16)
        pool.wait_ge(S["n_ready"], 1)
        pool.dma_start(o["s_n"][0].rearrange("b h k -> (b h) k"), nout[0:32, :]).then_inc(S["out_c"], 16)
        pool.dma_start(o["p_n"][0, 0], nout[32:36, :]).then_inc(S["out_c"], 16)

    def mlstm_pe(pe):
        pe.wait_ge(S["gate_in"], 32)
        pe.wait_ge(S["cst_ready"], 1)
        for k in range(KD):
            last = nc.tensor.matmul(ps[0:36, 5, 0:T], wgate[:, k, :], xn[:, k, :], start=(k == 0),
                                    stop=(k == KD - 1))
        last.then_inc(S["gate_ps"], 1)
        gemm_pe(pe, "in_a", 1)
        gemm_pe(pe, "in_b", 1)
        pe.wait_ge(S["small_in"], SMALL)
        for c in range(4):
            nc.tensor.transpose(ps[:, 6, 16 * c:16 * c + 16], cnat[0:16, 128 * c:128 * c + 128], ident[0:16, 0:16])
        nc.tensor.transpose(ps[:, 6, 64:96], n0[0:32, :], ident[0:32, 0:32]).then_inc(S["ml_ps"], 1)
        pe.wait_ge(S["kscaled"], 1)
        pe.wait_ge(S["gneg_ready"], 1)
        pe.wait_ge(S["ml_ev"], 1)
        g = G_ML
        for src in (zk, zv):
            for t0, n in TILES:
                tr_pe(pe, g, [src[:, i, t0:t0 + n] for i in range(4)], 128)
                g += 1
        pe.wait_ge(S["rows_ready"], 1)
        pe.wait_ge(S["tr_ev"], G_ML + 6)
        for i, (t0, n) in enumerate(TILES):
            last = nc.tensor.transpose(ps[0:n, 3, 4 * i:4 * i + 4], r_out[:, 704 + t0:704 + t0 + n], ident[0:4, 0:4])
        last.then_inc(S["ml_ps"], 1)
        pe.wait_ge(S["u_ready"], 2)
        for c in range(4):
            nc.tensor.transpose(ps[0:2, 1, 128 * c:128 * c + 128], cvt[:, c, :], ident)
        for c in range(4):
            last = nc.tensor.transpose(ps[0:16, 2, 128 * c:128 * c + 128], cvs[:, c, :], ident)
        last.then_inc(S["ml_ps"], 1)
        pe.wait_ge(S["ml_ev"], 3)
        pe.wait_ge(S["ml_ev"], 2)
        for h in range(HA):
            if h:
                pe.wait_ge(S["ei_ready"], h)
            sel = ident[0:4, h:h + 1].to_broadcast([4, 128])
            for (tile, n, c, w) in DGROUPS:
                t0 = T - 64 if tile == 2 else 128 * tile
                mname, mw = ("m_samp", 64) if tile == 2 else ("m_tri", 128)
                nc.tensor.matmul(ps[0:n, 4, c:c + w], sel[:, 0:n], r_out[:, t0:t0 + w], start=True, stop=False)
                nc.tensor.matmul(ps[0:n, 4, c:c + mw], identb[0:n, 0:n], mask(mname, n), start=False, stop=True)
            nc.tensor.matmul(ps[:, 5, 0:384], sel, r_out[:, 320:704], start=True, stop=True).then_inc(S["bc_ps"], 1)
            if h:
                pe.wait_ge(S["s_ready"], h)
            for (tile, n, c, w) in DGROUPS:
                t0 = T - 64 if tile == 2 else 128 * tile
                last = nc.tensor.matmul(ps[0:n, 6, c:c + w], zk[:, h, t0:t0 + n], zq[:, h, t0:t0 + w], start=True,
                                        stop=True)
            last.then_inc(S["s_ps"], 1)
            pe.wait_ge(slot_in[h % 2], 16 * (h // 2 + 1))
            if h:
                pe.wait_ge(S["c_ready"], h)
            for b in range(NB):
                last = nc.tensor.transpose(ps[:, 1 + b // 4, 128 * (b % 4):128 * (b % 4) + 128], c0[:, h % 2, b, :],
                                           ident)
            last.then_inc(S["ct_ps"], 1)
            pe.wait_ge(S["s_ready"], h + 1)
            pe.wait_ge(S["ct_ev"], h + 1)
            pe.wait_ge(S["q_ready"], h + 1)
            if h:
                pe.wait_ge(S["h_ready"], h)
            for bank, left in ((7, None), (0, ones)):
                first = True
                for (tile, n, c, w) in DGROUPS:
                    t0 = T - 64 if tile == 2 else 128 * tile
                    lhs = vtok[0:n, tile, 128 * h:128 * h + 128] if left is None else ones[0:n, :]
                    nc.tensor.matmul(ps[:, bank, t0:t0 + w], lhs, smat[0:n, c:c + w], start=first, stop=False,
                                     skip_group_check=True)
                    first = False
                if left is None:
                    for b in range(NB):
                        last = nc.tensor.matmul(ps[:, bank, NP + NI * b:NP + NI * b + NI], c0T[:, b, :],
                                                qi[:, NI * b:NI * b + NI], start=False, stop=(b == NB - 1),
                                                skip_group_check=True)
                else:
                    last = nc.tensor.matmul(ps[:, bank, NP:T], ones[:], qn[:], start=False, stop=True,
                                            skip_group_check=True)
            last.then_inc(S["num_ps"], 1)
            pe.wait_ge(S["vw_ready"], h + 1)
            kt = ktok[:, :, 128 * h:128 * h + 128]
            for b in range(NB):
                nc.tensor.matmul(ps[:, 1 + b // 4, 128 * (b % 4):128 * (b % 4) + 128], vw[0:64, b, :],
                                 kt[0:64, 2, :], start=True, stop=True)
            for i in range(2):
                nc.tensor.matmul(ps[:, 3, 0:128], vwp[:, i, :], kt[:, i, :], start=(i == 0), stop=(i == 1))
            nc.tensor.matmul(ps[:, 3, 128:136], kt[0:64, 2, :], dmat[0:64, h, 384 + NI - 1:448:NI], start=True,
                             stop=True)
            for i in range(2):
                last = nc.tensor.matmul(ps[:, 3, 136:137], kt[:, i, :], dmat[:, h, 255 + 128 * i:256 + 128 * i],
                                        start=(i == 0), stop=(i == 1))
            last.then_inc(S["cn_ps"], 1)
        pe.wait_ge(S["c_ready"], HA)
        nc.tensor.transpose(ps[0:36, 3, 0:128], nT[:], ident).then_inc(S["ml_ps"], 1)
        pe.wait_ge(S["hsq_ready"], 1)
        pe.wait_ge(S["h_ready"], HA)
        pe.wait_ge(S["s_ready"], HA)
        for h in range(HA):
            last = nc.tensor.matmul(ps[:, 4 + h, 0:T], ones[:], hsq[:, h, :], start=True, stop=True)
        last.then_inc(S["hsum_ready"], 1)

    def mlstm_act(act, link):
        act.wait_ge(S["gneg_ready"], 1)
        link(nc.scalar.activation(g_t[32:36, :], g_t[32:36, :], ACT.Exp))
        nc.scalar.activation(g_t[32:36, :], g_t[32:36, :], ACT.Ln, bias=epsc[32:36, 1:2]).then_inc(S["gln_ready"], 1)
        for h in range(HA):
            act.wait_ge(S["bc_ps"], h + 1)
            if h == 0:
                act.wait_ge(S["ml_ev"], 2)
            for (tile, n, c, w) in DGROUPS:
                last = nc.scalar.activation(dmat[0:n, h, c:c + w], ps[0:n, 4, c:c + w], ACT.Exp,
                                            bias=acol[0:n, 4 * tile + h:4 * tile + h + 1])
            last.then_inc(S["d_ready"], 1)
            nc.scalar.activation(ei[:, h, :], ps[:, 5, 0:384], ACT.Exp).then_inc(S["ei_ready"], 1)
            act.wait_ge(S["ct_ps"], h + 1)
            if h:
                act.wait_ge(S["num_ps"], h)
            nc.scalar.copy(c0T.rearrange("p (a b) c -> p a (b c)", a=2), ps[:, 1:3, :]).then_inc(S["ct_ev"], 1)
        act.wait_ge(S["h_ready"], HA)
        nc.scalar.activation(hsq, xn[:, 0:4, :], ACT.Square).then_inc(S["hsq_ready"], 1)
        nc.scalar.activation(zo[:], zo[:], ACT.Exp, scale=-1.0).then_inc(S["osig_ready"], 1)
        act.wait_ge(S["hsum_ready"], 1)
        nc.scalar.activation(hstd, ps[:, 4:8, 0:T], ACT.Sqrt, bias=epsc[:, 0:1],
                             scale=1.0 / 128).then_inc(S["hstd_ready"], 1)

    def mlstm_dve(dve, link):
        dve.wait_ge(S["w_ev"], UNIT["out_a"][0])
        nc.vector.tensor_scalar(zk[:], zk[:], 128 ** -0.5, None, ALU.mult).then_inc(S["kscaled"], 1)
        dve.wait_ge(S["ml_ps"], 1)
        nc.vector.tensor_copy(u_s[:, :, :, 0:2], ps[:, 6, 0:64].rearrange("p (c b w) -> p c b w", c=4, w=2))
        link(nc.vector.tensor_copy(n0T[:], ps[:, 6, 64:96]))
        nc.vector.memset(u_p[:, :, 0:2], 0.0).then_inc(S["ml_ev"], 1)
        dve.wait_ge(S["ml_ev"], 1)
        nc.vector.tensor_tensor(u_p[:, :, 2:], zgc[:, :, 0:NP], zhb[:, :, 0:NP], ALU.mult)
        for c in range(4):
            last = nc.vector.tensor_tensor(u_s[:, c, :, 2:], zgc[:, c, NP:T].rearrange("p (b i) -> p b i", b=NB),
                                           zhb[:, c, NP:T].rearrange("p (b i) -> p b i", b=NB), ALU.mult)
        link(last)
        nc.vector.tensor_copy(cvt[:], u_p[:, :, NP:NP + 2]).then_inc(S["u_ready"], 1)
        nc.vector.tensor_copy(cvs.rearrange("p c (b w) -> p c b w", w=2), u_s[:, :, :, NI:NI + 2]
                              ).then_inc(S["u_ready"], 1)
        for j in range(3):
            for c in range(4):
                v = VEC["conv"] + 4 * j + c
                for (dst, src) in ((xn[:, 4 + c, 0:NP], u_p[:, c, j:j + NP]),
                                   (xn[:, 4 + c, NP:T].rearrange("p (b i) -> p b i", b=NB), u_s[:, c, :, j:j + NI])):
                    if j == 0:
                        last = nc.vector.tensor_scalar(dst, src, vec[:, v:v + 1], None, ALU.mult)
                    else:
                        last = nc.vector.scalar_tensor_tensor(dst, src, vec[:, v:v + 1], dst, ALU.mult, ALU.add)
            link(last)
        link(nc.vector.tensor_tensor(xn[:, 4:8, :], xn[:, 4:8, :], zgb[:], ALU.mult))
        dve.wait_ge(S["gate_ps"], 1)
        nc.vector.tensor_scalar(g_ig, ps[0:4, 5, 0:T], gbias[0:4, :], None, ALU.add)
        link(nc.vector.tensor_scalar(g_f[32:36, :], ps[32:36, 5, 0:T], gbias[32:36, :], None, ALU.add))
        nc.vector.scalar_tensor_tensor(g_t[32:36, :], g_f[32:36, :], -1.0, g_f[32:36, :], ALU.mult, ALU.min
                                       ).then_inc(S["gneg_ready"], 1)
        for i, (t0, n) in enumerate(TILES):
            tr_dve(dve, G_ML + i, ktok[0:n, i, :].rearrange("p (a b) -> p a b", a=4), n, 128)
        for i, (t0, n) in enumerate(TILES):
            tr_dve(dve, G_ML + 3 + i, vtok[0:n, i, :].rearrange("p (a b) -> p a b", a=4), n, 128)
        dve.wait_ge(S["gln_ready"], 1)
        link(nc.vector.scalar_tensor_tensor(g_lf, g_f[32:36, :], 0.0, g_t[32:36, :], ALU.min, ALU.subtract))
        link(nc.vector.tensor_tensor_scan(g_b, const("seg", 4), g_lf, 0.0, ALU.mult, ALU.add))
        ar = r_out[:, 704:1024]
        link(nc.vector.tensor_tensor(ar, g_ig, g_b, ALU.subtract))
        link(nc.vector.tensor_copy(g_lf, ar))
        nc.vector.tensor_scalar(g_lf[:, 0:1], ar[:, 0:1], 0.0, None, ALU.max)
        link(nc.vector.tensor_tensor(g_lf[:, NP::NI], ar[:, NP::NI], m0row[0:4, :], ALU.max))
        link(nc.vector.tensor_tensor_scan(g_ig, const("segneg", 4), g_lf, 0.0, ALU.add, ALU.max))
        link(nc.vector.tensor_tensor(mrow[0:4, :], g_b, g_ig, ALU.add))
        nc.vector.tensor_scalar(r_out[:, 0:320], g_ig, -1.0, None, ALU.mult)
        nc.vector.tensor_scalar(r_out[:, 320:640], mrow[0:4, :], -1.0, None, ALU.mult)
        nc.vector.tensor_tensor(r_out[:, 640:704].rearrange("p (b i) -> p b i", b=NB),
                                m0row[0:4, :].unsqueeze(2).to_broadcast([4, NB, NI]),
                                g_ig[:, NP:T].rearrange("p (b i) -> p b i", b=NB), ALU.subtract
                                ).then_inc(S["rows_ready"], 1)
        dve.wait_ge(S["ml_ps"], 2)
        nc.vector.tensor_copy(acol[:, 0:8], ps[:, 3, 0:8])
        nc.vector.tensor_copy(acol[0:64, 8:12], ps[0:64, 3, 8:12]).then_inc(S["ml_ev"], 1)
        dve.wait_ge(S["ml_ps"], 3)
        link(nc.vector.tensor_copy(cout[0:2, :], ps[0:2, 1, :]))
        nc.vector.tensor_copy(cout[32:48, :], ps[0:16, 2, :]).then_inc(S["ml_ev"], 1)
        dve.wait_ge(S["ml_ev"], 3)
        for h in range(HA):
            dve.wait_ge(S["s_ps"], h + 1)
            dve.wait_ge(S["d_ready"], h + 1)
            if h:
                dve.wait_ge(S["num_ps"], h)
            for (tile, n, c, w) in DGROUPS:
                last = nc.vector.tensor_tensor(smat[0:n, c:c + w], ps[0:n, 6, c:c + w], dmat[0:n, h, c:c + w],
                                               ALU.mult)
            last.then_inc(S["s_ready"], 1)
            dve.wait_ge(S["ei_ready"], h + 1)
            link(nc.vector.tensor_tensor(qi[:], zq[:, h, NP:T], ei[:, h, 320:384], ALU.mult))
            nc.vector.tensor_tensor(qn.rearrange("p (b i) -> p b i", b=NB), qi.rearrange("p (b i) -> p b i", b=NB),
                                    n0T[:, h::HA].unsqueeze(2).to_broadcast([128, NB, NI]), ALU.mult
                                    ).then_inc(S["q_ready"], 1)
            if h:
                dve.wait_ge(S["cn_ps"], h)
            hs = slice(128 * h, 128 * h + 128)
            nc.vector.tensor_tensor(vw[0:64], vtok[0:64, 2, hs].unsqueeze(1).to_broadcast([64, NB, 128]),
                                    dmat[0:64, h, 384 + NI - 1:448:NI].unsqueeze(2).to_broadcast([64, NB, 128]),
                                    ALU.mult)
            for i in range(2):
                last = nc.vector.tensor_scalar(vwp[:, i, :], vtok[:, i, hs], dmat[:, h, 255 + 128 * i:256 + 128 * i],
                                               None, ALU.mult)
            last.then_inc(S["vw_ready"], 1)
            dve.wait_ge(S["num_ps"], h + 1)
            link(nc.vector.scalar_tensor_tensor(den[:, 0, :], ps[:, 0, 0:T], -1.0, ei[:, h, 0:T], ALU.mult, ALU.max))
            link(nc.vector.tensor_tensor(den[:, 0, :], ps[:, 0, 0:T], den[:, 0, :], ALU.max))
            link(nc.vector.reciprocal(den[:, 1, :], den[:, 0, :]))
            nc.vector.tensor_tensor(xn[:, h, :], ps[:, 7, 0:T], den[:, 1, :], ALU.mult).then_inc(S["h_ready"], 1)
            dve.wait_ge(S["cn_ps"], h + 1)
            dec = ei[:, h, 320 + NI - 1:384:NI]
            link(nc.vector.tensor_tensor(c0[:, h % 2], c0[:, h % 2], dec.unsqueeze(2).to_broadcast([128, NB, 128]),
                                         ALU.mult))
            nc.vector.tensor_tensor(c0[:, h % 2].rearrange("p (a b) c -> p a (b c)", a=2), ps[:, 1:3, :],
                                    c0[:, h % 2].rearrange("p (a b) c -> p a (b c)", a=2), ALU.add)
            nc.vector.tensor_copy(cp_out[:, h, :], ps[:, 3, 0:128])
            nc.vector.tensor_copy(nT[:, 32 + h:33 + h], ps[:, 3, 136:137])
            link(nc.vector.tensor_tensor(nT[:, h:32:HA], n0T[:, h::HA], dec, ALU.mult))
            nc.vector.tensor_tensor(nT[:, h:32:HA], nT[:, h:32:HA], ps[:, 3, 128:136], ALU.add
                                    ).then_inc(S["c_ready"], 1)
        dve.wait_ge(S["ml_ps"], 4)
        nc.vector.tensor_copy(nout[0:36, :], ps[0:36, 3, 0:128]).then_inc(S["n_ready"], 1)
        dve.wait_ge(S["osig_ready"], 1)
        link(nc.vector.tensor_scalar(zo[:], zo[:], 1.0, None, ALU.add))
        link(nc.vector.reciprocal(zo[:], zo[:]))
        dve.wait_ge(S["hstd_ready"], 1)
        link(nc.vector.reciprocal(hsq, hstd))
        link(nc.vector.tensor_tensor(xn[:, 0:4, :], xn[:, 0:4, :], hsq, ALU.mult))
        for h in range(HA):
            v = VEC["head"] + h
            last = nc.vector.scalar_tensor_tensor(xn[:, h, :], xn[:, h, :], vec[:, v:v + 1], zo[:, h, :], ALU.mult,
                                                  ALU.mult)
        last.then_inc(S["y_ready"], 1)
        dve.wait_ge(S["y_ready"], 1)


    ATT = {"m0": dict(tile0=0, batch0=0, kv0=32, dma=32, layer=0), "d": dict(tile0=2, batch0=8, kv0=160, dma=64, layer=1),
           "m1": dict(tile0=6, batch0=16, kv0=416, dma=32, layer=1)}
    for _k, _c in ATT.items():
        diff = _k == "d"
        _c.update(diff=diff, nt=4 if diff else 2, nq=64 if diff else 128, nh=8 if diff else 4,
                  rows=128 if diff else 32, width=T if diff else 256, c=64 if diff else 32,
                  scale=64 ** -0.5 if diff else 256 ** -0.5)
    psf = ps.rearrange("p b k -> p (b k)")
    qdiag = qpadf[:, 0:1152].rearrange("p (h x) -> p h x", x=144)
    qmem = qpadf[:, 0:288].rearrange("p (h x) -> p h x", x=72)[:, :, 0:64].rearrange("p h (c y) -> p h c y", y=32)

    def head_of(c, blk):
        return blk if c["diff"] else blk // 2

    def prompt_pe(pe, kind):
        c = ATT[kind]
        nh, nq = c["nh"], c["nq"]
        for t in range(c["nt"]):
            n = c["tile0"] + t
            nk = 64 * (t + 1) if c["diff"] else 256
            if c["diff"]:
                pe.wait_ge(S["qp_tile"], t + 1)
            if n:
                pe.wait_ge(S["pexp_ready"], n)
            for h in range(nh):
                out = psf[:, 2048 + 256 * h:2048 + 256 * h + nk]
                if c["diff"]:
                    nc.tensor.matmul(out, qpad[:, h, :], zc[:, 8 + h, 0:nk], start=True, stop=False,
                                     skip_group_check=True)
                    last = nc.tensor.matmul(out[:, 64 * t:nk], identb[:], mask("m_pair"), start=False, stop=True,
                                            skip_group_check=True)
                else:
                    for dc in range(2):
                        last = nc.tensor.matmul(out, zc[:, 2 * h + dc, 128 * t:128 * t + 128],
                                                memkT[:, c["layer"], 2 * h + dc, :], start=(dc == 0), stop=(dc == 1))
            last.then_inc(S["psc_ps"], 1)
            pe.wait_ge(S["pfr_ready"], n + 1)
            kts = [(kt, min(128, nk - 128 * kt)) for kt in range((nk + 127) // 128)]
            for kt, m in kts:
                for h in range(nh):
                    last = nc.tensor.matmul(ps[0:m, kt, nq * h:nq * h + nq], pp[:, h, 128 * kt:128 * kt + m],
                                            frp[:, nq * h:nq * h + nq], start=True, stop=True)
            last.then_inc(S["pat_ps"], 1)
            pe.wait_ge(S["pat_ev"], n + 1)
            if n:
                pe.wait_ge(S["ppv_ev"], n)
            for blk in range(8):
                h = head_of(c, blk)
                at = 1024 + nq * blk
                for kt, m in kts:
                    v = vtok3[0:m, kt, 128 * blk:128 * blk + 128] if c["diff"] else \
                        memv[0:m, c["layer"], kt, 128 * blk:128 * blk + 128]
                    last = nc.tensor.matmul(psf[:, at:at + nq], v, aTp[0:m, kt, nq * h:nq * h + nq], start=(kt == 0),
                                            stop=(kt == kts[-1][0]))
            last.then_inc(S["ppv_ps"], 1)

    def prompt_act(act, kind):
        c = ATT[kind]
        for t in range(c["nt"]):
            n = c["tile0"] + t
            nk = 64 * (t + 1) if c["diff"] else 256
            act.wait_ge(S["pmax_ready"], n + 1)
            if n:
                act.wait_ge(S["pat_ps"], n)
            for h in range(c["nh"]):
                last = nc.scalar.activation(pp[:, h, 0:nk], psf[:, 2048 + 256 * h:2048 + 256 * h + nk], ACT.Exp,
                                            bias=sst[:, 0, h:h + 1], scale=c["scale"], accum_out=sst[:, 1, h:h + 1])
            last.then_inc(S["pexp_ready"], 1)
            act.wait_ge(S["pat_ps"], n + 1)
            if n:
                act.wait_ge(S["ppv_ps"], n)
            for kt in range((nk + 127) // 128):
                m = min(128, nk - 128 * kt)
                last = nc.scalar.copy(aTp[0:m, kt, :], ps[0:m, kt, :])
            last.then_inc(S["pat_ev"], 1)

    def prompt_dve(dve, link, kind):
        c = ATT[kind]
        nh, nq = c["nh"], c["nq"]
        if c["diff"]:
            link(nc.vector.memset(qpadf[:], 0.0))
        for t in range(c["nt"]):
            n = c["tile0"] + t
            nk = 64 * (t + 1) if c["diff"] else 256
            if c["diff"]:
                if t:
                    dve.wait_ge(S["psc_ps"], n)
                for m in range(2):
                    r = slice(64 * m, 64 * m + 64)
                    last = nc.vector.tensor_copy(qpad[r, :, 64 * m:64 * m + 64], zc[r, 0:8, 64 * t:64 * t + 64])
                last.then_inc(S["qp_tile"], 1)
            dve.wait_ge(S["psc_ps"], n + 1)
            sc = psf[:, 2048:2048 + 256 * nh].rearrange("p (h k) -> p h k", h=nh)[:, :, 0:nk]
            link(nc.vector.reduce_max(sst[:, 2, 0:nh], sc, AX.X))
            nc.vector.tensor_scalar(sst[:, 0, 0:nh], sst[:, 2, 0:nh], -c["scale"], None, ALU.mult
                                    ).then_inc(S["pmax_ready"], 1)
            dve.wait_ge(S["pexp_ready"], n + 1)
            link(nc.vector.reciprocal(sst[:, 3, 0:nh], sst[:, 1, 0:nh]))
            if c["diff"]:
                link(nc.vector.tensor_scalar(sst[:, 3, 0:nh], sst[:, 3, 0:nh], lams[:, 5:6], None, ALU.mult))
            fold = const("fold_pair") if c["diff"] else ident
            nc.vector.tensor_tensor(frp.rearrange("p (h q) -> p h q", h=nh),
                                    fold.unsqueeze(1).to_broadcast([128, nh, nq]),
                                    sst[:, 3, 0:nh].unsqueeze(2).to_broadcast([128, nh, nq]), ALU.mult
                                    ).then_inc(S["pfr_ready"], 1)
            dve.wait_ge(S["ppv_ps"], n + 1)
            nc.vector.tensor_copy(xn[:, :, nq * t:nq * t + nq],
                                  psf[:, 1024:1024 + 8 * nq].rearrange("p (b q) -> p b q", b=8)
                                  ).then_inc(S["ppv_ev"], 1)

    def batch_pool(pool, link, kind):
        c = ATT[kind]

        def load(b, s):
            if c["diff"]:
                for p in range(2):
                    page = pool.value_load(ptab[0:1, ds(b * 2 + p, 1)] if not isinstance(b, int) else
                                           ptab[0:1, 2 * b + p:2 * b + p + 1], min_val=0, max_val=NPOOL - 1)
                    for cache, dst in ((a["cache_k"], kpg), (a["cache_v"], vpg)):
                        v = cache[0].rearrange("g t h m d -> g t (h m d)") if len(cache.shape) == 6 else \
                            cache[0].rearrange("g t h d -> g t (h d)")
                        pool.dma_start(dst[:, s, p, :], v[ds(page, 1), :, :].rearrange("g t d -> (g t) d")
                                       ).then_inc(slot_in[s], 16)
            else:
                for cache, dst in ((a["cache_mem_k"], kpg), (a["cache_mem_v"], vpg)):
                    v = cache[c["layer"]].rearrange("b (t p) h d -> b p t (h d)", p=128)
                    src = v[b] if isinstance(b, int) else v[ds(b, 1)].rearrange("g p t d -> (g p) t d")
                    pool.dma_start(dst[:, s], src).then_inc(slot_in[s], 16)

        for s in range(2):
            load(s, s)
        with pool.Fori(1, NB // 2) as i:
            for s in range(2):
                pool.wait_ge(S["bpv_ps"], i * 2 + (c["batch0"] + s - 1))
                load(i * 2 + s, s)

    def batch_pe(pe, kind):
        c = ATT[kind]
        R, C, b0 = c["rows"], c["c"], c["batch0"]

        def step(i, s, first):
            n = i * 2 + (b0 + s)
            b = i * 2 + s
            pe.wait_ge(slot_in[s], i * c["dma"] + (c["kv0"] + c["dma"]))
            if not first:
                pe.wait_ge(S["kt_ev"], n * 4)
            for p in range(2):
                for half in range(2):
                    for j in range(4):
                        at = 512 * half + 128 * j
                        last = nc.tensor.transpose(ps[:, 4 + 2 * p + half, 128 * j:128 * j + 128],
                                                   kpg[:, s, p, at:at + 128], ident)
                    last.then_inc(S["kt_ps"], 1)
            pe.wait_ge(S["qp_ready"], n + 1)
            pe.wait_ge(S["kt_ev"], n * 4 + 4)
            if not first:
                pe.wait_ge(S["bexp_ready"], n)
            for blk in range(8):
                last = nc.tensor.matmul(ps[0:R, 0, 0:256], qpadf[:, R * blk:R * blk + R], kTb[:, blk, :],
                                        start=(blk == 0), stop=(blk == 7), skip_group_check=True)
            if c["diff"]:
                nc.tensor.matmul(ps[:, 0, 256:T], identb[:], mask("m_new")[:, ds(b * 64, 64)] if
                                 not isinstance(b, int) else mask("m_new")[:, 64 * b:64 * b + 64], start=True,
                                 stop=False, skip_group_check=True)
                for blk in range(8):
                    last = nc.tensor.matmul(ps[:, 0, 256:T], qpadf[:, R * blk:R * blk + R], zc[:, 8 + blk, NP:T],
                                            start=False, stop=(blk == 7), skip_group_check=True)
            last.then_inc(S["bsc_ps"], 1)
            pe.wait_ge(S["bfr_ready"], n + 1)
            for kt in range(2):
                last = nc.tensor.matmul(ps[:, 1, 64 * kt:64 * kt + C], pb[0:R, 128 * kt:128 * kt + 128],
                                        fr[0:R, 0:C], start=True, stop=True)
            if c["diff"]:
                last = nc.tensor.matmul(ps[0:64, 1, 128:192], pb[:, 256:T], fr, start=True, stop=True)
            last.then_inc(S["bat_ps"], 1)
            pe.wait_ge(S["bat_ev"], n + 1)
            if not first:
                pe.wait_ge(S["bpv_ev"], n)
            for blk in range(8):
                q = 8 * head_of(c, blk)
                for kt in range(2):
                    last = nc.tensor.matmul(ps[:, 2, 8 * blk:8 * blk + 8], vpg[:, s, kt, 128 * blk:128 * blk + 128],
                                            aTb[:, kt, q:q + 8], start=(kt == 0), stop=(kt == 1 and not c["diff"]),
                                            skip_group_check=True)
                if c["diff"]:
                    last = nc.tensor.matmul(ps[:, 2, 8 * blk:8 * blk + 8], vtok3[0:64, 2, 128 * blk:128 * blk + 128],
                                            aTb[0:64, 2, q:q + 8], start=False, stop=True, skip_group_check=True)
            last.then_inc(S["bpv_ps"], 1)

        if kind == "m0":
            step(0, 0, True)
            step(0, 1, False)
            start = 1
        else:
            start = 0
        with pe.Fori(start, NB // 2) as i:
            for s in range(2):
                step(i, s, False)

    def batch_act(act, kind):
        c = ATT[kind]
        R, C, b0, W = c["rows"], c["c"], c["batch0"], c["width"]
        with act.Fori(0, NB // 2) as i:
            for s in range(2):
                n = i * 2 + (b0 + s)
                act.wait_ge(S["bmax_ready"], n + 1)
                nc.scalar.activation(pb[0:R, 0:W], ps[0:R, 0, 0:W], ACT.Exp, bias=sst[0:R, 0, 0:1],
                                     scale=c["scale"], accum_out=sst[0:R, 1, 0:1]).then_inc(S["bexp_ready"], 1)
                act.wait_ge(S["bat_ps"], n + 1)
                if c["diff"]:
                    nc.scalar.copy(aTb[0:64, 2, :], ps[0:64, 1, 128:192])
                nc.scalar.copy(aTb[:, 0:2, 0:C], ps[:, 1, 0:128].rearrange("p (t c) -> p t c", t=2)[:, :, 0:C]
                               ).then_inc(S["bat_ev"], 1)

    def batch_dve(dve, link, kind):
        c = ATT[kind]
        R, C, b0, W = c["rows"], c["c"], c["batch0"], c["width"]
        dve.wait_ge(S["ppv_ps"], c["tile0"] + c["nt"])
        link(nc.vector.memset(qpadf[:], 0.0))
        rounds = NB // 2
        with dve.Fori(0, rounds) as i:
            link.enter(i, 6 if c["diff"] else 4)
            for s in range(2):
                n = i * 2 + (b0 + s)
                at = ds(i * 16 + (NP + 8 * s), 8)
                if not (kind == "m0" and s == 0):
                    dve.wait_ge(S["bsc_ps"], n)
                if c["diff"]:
                    for m in range(2):
                        r = slice(64 * m, 64 * m + 64)
                        last = nc.vector.tensor_copy(qdiag[r, :, 8 * m:8 * m + 8], zc[r, 0:8, at])
                else:
                    last = nc.vector.tensor_copy(qmem[:, :, :, 0:8],
                                                 zc[:, 0:8, at].rearrange("p (h c) t -> p h c t", h=4))
                last.then_inc(S["qp_ready"], 1)
                for p in range(2):
                    for half in range(2):
                        dve.wait_ge(S["kt_ps"], n * 4 + (2 * p + half + 1))
                        nc.vector.tensor_copy(kTb[:, 4 * half:4 * half + 4, 128 * p:128 * p + 128],
                                              ps[:, 4 + 2 * p + half, :].rearrange("p (a b) -> p a b", a=4)
                                              ).then_inc(S["kt_ev"], 1)
                dve.wait_ge(S["bsc_ps"], n + 1)
                link(nc.vector.reduce_max(sst[0:R, 2, 0:1], ps[0:R, 0, 0:W], AX.X))
                nc.vector.tensor_scalar(sst[0:R, 0, 0:1], sst[0:R, 2, 0:1], -c["scale"], None, ALU.mult
                                        ).then_inc(S["bmax_ready"], 1)
                dve.wait_ge(S["bexp_ready"], n + 1)
                link(nc.vector.reciprocal(sst[0:R, 3, 0:1], sst[0:R, 1, 0:1]))
                if c["diff"]:
                    link(nc.vector.tensor_tensor(sst[:, 3, 0:1], sst[:, 3, 0:1], lams[:, 6:7], ALU.mult))
                fold = const("fold_heads") if c["diff"] else ident[0:32, 0:32]
                nc.vector.tensor_scalar(fr[0:R, 0:C], fold, sst[0:R, 3, 0:1], None, ALU.mult
                                        ).then_inc(S["bfr_ready"], 1)
                dve.wait_ge(S["bpv_ps"], n + 1)
                nc.vector.tensor_copy(xn[:, :, at], ps[:, 2, 0:64].rearrange("p (b q) -> p b q", b=8)
                                      ).then_inc(S["bpv_ev"], 1)
        link.leave(rounds)

    def rope_pe(pe):
        pe.wait_ge(S["w_ev"], UNIT["out_c"][0])
        for blk in range(16):
            if blk >= 4:
                pe.wait_ge(S["rot_done"], blk - 3)
            nc.tensor.matmul(ps[:, blk % 4, 0:T], const("rot"), zc[:, blk, :], start=True, stop=True
                             ).then_inc(S["rot_ps"], 1)
        g = G_DA
        for src in (8, 16):
            for t0, n in TILES:
                for half in range(2):
                    if src == 8:
                        pe.wait_ge(S["rot_done"], 16)
                    tr_pe(pe, g, [zc[:, src + 4 * half + j, t0:t0 + n] for j in range(4)], 128)
                    g += 1

    def rope_pool(pool, link):
        for blk in range(16):
            pool.wait_ge(S["rot_ps"], blk + 1)
            nc.gpsimd.tensor_tensor(zc[:, blk, :], zc[:, blk, :], const("cos"), ALU.mult
                                    ).then_inc(S["rot_cos"], 1)

    def rope_dve(dve, link):
        for blk in range(16):
            dve.wait_ge(S["rot_ps"], blk + 1)
            link(nc.vector.tensor_tensor(rstd[:, blk % 2, :], ps[:, blk % 4, 0:T], const("sin"), ALU.mult))
            dve.wait_ge(S["rot_cos"], blk + 1)
            nc.vector.tensor_tensor(zc[:, blk, :], zc[:, blk, :], rstd[:, blk % 2, :], ALU.add
                                    ).then_inc(S["rot_done"], 1)
        lv = lamv.rearrange("p (a d) -> p a d", a=4)
        dve.wait_ge(S["rot_done"], 16)
        link(nc.vector.tensor_tensor(rstd[:, 0, 0:128].rearrange("p (a d) -> p a d", a=2), lv[:, 0::2, :],
                                     lv[:, 1::2, :], ALU.mult))
        nc.vector.reduce_sum(lams[:, 0:2], rstd[:, 0, 0:128].rearrange("p (a d) -> p a d", a=2), AX.X
                             ).then_inc(S["lam_arg"], 1)
        dve.wait_ge(S["lam_exp"], 1)
        lam_init = 0.8 - 0.6 * math.exp(-0.3)
        link(nc.vector.tensor_tensor(lams[:, 4:5], lams[:, 3:4], lams[:, 2:3], ALU.subtract))
        link(nc.vector.tensor_scalar(lams[:, 4:5], lams[:, 4:5], -(1.0 + lam_init), None, ALU.add))
        for col, name in ((5, "map_pair"), (6, "map_heads")):
            link(nc.vector.tensor_scalar(lams[:, col:col + 1], const(name), lams[:, 4:5], 1.0, ALU.mult, ALU.add))
        g = G_DA
        for dst in (ktok3, vtok3):
            for i, (t0, n) in enumerate(TILES):
                for half in range(2):
                    tr_dve(dve, g, dst[0:n, i, 512 * half:512 * half + 512].rearrange("p (a b) -> p a b", a=4), n,
                           128)
                    g += 1

    def subln_pe(pe):
        pe.wait_ge(S["osq_ready"], 1)
        pe.wait_ge(S["ppv_ev"], ATT["d"]["tile0"] + 4)
        pe.wait_ge(S["bpv_ev"], ATT["d"]["batch0"] + 8)
        for h in range(HC):
            last = nc.tensor.matmul(ps[:, h, 0:T], ones[:], sq[:, h, :], start=True, stop=True)
        last.then_inc(S["osum_ready"], 1)

    def subln_act(act):
        act.wait_ge(S["bpv_ev"], ATT["d"]["batch0"] + 8)
        nc.scalar.activation(sq[:], xn[:], ACT.Square).then_inc(S["osq_ready"], 1)
        act.wait_ge(S["osum_ready"], 1)
        nc.scalar.activation(sq[:], ps[:, :, 0:T], ACT.Sqrt, bias=epsc[:, 0:1], scale=1.0 / 128
                             ).then_inc(S["ostd_ready"], 1)

    def subln_dve(dve, link):
        lam_init = 0.8 - 0.6 * math.exp(-0.3)
        v = VEC["subln"]
        link(nc.vector.tensor_scalar(lams[:, 7:8], vec[:, v:v + 1], 1.0 - lam_init, None, ALU.mult))
        dve.wait_ge(S["ostd_ready"], 1)
        link(nc.vector.reciprocal(sq[:], sq[:]))
        nc.vector.scalar_tensor_tensor(xn[:], xn[:], lams[:, 7:8], sq[:], ALU.mult, ALU.mult
                                       ).then_inc(S["on_ready"], 1)
        dve.wait_ge(S["on_ready"], 1)

    def route_pe(pe, l):
        for i, (t0, n) in enumerate(TILES):
            for k in range(KD):
                last = nc.tensor.matmul(ps[0:n, 5, 36 * i:36 * i + 36], xn[:, k, t0:t0 + n], wrt[:, l, k, :],
                                        start=(k == 0), stop=(k == KD - 1))
        last.then_inc(S["lg_ps"], 1)
        pe.wait_ge(S["gate_ready"], l + 1)
        pe.wait_ge(S["rc_in"], 16 * (l + 1))
        for i, (t0, n) in enumerate(TILES):
            for j in range(i):
                nc.tensor.matmul(ps[0:n, 7, NE * i:NE * i + NE], ones[:, 0:n], amat[:, j, :], start=(j == 0),
                                 stop=False)
            nc.tensor.matmul(ps[0:n, 7, NE * i:NE * i + NE], before[0:n, 0:n], amat[0:n, i, :], start=(i == 0),
                             stop=True)
        for i, (t0, n) in enumerate(TILES):
            last = nc.tensor.matmul(ps[:, 7, 96:128], ones[0:n, :], amat[0:n, i, :], start=(i == 0), stop=(i == 2))
        last.then_inc(S["rank_ps"], 1)

    def route_act(act, l):
        act.wait_ge(S["gsel_ready"], l + 1)
        nc.scalar.activation(rt[:, 4, :, 0:4], rt[:, 3, :, 0:4], ACT.Exp).then_inc(S["gexp_ready"], 1)
        act.wait_ge(S["rexp_ready"], 2 * l + 1)
        nc.scalar.activation(rt[:, 15, :, 0:1], rt[:, 14, :, 0:1], ACT.Exp).then_inc(S["rexp_ready"], 1)

    def route_dve(dve, link, l):
        V = nc.vector

        def bc(x, w):
            return x.to_broadcast([128, 3, w])

        link(V.memset(lg[:, 2, :], 0.0))
        dve.wait_ge(S["lg_ps"], l + 1)
        V.tensor_tensor(lg[:, 0:2, :], ps[:, 5, 0:72].rearrange("p (t n) -> p t n", t=2),
                        brt[:, l, :].unsqueeze(1).to_broadcast([128, 2, 36]), ALU.add)
        link(V.tensor_tensor(lg[0:64, 2, :], ps[0:64, 5, 72:108], brt[0:64, l, :], ALU.add))
        gl, el = lg[:, :, 0:4], lg[:, :, 4:36].rearrange("p t (g e) -> p t g e", g=4)

        def first_max(x, w, rank, at, oh):
            link(V.reduce_max(rt[:, at, :, 0:1], x, AX.X))
            link(V.tensor_tensor(rt[:, at + 1, :, 0:w], x, bc(rt[:, at, :, 0:1], w), ALU.is_equal))
            link(V.tensor_tensor(rt[:, at + 1, :, 0:w], rt[:, at + 1, :, 0:w],
                                 const(rank).unsqueeze(1).to_broadcast([128, 3, w]), ALU.mult))
            link(V.reduce_max(rt[:, at, :, 1:2], rt[:, at + 1, :, 0:w], AX.X))
            link(V.tensor_tensor(oh, rt[:, at + 1, :, 0:w], bc(rt[:, at, :, 1:2], w), ALU.is_equal))

        ohg = rt[:, 2, :, 0:4]
        first_max(gl, 4, "rank_g", 0, ohg)
        V.tensor_tensor(rt[:, 3, :, 0:4], gl, bc(rt[:, 0, :, 0:1], 4), ALU.subtract).then_inc(S["gsel_ready"], 1)
        prod = rt[:, 16:20].rearrange("p a t e -> p (a t e)").rearrange("p (t g e) -> p t g e", t=3, g=4)
        link(V.tensor_tensor(prod, el, ohg.unsqueeze(3).to_broadcast([128, 3, 4, 8]), ALU.mult))
        es, oh1, es2, oh2 = rt[:, 5], rt[:, 8], rt[:, 9], rt[:, 12]
        link(V.tensor_tensor(es, prod[:, :, 0, :], prod[:, :, 1, :], ALU.add))
        link(V.tensor_tensor(es, es, prod[:, :, 2, :], ALU.add))
        link(V.tensor_tensor(es, es, prod[:, :, 3, :], ALU.add))
        first_max(es, 8, "rank_e", 6, oh1)
        link(V.tensor_scalar(es2, oh1, -BIG, None, ALU.mult))
        link(V.tensor_tensor(es2, es2, es, ALU.add))
        first_max(es2, 8, "rank_e", 10, oh2)
        V.tensor_tensor(rt[:, 14, :, 0:1], rt[:, 10, :, 0:1], rt[:, 6, :, 0:1], ALU.subtract
                        ).then_inc(S["rexp_ready"], 1)
        dve.wait_ge(S["gexp_ready"], l + 1)
        link(V.reduce_sum(rt[:, 13, :, 0:1], rt[:, 4, :, 0:4], AX.X))
        dve.wait_ge(S["rexp_ready"], 2 * l + 2)
        link(V.tensor_scalar(rt[:, 13, :, 1:2], rt[:, 15, :, 0:1], 1.0, None, ALU.add))
        link(V.tensor_tensor(rt[:, 13, :, 2:3], rt[:, 13, :, 0:1], rt[:, 13, :, 1:2], ALU.mult))
        link(V.reciprocal(rt[:, 13, :, 3:4], rt[:, 13, :, 2:3]))
        ew, both = rt[:, 20], rt[:, 21]
        link(V.tensor_tensor(ew, oh2, bc(rt[:, 15, :, 0:1], 8), ALU.mult))
        link(V.tensor_tensor(ew, ew, oh1, ALU.add))
        V.tensor_tensor(rt[:, 13, :, 4:5], rt[:, 13, :, 3:4], rt[:, 15, :, 0:1], ALU.mult)
        V.tensor_tensor(both, oh1, oh2, ALU.add)
        link(V.tensor_tensor(ew, ew, bc(rt[:, 13, :, 3:4], 8), ALU.mult))
        for dst, src in ((gate, ew), (amat, both)):
            for i in range(3):
                last = V.tensor_tensor(dst[:, i, :].rearrange("p (g e) -> p g e", g=4),
                                       ohg[:, i, :].unsqueeze(2).to_broadcast([128, 4, 8]),
                                       src[:, i, :].unsqueeze(1).to_broadcast([128, 4, 8]), ALU.mult)
        last.then_inc(S["gate_ready"], 1)
        dve.wait_ge(S["rank_ps"], l + 1)
        link(V.tensor_copy(cnt, ps[:, 7, 96:128]))
        link(V.tensor_tensor_scan(off, ones[:, 0:NE], cnt, 0.0, ALU.mult, ALU.add))
        link(V.tensor_tensor(off, off, cnt, ALU.subtract))
        pos = lg[:, :, 0:NE]
        link(V.memset(lg[:, 2, :], 0.0))
        V.tensor_tensor(pos[:, 0:2, :], ps[:, 7, 0:64].rearrange("p (t n) -> p t n", t=2),
                        off.unsqueeze(1).to_broadcast([128, 2, NE]), ALU.add)
        link(V.tensor_tensor(pos[0:64, 2, :], ps[0:64, 7, 64:96], off[0:64, :], ALU.add))
        pos4 = pos.rearrange("p t (g e) -> p t g e", g=4)
        link(V.tensor_tensor(prod, pos4, ohg.unsqueeze(3).to_broadcast([128, 3, 4, 8]), ALU.mult))
        for g in range(1, 4):
            link(V.tensor_tensor(es, prod[:, :, 0, :] if g == 1 else es, prod[:, :, g, :], ALU.add))
        for oh, at in ((oh1, 5), (oh2, 6)):
            link(V.tensor_tensor(both, es, oh, ALU.mult))
            link(V.reduce_sum(rt[:, 13, :, at:at + 1], both, AX.X))
        link(V.reduce_max(cmax, cnt, AX.X))
        V.tensor_copy(roff[0:1, 0:NE], off[0:1, :])
        V.tensor_scalar(roff[0:1, NE:NE + 1], cmax[0:1, :], CAP + 0.5, None, ALU.is_le).then_inc(S["off_ready"], 1)

    def moe_all_pe(pe, l):
        M = ML[l]
        u0 = UNIT[f"moe{l}"][0]
        for i, (t0, n) in enumerate(TILES):
            last = nc.tensor.transpose(ps[0:32, 6, t0:t0 + n], gate[0:n, i, :], ident[0:n, 0:n])
        last.then_inc(M["g_ps"], 1)
        pe.wait_ge(M["g_ev"], 1)
        for e in range(NE):
            if e >= 4:
                pe.wait_ge(M["gs_ready"], e - 3)
            nc.tensor.matmul(ps[:, 4 + e % 4, 0:T], ident[0:32, e:e + 1].to_broadcast([32, 128]), gT[0:32, :],
                             start=True, stop=True).then_inc(M["gs_ps"], 1)

        def up(u, s, bank):
            pe.wait_ge(S["w_lo"], u * 2 + 2)
            for j in range(2):
                for k in range(KD):
                    last = mm3(ps[:, bank + j, 0:T], s, k, 128 * j, xh[:, k, :], xl[:, k, :], k == 0, k == KD - 1)
            last.then_inc(S["w_used"], 1)

        def down(u, s, bank):
            pe.wait_ge(S["w_lo"], u * 2 + 2)
            for j in range(4):
                for k in range(4):
                    last = mm3(ps[:, bank + j, 0:T], s, k, 128 * j, hh[:, k, :], hl[:, k, :], k == 0, k == 3, 512)
            last.then_inc(S["w_used"], 1)

        pe.wait_ge(S["w_ev"], u0)
        up(u0, 0, 0)
        up(u0 + 1, 1, 2)
        pe.wait_ge(M["gs_ready"], NE)
        up(u0 + 2, 0, 4)
        up(u0 + 3, 1, 6)
        with pe.Fori(1, NE // 2) as i:
            u = i * 6 + (u0 - 2)
            pe.wait_ge(S["w_ev"], u - 2)
            up(u, 0, 0)
            up(u + 1, 1, 2)
            pe.wait_ge(S["w_ev"], u)
            pe.wait_ge(M["hl"], i * 2)
            down(u + 2, 0, 4)
            pe.wait_ge(S["w_ev"], u + 2)
            down(u + 3, 1, 0)
            pe.wait_ge(S["w_ev"], u + 3)
            up(u + 4, 0, 4)
            up(u + 5, 1, 6)
        u = u0 + 94
        pe.wait_ge(S["w_ev"], u)
        pe.wait_ge(M["hl"], NE)
        down(u, 0, 4)
        down(u + 1, 1, 0)

    def moe_all_act(act, l, last_layer):
        M = ML[l]
        u0 = UNIT[f"moe{l}"][0]

        def hi(u, s):
            act.wait_ge(S["w_used"], u + 1)
            split_hi(act, u + 2, s)

        def sig(u, bank, prev):
            if prev is not None:
                act.wait_ge(S["w_ev"], prev + 1)
            nc.scalar.activation(e_t, ps[:, bank:bank + 2, 0:T], ACT.Exp, scale=-1.0 / WSCALE
                                 ).then_inc(M["exp"], 1)

        def hid(n, j):
            act.wait_ge(M["c"], n + 1)
            nc.scalar.copy(hh[:, 2 * j:2 * j + 2, :], cg[:, j]).then_inc(M["hh"], 1)

        n0_ = 0
        for e in range(NE):
            act.wait_ge(M["gs_ps"], e + 1)
            nc.scalar.copy(gbc[:, e, :], ps[:, 4 + e % 4, 0:T]).then_inc(M["gs_ready"], 1)
        hi(u0, 0)
        sig(u0, 0, None)
        hi(u0 + 1, 1)
        hid(n0_, 0)
        hi(u0 + 2, 0)
        sig(u0 + 2, 4, u0 + 1)
        hi(u0 + 3, 1)
        hid(n0_ + 1, 1)
        with act.Fori(1, NE // 2) as i:
            u = i * 6 + (u0 - 2)
            n = i * 2 + n0_
            hi(u, 0)
            sig(u, 0, u - 1)
            hi(u + 1, 1)
            hi(u + 2, 0)
            hi(u + 3, 1)
            hid(n, 0)
            hi(u + 4, 0)
            sig(u + 4, 4, u + 1)
            hi(u + 5, 1)
            hid(n + 1, 1)
        if not last_layer:
            hi(u0 + 94, 0)
            hi(u0 + 95, 1)

    def moe_all_pool(pool, l):
        M = ML[l]
        def gated(u, n, e, j):
            pool.wait_ge(S["w_ev"], u + 1)
            if not isinstance(n, int) or n >= 2:
                pool.wait_ge(M["hl"], n - 1)
            for c in range(2):
                g = gbc[:, e, :] if isinstance(e, int) else gbc[:, ds(e, 1), :].rearrange("p a t -> p (a t)")
                last = nc.gpsimd.tensor_tensor(cg[:, j, c, :], b_t[:, c, :], g, ALU.mult)
            last.then_inc(M["c"], 1)

        u0 = UNIT[f"moe{l}"][0]
        pool.wait_ge(M["gs_ready"], NE)
        gated(u0 + 1, 0, 0, 0)
        gated(u0 + 3, 1, 1, 1)
        with pool.Fori(1, NE // 2) as i:
            u = i * 6 + (u0 - 2)
            gated(u + 1, i * 2, i * 2, 0)
            gated(u + 5, i * 2 + 1, i * 2 + 1, 1)

    def moe_all_dve(dve, l, last_layer):
        M = ML[l]
        link = Chain(dve, M["chain"], M["loop"])
        u0 = UNIT[f"moe{l}"][0]

        def lo(u, s):
            dve.wait_ge(S["w_used"], u + 1)
            split_lo(dve, u + 2, s)

        def act_fn(u, n, bank, nfirst=False):
            dve.wait_ge(M["exp"], n + 1)
            link(nc.vector.tensor_scalar(r_t, e_t, 1.0, None, ALU.add))
            link(nc.vector.reciprocal(r_t, r_t))
            nc.vector.scalar_tensor_tensor(a_t, ps[:, bank:bank + 2, 0:T], 1 / WSCALE, r_t, ALU.mult, ALU.mult
                                           ).then_inc(S["w_ev"], 1)
            dve.wait_ge(S["w_ev"], u + 1)
            if not nfirst:
                dve.wait_ge(M["c"], n)
            nc.vector.scalar_tensor_tensor(b_t, ps[:, bank + 2:bank + 4, 0:T], 1 / WSCALE, a_t, ALU.mult, ALU.mult
                                           ).then_inc(S["w_ev"], 1)

        def low(n, j):
            dve.wait_ge(M["hh"], n + 1)
            nc.vector.tensor_tensor(hl[:, 2 * j:2 * j + 2, :], cg[:, j], hh[:, 2 * j:2 * j + 2, :], ALU.subtract
                                    ).then_inc(M["hl"], 1)

        def add(half, bank):
            x = xT[:, 4 * half:4 * half + 4, :]
            nc.vector.scalar_tensor_tensor(x, ps[:, bank:bank + 4, 0:T], 1 / WSCALE, x, ALU.mult, ALU.add
                                           ).then_inc(S["w_ev"], 1)

        n0_ = 0
        dve.wait_ge(M["g_ps"], 1)
        nc.vector.tensor_copy(gT[0:32, :], ps[0:32, 6, 0:T]).then_inc(M["g_ev"], 1)
        lo(u0, 0)
        lo(u0 + 1, 1)
        act_fn(u0, n0_, 0, nfirst=True)
        low(n0_, 0)
        lo(u0 + 2, 0)
        lo(u0 + 3, 1)
        act_fn(u0 + 2, n0_ + 1, 4)
        low(n0_ + 1, 1)
        with dve.Fori(1, NE // 2) as i:
            link.enter(i - 1, 4)
            u = i * 6 + (u0 - 2)
            n = i * 2 + n0_
            lo(u, 0)
            lo(u + 1, 1)
            act_fn(u, n, 0)
            lo(u + 2, 0)
            add(0, 4)
            lo(u + 3, 1)
            add(1, 0)
            low(n, 0)
            lo(u + 4, 0)
            lo(u + 5, 1)
            act_fn(u + 4, n + 1, 4)
            low(n + 1, 1)
        link.leave(NE // 2 - 1)
        if last_layer:
            dve.wait_ge(S["w_used"], u0 + 95)
            add(0, 4)
            dve.wait_ge(S["w_used"], u0 + 96)
            add(1, 0)
        else:
            lo(u0 + 94, 0)
            add(0, 4)
            lo(u0 + 95, 1)
            add(1, 0)
        dve.wait_ge(S["w_ev"], u0 + 96)
        nc.vector.memset(gT[0:1, 0:1], 0.0).then_inc(S["moe_done"], 1)

    def pack_pe(pe, l):
        M = ML[l]
        pe.wait_ge(S["xn_ready"], 3 * l + 3)
        for g in range(6):
            i, half = g // 2, g % 2
            t0, n = TILES[i]
            if g >= 4:
                pe.wait_ge(M["xt_ev"], g - 3)
            for j in range(4):
                last = nc.tensor.transpose(ps[0:n, g % 4, 128 * j:128 * j + 128], xn[:, 4 * half + j, t0:t0 + n],
                                           ident)
            last.then_inc(M["xt_ps"], 1)
        pe.wait_ge(M["p_ready"], 1)
        for half in range(2):
            c = slice(SH * half, SH * half + SH)
            for i, (t0, n) in enumerate(TILES):
                last = nc.tensor.matmul(ps[:, 4 + half, 0:SH], ones[0:n, :], pw[0:n, i, c], start=(i == 0),
                                        stop=(i == 2))
        last.then_inc(M["gs_ps"], 1)
        for st in range(5):
            if st >= 2:
                pe.wait_ge(M["g_ev"], st - 1)
            for i, (t0, n) in enumerate(TILES):
                last = nc.tensor.matmul(ps[:, 6 + st % 2, t0:t0 + n], pk[0:n, i, 128 * st:128 * st + 128],
                                        identb[0:n, 0:n], start=True, stop=True)
            last.then_inc(M["g_ps"], 1)
        pe.wait_ge(M["xt_ev"], 6)
        pe.wait_ge(M["g_ev"], 5)
        pe.wait_ge(M["gs_ready"], 1)
        for g in range(32):
            k, half, part = g // 4, (g // 2) % 2, g % 2
            if g >= 8:
                pe.wait_ge(M["xg_hi"] if part == 0 else M["xg_lo"], (g - 8) // 2 + 1)
            src = (xth, xtl)[part]
            for i, (t0, n) in enumerate(TILES):
                last = nc.tensor.matmul(ps[:, g % 8, 0:SH], src[0:n, i, 128 * k:128 * k + 128],
                                        pk[0:n, i, SH * half:SH * half + SH], start=(i == 0), stop=(i == 2))
            last.then_inc(M["xg_ps"], 1)

    def pack_act(act, l):
        M = ML[l]
        for g in range(6):
            i, half = g // 2, g % 2
            n = TILES[i][1]
            act.wait_ge(M["xt_ps"], g + 1)
            nc.scalar.copy(xth[0:n, i, 512 * half:512 * half + 512], ps[0:n, g % 4, :]).then_inc(M["xt_hi"], 1)
        for st in range(5):
            act.wait_ge(M["g_ps"], st + 1)
            nc.scalar.copy(gk[:, st, :], ps[:, 6 + st % 2, 0:T]).then_inc(M["g_ev"], 1)
        for g in range(0, 32, 2):
            k, half = g // 4, (g // 2) % 2
            act.wait_ge(M["xg_ps"], g + 1)
            nc.scalar.copy(xgh[:, k, SH * half:SH * half + SH], ps[:, g % 8, 0:SH]).then_inc(M["xg_hi"], 1)

    def pack_dve(dve, l, link):
        M = ML[l]
        dve.wait_ge(S["rc_in"], 16 * (l + 1))
        for i in range(3):
            p1, p2, w1, w2 = (rt[:, 13, i, c:c + 1] for c in (5, 6, 3, 4))
            nc.vector.tensor_scalar(pk[:, i, :], iota, p1, None, ALU.is_equal)
            nc.vector.tensor_scalar(pw[:, i, :], iota, p1, w1, ALU.is_equal, ALU.mult)
            link(nc.vector.tensor_scalar(gslot, iota, p2, w2, ALU.is_equal, ALU.mult))
            nc.vector.scalar_tensor_tensor(pk[:, i, :], iota, p2, pk[:, i, :], ALU.is_equal, ALU.add)
            last = nc.vector.tensor_tensor(pw[:, i, :], pw[:, i, :], gslot, ALU.add)
            if i < 2:
                link(last)
        last.then_inc(M["p_ready"], 1)
        for g in range(6):
            i, half = g // 2, g % 2
            n = TILES[i][1]
            dve.wait_ge(M["xt_hi"], g + 1)
            nc.vector.tensor_tensor(xtl[0:n, i, 512 * half:512 * half + 512], ps[0:n, g % 4, :],
                                    xth[0:n, i, 512 * half:512 * half + 512], ALU.subtract).then_inc(M["xt_ev"], 1)
        dve.wait_ge(M["gs_ps"], 1)
        nc.vector.tensor_copy(gslot.rearrange("p (a b) -> p a b", a=2), ps[:, 4:6, 0:SH]).then_inc(M["gs_ready"], 1)
        for g in range(1, 32, 2):
            k, half = g // 4, (g // 2) % 2
            dve.wait_ge(M["xg_ps"], g + 1)
            nc.vector.tensor_copy(xgl[:, k, SH * half:SH * half + SH], ps[:, g % 8, 0:SH]).then_inc(M["xg_lo"], 1)

    def offset(eng, e):
        at = roff[0:1, e:e + 1] if isinstance(e, int) else roff[0:1, ds(e, 1)]
        return eng.value_load(at, min_val=0, max_val=2 * T)

    def moe_pack_pe(pe, l):
        M = ML[l]
        u0 = UNIT[f"moe{l}"][0]
        pack_pe(pe, l)
        pe.wait_ge(M["xg_hi"], 16)
        pe.wait_ge(M["xg_lo"], 16)

        def up(u, s, bank, at):
            pe.wait_ge(S["w_lo"], u * 2 + 2)
            for j in range(2):
                for k in range(KD):
                    last = mm3(ps[:, bank, CAP * j:CAP * j + CAP], s, k, 128 * j, xgh[:, k, ds(at, CAP)],
                               xgl[:, k, ds(at, CAP)], k == 0, k == KD - 1)
            last.then_inc(S["w_used"], 1)

        def down(u, s, bank):
            pe.wait_ge(S["w_lo"], u * 2 + 2)
            for e in range(2):
                for j in range(4):
                    for k in range(2):
                        c = CAP * (4 * e + j)
                        last = mm3(ps[:, bank, c:c + CAP], s, 2 * e + k, 128 * j, hh[:, 2 * e + k, 0:CAP],
                                   hl[:, 2 * e + k, 0:CAP], k == 0, k == 1, 512)
            last.then_inc(S["w_used"], 1)

        at = offset(pe, 0)
        up(u0, 0, 0, at)
        up(u0 + 1, 1, 1, at)
        at = offset(pe, 1)
        up(u0 + 2, 0, 2, at)
        up(u0 + 3, 1, 3, at)
        with pe.Fori(1, NE // 2) as i:
            u = i * 6 + (u0 - 2)
            at = offset(pe, i * 2)
            pe.wait_ge(M["b"], i * 2 - 1)
            up(u, 0, 0, at)
            up(u + 1, 1, 1, at)
            pe.wait_ge(M["hl"], i * 2)
            down(u + 2, 0, 4)
            down(u + 3, 1, 5)
            at = offset(pe, i * 2 + 1)
            pe.wait_ge(M["b"], i * 2)
            up(u + 4, 0, 2, at)
            pe.wait_ge(M["y"], i * 4)
            up(u + 5, 1, 3, at)
        pe.wait_ge(M["hl"], NE)
        down(u0 + 94, 0, 4)
        down(u0 + 95, 1, 5)
        pe.wait_ge(M["y"], 2 * NE)
        for g in range(10):
            st, half = g // 2, g % 2
            if g >= 4:
                pe.wait_ge(M["ys_lo"], g - 3)
            for j in range(4):
                last = nc.tensor.transpose(ps[:, g % 4, 128 * j:128 * j + 128],
                                           yc[:, 4 * half + j, 128 * st:128 * st + 128], ident)
            last.then_inc(M["ys_ps"], 1)
        pe.wait_ge(M["ys_lo"], 10)
        for k in range(KD):
            for st in range(5):
                for part in (ysh, ysl):
                    last = nc.tensor.matmul(ps[:, k, 0:T], part[:, st, 128 * k:128 * k + 128], gk[:, st, :],
                                            start=(st == 0 and part is ysh), stop=(st == 4 and part is ysl))
            last.then_inc(M["z_ps"], 1)

    def moe_pack_act(act, l, last_layer):
        M = ML[l]
        u0 = UNIT[f"moe{l}"][0]
        pack_act(act, l)

        def hi(u, s):
            act.wait_ge(S["w_used"], u + 1)
            split_hi(act, u + 2, s)

        def sig(n, bank):
            act.wait_ge(M["b"], n)
            nc.scalar.activation(e_t[:, :, 0:CAP], ps[:, bank, 0:2 * CAP].rearrange("p (a b) -> p a b", a=2),
                                 ACT.Exp, scale=-1.0 / WSCALE).then_inc(M["exp"], 1)

        def hid(n, j):
            act.wait_ge(M["c"], n + 1)
            nc.scalar.copy(hh[:, 2 * j:2 * j + 2, 0:CAP], cg[:, j, :, 0:CAP]).then_inc(M["hh"], 1)

        def out(p, half, at):
            for e in range(2):
                nc.scalar.mul(yc[:, 4 * half:4 * half + 4, ds(at[e], CAP)],
                              ps[:, 4 + half, 256 * e:256 * e + 256].rearrange("p (a b) -> p a b", a=4),
                              1 / WSCALE).then_inc(M["y"], 1)
                if e == 0:
                    act.wait_ge(M["y"], p * 4 + (2 * half + 1))

        def first():
            hi(u0, 0)
            nc.scalar.activation(e_t[:, :, 0:CAP], ps[:, 0, 0:2 * CAP].rearrange("p (a b) -> p a b", a=2),
                                 ACT.Exp, scale=-1.0 / WSCALE).then_inc(M["exp"], 1)
            hi(u0 + 1, 1)
            hid(0, 0)
            hi(u0 + 2, 0)
            sig(1, 2)
            hi(u0 + 3, 1)
            hid(1, 1)

        first()
        with act.Fori(1, NE // 2) as i:
            u = i * 6 + (u0 - 2)
            n = i * 2
            at = [offset(act, i * 2 - 2), offset(act, i * 2 - 1)]
            hi(u, 0)
            sig(n, 0)
            hi(u + 1, 1)
            hi(u + 2, 0)
            out(i - 1, 0, at)
            hi(u + 3, 1)
            out(i - 1, 1, at)
            hid(n, 0)
            hi(u + 4, 0)
            sig(n + 1, 2)
            hi(u + 5, 1)
            hid(n + 1, 1)
        at = [offset(act, NE - 2), offset(act, NE - 1)]
        for half in range(2):
            if last_layer:
                act.wait_ge(S["w_used"], u0 + 95 + half)
            else:
                hi(u0 + 94 + half, half)
            out(NE // 2 - 1, half, at)
        for g in range(10):
            st, half = g // 2, g % 2
            act.wait_ge(M["ys_ps"], g + 1)
            nc.scalar.copy(ysh[:, st, 512 * half:512 * half + 512], ps[:, g % 4, :]).then_inc(M["ys_hi"], 1)

    def moe_pack_pool(pool, l):
        M = ML[l]

        def gated(n, j):
            at = offset(pool, n)
            pool.wait_ge(M["b"], n + 1)
            if not isinstance(n, int) or n >= 2:
                pool.wait_ge(M["hl"], n - 1)
            for c in range(2):
                last = nc.gpsimd.tensor_tensor(cg[:, j, c, 0:CAP], b_t[:, c, 0:CAP], gslot[:, ds(at, CAP)], ALU.mult)
            last.then_inc(M["c"], 1)

        pool.wait_ge(M["gs_ready"], 1)
        gated(0, 0)
        gated(1, 1)
        with pool.Fori(1, NE // 2) as i:
            gated(i * 2, 0)
            gated(i * 2 + 1, 1)

    def moe_pack_dve(dve, l, last_layer):
        M = ML[l]
        u0 = UNIT[f"moe{l}"][0]
        link = Chain(dve, M["chain"], M["loop"])
        pack_dve(dve, l, link)

        def lo(u, s):
            dve.wait_ge(S["w_used"], u + 1)
            split_lo(dve, u + 2, s)

        def act_fn(n, bank):
            dve.wait_ge(M["exp"], n + 1)
            r, ab, bb = r_t[:, :, 0:CAP], a_t[:, :, 0:CAP], b_t[:, :, 0:CAP]
            g, u = (ps[:, bank + c, 0:2 * CAP].rearrange("p (a b) -> p a b", a=2) for c in range(2))
            link(nc.vector.tensor_scalar(r, e_t[:, :, 0:CAP], 1.0, None, ALU.add))
            link(nc.vector.reciprocal(r, r))
            link(nc.vector.scalar_tensor_tensor(ab, g, 1 / WSCALE, r, ALU.mult, ALU.mult))
            if not isinstance(n, int) or n >= 1:
                dve.wait_ge(M["c"], n)
            nc.vector.scalar_tensor_tensor(bb, u, 1 / WSCALE, ab, ALU.mult, ALU.mult).then_inc(M["b"], 1)

        def low(n, j):
            dve.wait_ge(M["hh"], n + 1)
            nc.vector.tensor_tensor(hl[:, 2 * j:2 * j + 2, 0:CAP], cg[:, j, :, 0:CAP],
                                    hh[:, 2 * j:2 * j + 2, 0:CAP], ALU.subtract).then_inc(M["hl"], 1)

        lo(u0, 0)
        lo(u0 + 1, 1)
        act_fn(0, 0)
        low(0, 0)
        lo(u0 + 2, 0)
        lo(u0 + 3, 1)
        act_fn(1, 2)
        low(1, 1)
        with dve.Fori(1, NE // 2) as i:
            link.enter(i - 1, 6)
            u = i * 6 + (u0 - 2)
            n = i * 2
            lo(u, 0)
            lo(u + 1, 1)
            act_fn(n, 0)
            lo(u + 2, 0)
            lo(u + 3, 1)
            low(n, 0)
            lo(u + 4, 0)
            lo(u + 5, 1)
            act_fn(n + 1, 2)
            low(n + 1, 1)
        link.leave(NE // 2 - 1)
        if not last_layer:
            lo(u0 + 94, 0)
            lo(u0 + 95, 1)
        for g in range(10):
            st, half = g // 2, g % 2
            dve.wait_ge(M["ys_hi"], g + 1)
            nc.vector.tensor_tensor(ysl[:, st, 512 * half:512 * half + 512], ps[:, g % 4, :],
                                    ysh[:, st, 512 * half:512 * half + 512], ALU.subtract).then_inc(M["ys_lo"], 1)
        for k in range(KD):
            dve.wait_ge(M["z_ps"], k + 1)
            last = nc.vector.tensor_tensor(xT[:, k, :], xT[:, k, :], ps[:, k, 0:T], ALU.add)
        last.then_inc(S["w_ev"], 96)
        dve.wait_ge(S["w_ev"], u0 + 96)
        nc.vector.memset(gslot[0:1, 0:1], 0.0).then_inc(S["moe_done"], 1)

    def moe(eng, l, packed, general, *args):
        eng.wait_ge(S["off_ready"], l + 1)
        fits = eng.value_load(roff[0:1, NE:NE + 1], min_val=0, max_val=1)
        with eng.If(fits > 0):
            packed(eng, l, *args)
        with eng.Else():
            general(eng, l, *args)

    def pe_memory(pe, l):
        n = 1 + 3 * l
        norm_pe(pe, n)
        gemm_pe(pe, f"memq{l}", (3, 8)[l])
        pe.wait_ge(S["w_ev"], sum(UNIT[f"memq{l}"]))
        prompt_pe(pe, f"m{l}")
        batch_pe(pe, f"m{l}")
        pe.wait_ge(S["bpv_ev"], ATT[f"m{l}"]["batch0"] + 8)
        gemm_pe(pe, f"memo{l}", (4, 9)[l])
        norm_pe(pe, n + 1)
        pe.wait_ge(S["xn_ready"], n + 2)
        route_pe(pe, l)
        moe(pe, l, moe_pack_pe, moe_all_pe)

    def pe_rest(pe):
        pe.wait_ge(S["vec_in"], NVIN)
        pe_memory(pe, 0)
        norm_pe(pe, 3)
        gemm_pe(pe, "qkv", 6)
        rope_pe(pe)
        pe.wait_ge(S["tr_ev"], G_Y)
        prompt_pe(pe, "d")
        batch_pe(pe, "d")
        subln_pe(pe)
        pe.wait_ge(S["ostd_ready"], 1)
        gemm_pe(pe, "out_c", 7)
        pe_memory(pe, 1)
        norm_pe(pe, 6)
        pe.wait_ge(S["xn_ready"], 7)
        g = G_Y
        for i, (t0, n) in enumerate(TILES):
            for half in range(2):
                tr_pe(pe, g, [xn[:, 4 * half + j, t0:t0 + n] for j in range(4)], 128)
                g += 1

    def act_memory(act, link, l):
        n = 1 + 3 * l
        norm_act(act, n)
        act.wait_ge(S["xn_ready"], n + 1)
        input_act(act, xn[:])
        gemm_copy_act(act, f"memq{l}", z[:, 0:8])
        prompt_act(act, f"m{l}")
        batch_act(act, f"m{l}")
        act.wait_ge(S["bpv_ev"], ATT[f"m{l}"]["batch0"] + 8)
        input_act(act, xn[:])
        gemm_split_act(act, f"memo{l}")
        act.wait_ge(S["w_ev"], sum(UNIT[f"memo{l}"]))
        norm_act(act, n + 1)
        act.wait_ge(S["xn_ready"], n + 2)
        input_act(act, xn[:])
        route_act(act, l)
        moe(act, l, moe_pack_act, moe_all_act, l == 1)

    def act_rest(act, link):
        act.wait_ge(S["w_ev"], sum(UNIT["out_a"]))
        act.wait_ge(S["out_c"], 16 * 10)
        act.wait_ge(c_out[0], 32)
        act.wait_ge(c_out[1], 32)
        act_memory(act, link, 0)
        act.wait_ge(S["moe_done"], 1)
        norm_act(act, 3)
        act.wait_ge(S["xn_ready"], 4)
        input_act(act, xn[:])
        gemm_copy_act(act, "qkv", zc[:])
        act.wait_ge(S["lam_arg"], 1)
        nc.scalar.activation(lams[:, 2:4], lams[:, 0:2], ACT.Exp).then_inc(S["lam_exp"], 1)
        prompt_act(act, "d")
        batch_act(act, "d")
        subln_act(act)
        act.wait_ge(S["on_ready"], 1)
        input_act(act, xn[:])
        gemm_split_act(act, "out_c")
        act.wait_ge(S["w_ev"], sum(UNIT["out_c"]))
        act_memory(act, link, 1)
        act.wait_ge(S["moe_done"], 2)
        norm_act(act, 6)

    def dve_memory(dve, link, l):
        n = 1 + 3 * l
        norm_dve(dve, link, n)
        input_dve(dve, (3, 8)[l], xn[:])
        gemm_split_dve(dve, f"memq{l}")
        dve.wait_ge(S["w_ev"], sum(UNIT[f"memq{l}"]))
        prompt_dve(dve, link, f"m{l}")
        batch_dve(dve, link, f"m{l}")
        dve.wait_ge(S["bpv_ev"], ATT[f"m{l}"]["batch0"] + 8)
        input_dve(dve, (4, 9)[l], xn[:])
        gemm_add_dve(dve, f"memo{l}")
        norm_dve(dve, link, n + 1)
        input_dve(dve, (5, 10)[l], xn[:])
        route_dve(dve, link, l)
        moe(dve, l, moe_pack_dve, moe_all_dve, l == 1)
        dve.wait_ge(S["moe_done"], l + 1)

    def dve_rest(dve, link):
        dve_memory(dve, link, 0)
        norm_dve(dve, link, 3)
        input_dve(dve, 6, xn[:])
        gemm_split_dve(dve, "qkv")
        rope_dve(dve, link)
        prompt_dve(dve, link, "d")
        batch_dve(dve, link, "d")
        subln_dve(dve, link)
        input_dve(dve, 7, xn[:])
        gemm_add_dve(dve, "out_c")
        dve_memory(dve, link, 1)
        norm_dve(dve, link, 6)
        g = G_Y
        for i, (t0, n) in enumerate(TILES):
            for half in range(2):
                tr_dve(dve, g, x_nat[0:n, i, 512 * half:512 * half + 512].rearrange("p (a b) -> p a b", a=4), n, 128)
                g += 1

    def pool_rest(pool, link):
        pool.wait_ge(S["out_c"], 16 * 10)
        pool.wait_ge(c_out[0], 32)
        pool.wait_ge(c_out[1], 32)
        pool.wait_ge(S["in_lo"], 3)
        batch_pool(pool, link, "m0")
        pool.wait_ge(S["in_lo"], 5)
        pool.dma_start(rc, a["slots"]).then_inc(S["rc_in"], 16)
        moe(pool, 0, moe_pack_pool, moe_all_pool)
        rope_pool(pool, link)
        pool.wait_ge(S["tr_ev"], G_Y)
        pool.dma_start(o["p_k"][0, 0].rearrange("(t p) h m d -> p t (h m d)", p=128), ktok3[:, 0:2, :]
                       ).then_inc(S["out_p"], 16)
        pool.dma_start(o["s_k"][0].rearrange("b i h m d -> (b i) (h m d)"), ktok3[0:64, 2, :]).then_inc(S["out_p"], 16)
        pool.dma_start(o["p_v"][0, 0].rearrange("(t p) h d -> p t (h d)", p=128), vtok3[:, 0:2, :]
                       ).then_inc(S["out_p"], 16)
        pool.dma_start(o["s_v"][0].rearrange("b i h d -> (b i) (h d)"), vtok3[0:64, 2, :]).then_inc(S["out_p"], 16)
        pool.wait_ge(S["out_p"], 64)
        batch_pool(pool, link, "d")
        pool.wait_ge(S["in_lo"], 8)
        batch_pool(pool, link, "m1")
        pool.wait_ge(S["in_lo"], 10)
        pool.dma_start(rc, a["slots"]).then_inc(S["rc_in"], 16)
        moe(pool, 1, moe_pack_pool, moe_all_pool)
        pool.wait_ge(S["tr_ev"], G_Y + 6)
        pool.dma_start(o["y_prompt"][0].rearrange("(t p) d -> p t d", p=128), x_nat[:, 0:2, :]).then_inc(S["out_y"], 16)
        pool.dma_start(o["y_sample"].rearrange("b i d -> (b i) d"), x_nat[0:64, 2, :]).then_inc(S["out_y"], 16)
        pool.wait_ge(S["out_y"], 32)

    @block.gpsimd
    def _(pool):
        link = Chain(pool, S["pool_chain"], S["pool_loop"])
        nc.gpsimd.memset(ones[:], 1.0)
        nc.gpsimd.memset(wgate[:], 0.0)
        nc.gpsimd.memset(epsc[:, 0:1], EPS)
        nc.gpsimd.memset(epsc[:, 1:2], 1.0).then_inc(S["cst_ready"], 1)
        pool.dma_start(cst[:], a["consts"]).then_inc(S["const_in"], 16)
        pool.dma_start(mem_nat, a["mem_prompt"][0].rearrange("(t p) d -> p t d", p=128)).then_inc(S["mem_in"], 16)
        pool.dma_start(x_nat[:, 0:2, :], a["x_prompt"][0].rearrange("(t p) d -> p t d", p=128)
                       ).then_inc(S["x_in"], 16)
        pool.dma_start(x_nat[0:64, 2, :], a["x_sample"].rearrange("b i d -> (b i) d")).then_inc(S["x_in"], 16)
        r = 0
        for name in ("norm_mix_g", "norm_mem_g", "norm_ffn_g"):
            pool.dma_start(vecs[r:r + 16, :], a[name].rearrange("l (k p) -> (l k) p", p=128)
                           ).then_inc(S["vec_in"], 16)
            r += 16
        pool.dma_start(vecs[r:r + 8, :], a["final_norm_g"].rearrange("(k p) -> k p", p=128)
                       ).then_inc(S["vec_in"], 16)
        pool.dma_start(vecs[r + 8:r + 12, :], a["head_norm_g_a"][0].rearrange("(k p) -> k p", p=128)
                       ).then_inc(S["vec_in"], 16)
        pool.dma_start(vecs[r + 12:r + 13, :], a["subln_g_c"]).then_inc(S["vec_in"], 16)
        pool.dma_start(vecs[r + 13:r + 25, :], a["conv_w_b"][0].rearrange("j (k p) -> (j k) p", p=128)
                       ).then_inc(S["vec_in"], 16)
        pool.dma_start(ptab[:], a["page_table"].rearrange("b n -> (b n)").unsqueeze(0)).then_inc(S["tab_in"], 16)
        pool.wait_ge(S["tab_in"], 16)
        pool.wait_ge(S["cst_ready"], 1)
        wg = a["w_in_a"][0].rearrange("(k p) n -> p k n", p=128)
        pool.dma_start(wgate[:, :, 0:4], wg[:, :, 2048:2052]).then_inc(S["gate_in"], 16)
        pool.dma_start(wgate[:, :, 32:36], wg[:, :, 2052:2056]).then_inc(S["gate_in"], 16)
        pool.dma_start(gbias[0:4, :], a["gate_b_a"][0, 0].rearrange("(h o) -> h o", o=1)).then_inc(S["vec_in"], 16)
        pool.dma_start(gbias[32:36, :], a["gate_b_a"][0, 1].rearrange("(h o) -> h o", o=1)
                       ).then_inc(S["vec_in"], 16)
        for l in range(2):
            pool.dma_start(wrt[:, l, :, 0:4], a["w_router_g"][l].rearrange("(k p) n -> p k n", p=128)
                           ).then_inc(S["vec_in"], 16)
            pool.dma_start(wrt[:, l, :, 4:36], a["w_router_e"][l].rearrange("(k p) n -> p k n", p=128)
                           ).then_inc(S["vec_in"], 16)
            pool.dma_start(brt[:, l, 0:4], a["b_router_g"][l].partition_broadcast(128)).then_inc(S["vec_in"], 16)
            pool.dma_start(brt[:, l, 4:36], a["b_router_e"][l].partition_broadcast(128)).then_inc(S["vec_in"], 16)
        pool.dma_start(lamv[:], a["lambda_c"][0].rearrange("a b -> (a b)").partition_broadcast(128)
                       ).then_inc(S["vec_in"], 16)
        for l in range(2):
            pool.wait_ge(S["tr_ev"], G_MKV + 8 * l + 4)
            pool.dma_start(o["p_mem_k"][l, 0].rearrange("(t p) h d -> p t (h d)", p=128), mk_out
                           ).then_inc(S["out_mem"], 16)
            pool.wait_ge(S["tr_ev"], G_MKV + 8 * l + 8)
            pool.dma_start(o["p_mem_v"][l, 0].rearrange("(t p) h d -> p t (h d)", p=128), memv[:, l]
                           ).then_inc(S["out_mem"], 16)
        pool.wait_ge(S["out_mem"], 64)
        pool.wait_ge(S["in_lo"], 2)
        mlstm_pool(pool, link)
        mlstm_pool_out(pool, link)
        pool_rest(pool, link)

    @block.tensor
    def _(pe):
        pe.wait_ge(S["const_in"], 16)
        pe.wait_ge(S["cst_ready"], 1)
        g = G_X
        pe.wait_ge(S["x_in"], 32)
        for i, (t0, n) in enumerate(TILES):
            for half in range(2):
                tr_pe(pe, g, [x_nat[0:n, i, 512 * half + 128 * j:512 * half + 128 * j + 128] for j in range(4)], n)
                g += 1
        pe.wait_ge(S["mem_in"], 16)
        for i in range(2):
            for half in range(2):
                tr_pe(pe, g, [mem_nat[:, i, 512 * half + 128 * j:512 * half + 128 * j + 128] for j in range(4)], 128)
                g += 1
        pe.wait_ge(S["vec_in"], NVIN)
        pe.wait_ge(S["tr_ev"], G_MKV)
        nc.tensor.transpose(ps[:, 4, 0:NVEC], vecs[:], ident[0:NVEC, 0:NVEC]).then_inc(S["vec_ps"], 1)
        pe.wait_ge(S["vec_ev"], 1)
        for l in range(2):
            for kv in range(2):
                name = ("memk", "memv")[kv] + str(l)
                gemm_pe(pe, name, 0, 256)
                pe.wait_ge(S["w_ev"], sum(UNIT[name]))
                src = memkT[:, l] if kv == 0 else mvT
                for i in range(2):
                    for half in range(2):
                        tr_pe(pe, g, [src[:, 4 * half + j, 128 * i:128 * i + 128] for j in range(4)], 128)
                        g += 1
        pe.wait_ge(S["tr_ev"], g)
        norm_pe(pe, 0)
        pe.wait_ge(S["xn_ready"], 1)
        mlstm_pe(pe)
        gemm_pe(pe, "out_a", 2)
        pe_rest(pe)

    @block.scalar
    def _(act):
        link = Chain(act, S["act_chain"], S["act_loop"])
        for s in range(2):
            split_hi(act, s, s)
        act.wait_ge(S["tr_ev"], G_MKV)
        input_act(act, sq[:, :, 0:256], 256)
        for l in range(2):
            gemm_copy_act(act, f"memk{l}", memkT[:, l], 256)
            if l:
                act.wait_ge(S["tr_ps"], G_MKV + 8)
            gemm_copy_act(act, f"memv{l}", mvT, 256)
        act.wait_ge(S["in_lo"], 1)
        norm_act(act, 0)
        act.wait_ge(S["xn_ready"], 1)
        input_act(act, xn[:])
        act.wait_ge(S["out_mem"], 64)
        gemm_copy_act(act, "in_a", z[:, 0:16])
        gemm_copy_act(act, "in_b", z[:, 16:28])
        mlstm_act(act, link)
        act.wait_ge(S["y_ready"], 1)
        input_act(act, xn[:])
        gemm_split_act(act, "out_a")
        act_rest(act, link)

    @block.vector
    def _(dve):
        link = Chain(dve, S["dve_chain"], S["dve_loop"])
        dve.wait_ge(S["const_in"], 16)
        nc.vector.tensor_copy(maskb[:], cst[:, m0:m0 + 768])
        link(nc.vector.tensor_copy(identb[:], ident))
        for s in range(2):
            split_lo(dve, s, s)
        g = G_X
        for i, (t0, n) in enumerate(TILES):
            for half in range(2):
                tr_dve(dve, g, xT[:, 4 * half:4 * half + 4, t0:t0 + n], 128, n)
                g += 1
        for i in range(2):
            for half in range(2):
                tr_dve(dve, g, sq[:, 4 * half:4 * half + 4, 128 * i:128 * i + 128], 128, 128)
                g += 1
        dve.wait_ge(S["vec_ps"], 1)
        nc.vector.tensor_copy(vec[:], ps[:, 4, 0:NVEC]).then_inc(S["vec_ev"], 1)
        dve.wait_ge(S["tr_ev"], G_MKV)
        input_dve(dve, 0, sq[:, :, 0:256], 256)
        for l in range(2):
            for kv in range(2):
                gemm_split_dve(dve, ("memk", "memv")[kv] + str(l))
                if kv == 0 and l == 1:
                    dve.wait_ge(S["out_mem"], 32)
                for i in range(2):
                    for half in range(2):
                        dst = mk_out if kv == 0 else memv[:, l]
                        tr_dve(dve, g, dst[:, i, 512 * half:512 * half + 512].rearrange("p (a b) -> p a b", a=4),
                               128, 128)
                        g += 1
        norm_dve(dve, link, 0)
        input_dve(dve, 1, xn[:])
        gemm_split_dve(dve, "in_a")
        gemm_split_dve(dve, "in_b")
        mlstm_dve(dve, link)
        input_dve(dve, 2, xn[:])
        gemm_add_dve(dve, "out_a")
        dve_rest(dve, link)



_INS = ['x_prompt', 'x_sample', 'state_mlstm_C', 'state_mlstm_n', 'state_mlstm_m', 'state_conv', 'cache_k', 'cache_v',
        'page_table', 'cache_mem_k', 'cache_mem_v', 'mem_prompt', 'norm_mix_g', 'norm_mem_g', 'norm_ffn_g',
        'final_norm_g', 'w_in_a', 'gate_b_a', 'head_norm_g_a', 'conv_w_b', 'w_out_a', 'w_qkv_c', 'lambda_c',
        'subln_g_c', 'w_out_c', 'w_mem_q', 'w_mem_k', 'w_mem_v', 'w_mem_o', 'w_router_g', 'b_router_g', 'w_router_e',
        'b_router_e', 'w_exp_gate', 'w_exp_up', 'w_exp_down']
_OUTS = [("y_prompt", (1, 256, 1024)), ("y_sample", (8, 8, 1024)), ("p_C", (1, 1, 4, 128, 128)),
         ("p_n", (1, 1, 4, 128)), ("p_m", (1, 1, 4)), ("p_conv", (1, 1, 2, 512)), ("p_k", (1, 1, 256, 8, 2, 64)),
         ("p_v", (1, 1, 256, 8, 128)), ("p_mem_k", (2, 1, 256, 4, 256)), ("p_mem_v", (2, 1, 256, 4, 256)),
         ("s_C", (1, 8, 4, 128, 128)), ("s_n", (1, 8, 4, 128)), ("s_m", (1, 8, 4)), ("s_conv", (1, 8, 2, 512)),
         ("s_k", (1, 8, 8, 8, 2, 64)), ("s_v", (1, 8, 8, 8, 128))]


def kernel(**inputs):
    import concourse.bacc as bacc
    from concourse import mybir
    from concourse.bass_utils import run_bass_kernel_spmd

    nc = bacc.Bacc("TRN2", target_bir_lowering=False, num_devices=1)
    arrays = {f"in_{n}": np.ascontiguousarray(inputs[n]) for n in _INS}
    arrays["in_consts"] = constants()
    arrays["in_slots"] = slot_constants()
    a = {n[3:]: nc.dram_tensor(n, v.shape, mybir.dt.from_np(v.dtype), kind="ExternalInput").ap()
         for n, v in arrays.items()}
    o = {n: nc.dram_tensor(f"out_{n}", s, mybir.dt.float32, kind="ExternalOutput").ap() for n, s in _OUTS}
    build(nc, a, o)
    r = run_bass_kernel_spmd(nc, [arrays], core_ids=[0])
    return tuple(r.results[0][f"out_{n}"] for n, _ in _OUTS)
```

```python
import math

import numpy as np

D = 1024
KD = D // 128
NP, NB, NI = 256, 8, 8
NS = NB * NI
T = NP + NS
HA, HC, HM = 4, 8, 4
PAST, PAGE = 256, 128
NG, EPG = 4, 8
NE = NG * EPG
EPS = 1e-6
WSCALE = 64.0
BIG = 1e30
CAP = 64
NSLOT = 2 * T + CAP
SH = NSLOT // 2
TILES = ((0, 128), (128, 128), (256, 64))

CONST = {}
_at = 0
for _n, _w in (("ident", 128), ("rot", 128), ("fold_pair", 64), ("fold_heads", 64), ("m_tri", 128), ("m_samp", 64),
               ("m_pair", 64), ("m_new", 512), ("cos", T), ("sin", T), ("seg", T), ("segneg", T), ("rank_g", 4),
               ("rank_e", 8), ("map_pair", 1), ("map_heads", 1)):
    CONST[_n] = (_at, _w)
    _at += _w
NCONST = _at


def constants():
    f = np.float32
    c = np.zeros((128, NCONST), f)

    def put(name, a):
        at, w = CONST[name]
        c[:a.shape[0], at:at + w] = a

    p = np.arange(128)
    put("ident", np.eye(128, dtype=f))
    rot = np.zeros((128, 128), f)
    for m in range(128):
        if m % 64 < 32:
            rot[m + 32, m] = -1
        else:
            rot[m - 32, m] = 1
    put("rot", rot)
    put("fold_pair", (p[:, None] % 64 == np.arange(64)[None]).astype(f))
    h, t = p // 16, p % 8
    j = np.arange(64)
    put("fold_heads", ((h[:, None] == j[None] // 8) & (t[:, None] == j[None] % 8)).astype(f))
    neg = f(-BIG)
    put("m_tri", np.where(p[:, None] > p[None], neg, f(0)))
    put("m_samp", np.where((j[:, None] // 8 == j[None] // 8) & (j[:, None] <= j[None]), f(0), neg))
    put("m_pair", np.where(j[None] > p[:, None] % 64, neg, f(0)))
    b = np.arange(8)
    new = np.where((b[None, :, None] == j[None, None] // 8) & (j[None, None] % 8 <= t[:, None, None]), f(0), neg)
    put("m_new", new.reshape(128, 512).astype(f))
    pos = np.concatenate([np.arange(NP), np.tile(PAST + np.arange(NI), NB)]).astype(f)
    inv = np.exp(f(-math.log(10000.0)) * np.arange(32, dtype=f) / f(32)).astype(f)
    ang = (pos[None] * inv[p % 32][:, None]).astype(f)
    put("cos", np.cos(ang).astype(f))
    put("sin", np.sin(ang).astype(f))
    seg = np.ones((4, T), f)
    seg[:, 0] = 0
    seg[:, NP::NI] = 0
    put("seg", seg)
    put("segneg", (seg - 1) * f(BIG))
    put("rank_g", np.tile(8 - np.arange(4, dtype=f), (128, 1)))
    put("rank_e", np.tile(16 - np.arange(8, dtype=f), (128, 1)))
    put("map_pair", (p[:, None] // 64).astype(f))
    put("map_heads", (p[:, None] // 8 % 2).astype(f))
    return c


VEC = dict(mix=0, mem=16, ffn=32, final=48, head=56, subln=60, conv=61)
NVEC = 73

STREAM = [("memk0", 4), ("memv0", 4), ("memk1", 4), ("memv1", 4), ("in_a", 8), ("in_b", 6), ("out_a", 4),
          ("memq0", 4), ("memo0", 4), ("moe0", 96), ("qkv", 12), ("out_c", 4), ("memq1", 4), ("memo1", 4),
          ("moe1", 96)]
UNIT = {}
_at = 0
for _n, _w in STREAM:
    UNIT[_n] = (_at, _w)
    _at += _w
NUNITS = _at


def slot_constants():
    c = np.zeros((128, NSLOT + 128), np.float32)
    c[:, :NSLOT] = np.arange(NSLOT)
    c[:, NSLOT:] = np.arange(128)[:, None] < np.arange(128)[None]
    return c


def build(nc, a, o):
    import concourse.bass as bass
    from concourse import mybir
    from contextlib import ExitStack

    F32, F16, BF16, I32 = mybir.dt.float32, mybir.dt.float16, mybir.dt.bfloat16, mybir.dt.int32
    ALU, ACT, AX = mybir.AluOpType, mybir.ActivationFunctionType, mybir.AxisListType
    ds = bass.ds
    ctx = ExitStack()
    ctx.enter_context(nc.allow_non_contiguous_dma("small vectors and strided outputs"))

    def sb(name, shape, dt=F32):
        return ctx.enter_context(nc.sbuf_tensor(name, shape, dt))

    def sem(name):
        return ctx.enter_context(nc.semaphore(name))

    cst = sb("cst", [128, NCONST])
    maskb = sb("maskb", [128, 768], BF16)
    identb = sb("identb", [128, 128], BF16)
    ones = sb("ones", [128, 128])
    epsc = sb("epsc", [128, 2])
    vecs = sb("vecs", [NVEC, 128])
    vec = sb("vec", [128, NVEC])
    xT = sb("xT", [128, KD, T])
    xn = sb("xn", [128, KD, T])
    xh = sb("xh", [128, KD, T], F16)
    xl = sb("xl", [128, KD, T], F16)
    stg = sb("stg", [128, 2, 2048])
    wh = sb("wh", [128, 2, 2048], F16)
    wl = sb("wl", [128, 2, 2048], F16)
    memkT = sb("memkT", [128, 2, KD, 256])
    memv = sb("memv", [128, 2, 2, 1024])
    rstd = sb("rstd", [128, 2, T])
    brt = sb("brt", [128, 2, 36])
    lamv = sb("lamv", [128, 256])
    lams = sb("lams", [128, 8])
    gbias = sb("gbias", [36, 1])
    wgate = sb("wgate", [128, KD, 36])
    wrt = sb("wrt", [128, 2, KD, 36])
    roff = sb("roff", [1, NE + 1], I32)
    ptab = sb("ptab", [1, 16], I32)
    NAR = (nc.sbuf_bytes_remaining - 2048) // 4 if isinstance(nc.sbuf_bytes_remaining, int) else 22000
    arena = sb("arena", [128, NAR])
    ps = ctx.enter_context(nc.psum_tensor("ps", [128, 8, 512], F32))

    def const(name, rows=128):
        at, w = CONST[name]
        return cst[0:rows, at:at + w]

    ident = const("ident")
    m0 = CONST["m_tri"][0]

    def mask(name, rows=128):
        at, w = CONST[name]
        return maskb[0:rows, at - m0:at - m0 + w]

    def area(start):
        pos = [start]

        def take(*shape, dt=F32):
            n = int(np.prod(shape))
            words = n if dt == F32 else (n + 1) // 2
            v = arena[:, pos[0]:pos[0] + words]
            pos[0] += words
            assert pos[0] <= NAR, (pos[0], NAR)
            if dt != F32:
                v = v.bitcast(dt)
            if len(shape) == 1:
                return v
            names = " ".join("abcd"[:len(shape)])
            return v.rearrange(f"p ({names}) -> p {names}", **{"abcd"[i]: shape[i] for i in range(1, len(shape))})
        return take

    take = area(0)
    x_nat = take(3, 1024)
    mem_nat = take(2, 1024)
    mvT = take(KD, 256)
    mk_out = take(2, 1024)
    take = area(0)
    z = take(28, T)
    zq, zk, zv, zo = z[:, 0:4], z[:, 4:8], z[:, 8:12], z[:, 12:16]
    zgb, zgc, zhb = z[:, 16:20], z[:, 20:24], z[:, 24:28]
    ktok = take(3, 512)
    vtok = take(3, 512)
    dmat = take(4, 448)
    smat = take(448)
    ei = take(4, 384)
    c0 = take(2, 8, 128)
    c0T = take(8, 128)
    vw = take(8, 128)
    vwp = take(2, 128)
    cp_out = take(4, 128)
    u_p = take(4, NP + 2)
    u_s = take(4, NB, NI + 2)
    qi = take(NS)
    qn = take(NS)
    den = take(2, T)
    n0 = take(128)
    n0T = take(32)
    nT = take(36)
    nout = take(128)
    acol = take(12)
    cvt = take(4, 2)
    cvs = take(4, 16)
    m0row = take(8)
    rowsp = z[:, 20:28].rearrange("p a b -> p (a b)")
    r_out = rowsp[0:4, 0:1024]
    cout = rowsp[:, 1024:1536]
    mrow = rowsp[:, 1536:1536 + T]
    cnat = dmat.rearrange("p a b -> p (a b)")[:, 0:512]
    hsq, hstd = z[:, 0:4], z[:, 4:8]
    grow = c0T.rearrange("p a b -> p (a b)")
    g_ig = vw.rearrange("p a b -> p (a b)")[0:4, 0:T]
    g_f = grow[:, 0:T]
    g_t = grow[:, T:2 * T]
    g_lf = vw.rearrange("p a b -> p (a b)")[0:4, T:2 * T]
    g_b = vw.rearrange("p a b -> p (a b)")[0:4, 2 * T:3 * T]
    take = area(0)
    zc = take(24, T)
    vtok3 = take(3, 1024)
    kpg = take(2, 2, 1024)
    vpg = take(2, 2, 1024)
    kTh = take(KD, 256, dt=F16)
    kTl = take(KD, 256, dt=F16)
    qpad = take(8, 128)
    aTp = take(2, 512)
    aTf = aTp.rearrange("p a b -> p (a b)")
    pb, fr = aTf[:, 0:T], aTf[:, T:T + 64]
    aTh, aTl = (aTf[:, c:c + 96].bitcast(F16).rearrange("p (a b) -> p a b", a=3) for c in (384, 480))
    xhf, xlf = (x[:].rearrange("p k t -> p (k t)") for x in (xh, xl))
    vh, vl = (x[:, 0:2048].rearrange("p (a b) -> p a b", a=2) for x in (xhf, xlf))
    sideh, sidel = (x[:, 2048:2560].rearrange("p (a b) -> p a b", a=8) for x in (xhf, xlf))
    qpf = qpad.rearrange("p a b -> p (a b)")
    qph, qpl = (qpf[:, c:c + 512].bitcast(F16).rearrange("p (a b) -> p a b", a=8) for c in (0, 512))
    vnh, vnl = (vtok3[0:64, 0, c:c + 512].bitcast(F16) for c in (0, 512))
    sTb = aTf[:, 576:960].rearrange("p (a b) -> p a b", a=3)
    sst = take(4, 8)
    ktok3 = kpg.rearrange("p a b c -> p (a b c)")[:, 0:3072].rearrange("p (t c) -> p t c", t=3)
    pp = zc[:, 16:24].rearrange("p a b -> p (a b)")[:, 0:2048].rearrange("p (a b) -> p a b", a=8)
    frp = zc[:, 16:24].rearrange("p a b -> p (a b)")[:, 2048:2560]
    take = area(0)
    gbc = take(NE, T)
    take = area(0)
    xgh = take(KD, NSLOT, dt=F16)
    xgl = take(KD, NSLOT, dt=F16)
    yc = take(KD, NSLOT)
    after = area(0)
    ysh = after(5, 1024, dt=F16)
    ysl = after(5, 1024, dt=F16)
    before_yc = area(KD * NSLOT)
    xth = before_yc(3, 1024, dt=F16)
    xtl = before_yc(3, 1024, dt=F16)
    pw = before_yc(3, NSLOT)
    pk = take(3, NSLOT, dt=F16)
    gk = take(5, T, dt=F16)
    gslot = take(NSLOT)
    gcol = take(5)
    rc = take(NSLOT + 128)
    iota, before = rc[:, 0:NSLOT], rc[:, NSLOT:NSLOT + 128]
    amat = take(3, NE)
    cnt = take(NE)
    off = take(NE)
    cmax = take(1)
    e_t = take(2, T)
    r_t = take(2, T)
    a_t = take(2, T)
    b_t = take(2, T)
    cg = take(2, 2, T)
    hh = take(4, T, dt=F16)
    hl = take(4, T, dt=F16)
    gT = take(T)
    lg = take(3, 36)
    rt = take(24, 3, 8)
    gate = take(3, NE)
    take = area(NAR - 2560)
    sq = take(KD, T)

    names = """const_in tab_in vec_in small_in x_in mem_in gate_in cst_ready vec_ps vec_ev tr_ps tr_ev w_hi w_lo
        w_used w_ev in_hi in_lo sq_ready sum_ready std_ready xn_ready gate_ps gneg_ready gln_ready rows_ready
        kscaled bc_ps d_ready ei_ready s_ps s_ready ct_ps ct_ev q_ready vw_ready num_ps h_ready cn_ps c_ready
        n_ready hsq_ready hsum_ready hstd_ready osig_ready y_ready u_ready dve_chain act_chain
        dve_loop rot_ps rot_cos rot_done lam_arg lam_exp psc_ps pmax_ready pexp_ready
        pfr_ready pat_ps pat_ev ppv_ps ppv_ev kt_ps kt_ev qp_tile bq_ready k_hi v_hi v_lo at_hi bst_ps bst_ev bsc_ps bmax_ready bexp_ready
        bfr_ready bat_ps bat_ev bpv_ps bpv_ev osq_ready osum_ready ostd_ready on_ready lg_ps gexp_ready
        gsel_ready rexp_ready gate_ready rank_ps off_ready rc_in moe_done out_mem out_p out_c out_y ml_ps
        ml_ev""".split()
    S = {n: sem(n) for n in names}
    ML = [{n: sem(f"moe{l}_{n}") for n in """exp c hh hl chain loop xt_ps xt_hi xt_ev p_ready
           gs_ps gs_ready g_ps g_ev xg_ps xg_hi xg_lo b y ys_ps ys_hi ys_lo z_ps""".split()} for l in range(2)]
    w_load = [sem(f"w_load{n}") for n in range(4)]
    slot_in = [sem("slot_in0"), sem("slot_in1")]
    v_in = [sem("v_in0"), sem("v_in1")]
    c_out = [sem("c_out0"), sem("c_out1")]

    class Chain:

        def __init__(self, eng, name, loop):
            self.eng, self.sem, self.n = eng, name, 0
            self.lsem, self.base, self.per, self.i, self.k = loop, 0, 0, None, 0

        def __call__(self, ins):
            if self.i is None:
                self.n += 1
                ins.then_inc(self.sem, 1)
                self.eng.wait_ge(self.sem, self.n)
            else:
                self.k += 1
                ins.then_inc(self.lsem, 1)
                self.eng.wait_ge(self.lsem, self.i * self.per + (self.base + self.k))

        def enter(self, i, per):
            self.i, self.per, self.k = i, per, 0

        def leave(self, rounds):
            assert self.k == self.per, (self.k, self.per)
            self.base += rounds * self.per
            self.i = None

    block = ctx.enter_context(nc.Block())

    def cols(w, j0, n=256):
        return w.rearrange("(k p) n -> p k n", p=128)[:, :, ds(j0, n)]

    a_cols = a["w_in_a"][0]
    MATRIX = {"memk0": lambda j: cols(a["w_mem_k"][0], j * 256), "memv0": lambda j: cols(a["w_mem_v"][0], j * 256),
              "memk1": lambda j: cols(a["w_mem_k"][1], j * 256), "memv1": lambda j: cols(a["w_mem_v"][1], j * 256),
              "in_a": lambda j: cols(a_cols, j * 256), "in_b": lambda j: cols(a_cols, j * 256 + 2056),
              "out_a": lambda j: cols(a["w_out_a"][0], j * 256),
              "memq0": lambda j: cols(a["w_mem_q"][0], j * 256), "memo0": lambda j: cols(a["w_mem_o"][0], j * 256),
              "qkv": lambda j: cols(a["w_qkv_c"][0], j * 256), "out_c": lambda j: cols(a["w_out_c"][0], j * 256),
              "memq1": lambda j: cols(a["w_mem_q"][1], j * 256), "memo1": lambda j: cols(a["w_mem_o"][1], j * 256)}
    w_gate_f = a["w_exp_gate"].rearrange("l g e (k p) f -> (l g e) p k f", p=128)
    w_up_f = a["w_exp_up"].rearrange("l g e (k p) f -> (l g e) p k f", p=128)
    w_down_f = a["w_exp_down"].rearrange("l g e (k p) d -> (l g e k) p d", p=128)

    def stage8(s):
        return stg[:, s].rearrange("p (k n) -> p k n", k=KD)

    @block.sync
    def _(sp):
        def load(u, s, dst, src, first=False):
            kk = dst.shape[1] // 2
            for h in range(2):
                if not first:
                    sp.wait_ge(S["w_lo"], u * 2 + (h - 3))
                sp.dma_start(dst[:, kk * h:kk * h + kk], src[:, kk * h:kk * h + kk]).then_inc(w_load[2 * s + h], 16)

        def load_expert(u, e):
            load(u, 0, stage8(0), w_gate_f[e, :, :, :] if isinstance(e, int) else
                 w_gate_f[ds(e, 1), :, :, :].rearrange("a p k f -> p (a k) f"))
            load(u + 1, 1, stage8(1), w_up_f[e, :, :, :] if isinstance(e, int) else
                 w_up_f[ds(e, 1), :, :, :].rearrange("a p k f -> p (a k) f"))

        def load_down(u, row):
            for s in range(2):
                load(u + s, s, stg[:, s].rearrange("p (k n) -> p k n", k=4),
                     w_down_f[ds(row, 4), :, 512 * s:512 * s + 512].rearrange("k p n -> p k n"))

        for name, n in STREAM:
            u0 = UNIT[name][0]
            if name.startswith("moe"):
                layer = int(name[-1])
                load_expert(u0, NE * layer)
                load_expert(u0 + 2, NE * layer + 1)
                with sp.Fori(1, NE // 2) as i:
                    u = i * 6 + (u0 - 2)
                    load_expert(u, i * 2 + NE * layer)
                    load_down(u + 2, i * 4 + (NE * 2 * layer - 4))
                    load_expert(u + 4, i * 2 + (NE * layer + 1))
                load_down(u0 + n - 2, NE * 2 * layer + 2 * NE - 4)
            else:
                start = 0
                if u0 == 0:
                    for s in range(2):
                        load(s, s, stage8(s), MATRIX[name](s), first=True)
                    start = 1
                with sp.Fori(start, n // 2) as i:
                    for s in range(2):
                        load(i * 2 + (u0 + s), s, stage8(s), MATRIX[name](i * 2 + s))

    def split_hi(act, u, s):
        for h in range(2):
            c = slice(1024 * h, 1024 * h + 1024)
            act.wait_ge(w_load[2 * s + h], (u - s) * 8 + 16)
            nc.scalar.mul(wh[:, s, c], stg[:, s, c], WSCALE).then_inc(S["w_hi"], 1)

    def split_lo(dve, u, s):
        for h in range(2):
            c = slice(1024 * h, 1024 * h + 1024)
            dve.wait_ge(S["w_hi"], u * 2 + (h + 1))
            nc.vector.scalar_tensor_tensor(wl[:, s, c], stg[:, s, c], WSCALE, wh[:, s, c], ALU.mult,
                                           ALU.subtract).then_inc(S["w_lo"], 1)

    def mm3(out, s, kk, c0_, hi, lo, start, stop, width=256):
        at = kk * width + c0_
        nc.tensor.matmul(out, wh[:, s, at:at + 128], hi, start=start, stop=False)
        nc.tensor.matmul(out, wh[:, s, at:at + 128], lo, start=False, stop=False)
        return nc.tensor.matmul(out, wl[:, s, at:at + 128], hi, start=False, stop=stop)

    def gemm_pe(pe, name, g, n=T):
        u0, units = UNIT[name]
        pe.wait_ge(S["in_lo"], 2 * g + 2)

        def unit(u, s):
            pe.wait_ge(S["w_lo"], u * 2 + 2)
            pe.wait_ge(S["w_ev"], u - 1)
            for j in range(2):
                for k in range(KD):
                    last = mm3(ps[:, 2 * s + j, 0:n], s, k, 128 * j, xh[:, k, 0:n], xl[:, k, 0:n], k == 0,
                               k == KD - 1)
            last.then_inc(S["w_used"], 1)

        start = 0
        if u0 == 0:
            for s in range(2):
                pe.wait_ge(S["w_lo"], 2 * s + 2)
                for j in range(2):
                    for k in range(KD):
                        last = mm3(ps[:, 2 * s + j, 0:n], s, k, 128 * j, xh[:, k, 0:n], xl[:, k, 0:n], k == 0,
                                   k == KD - 1)
                last.then_inc(S["w_used"], 1)
            start = 1
        with pe.Fori(start, units // 2) as i:
            for s in range(2):
                unit(i * 2 + (u0 + s), s)

    def gemm_copy_act(act, name, dst, n=T):
        u0, units = UNIT[name]
        with act.Fori(0, units // 2) as i:
            for s in range(2):
                act.wait_ge(S["w_used"], i * 2 + (u0 + s + 1))
                nc.scalar.mul(dst[:, ds(i * 4 + 2 * s, 2), :], ps[:, 2 * s:2 * s + 2, 0:n],
                              1 / WSCALE).then_inc(S["w_ev"], 1)
                split_hi(act, i * 2 + (u0 + s + 2), s)

    def gemm_split_act(act, name):
        u0, units = UNIT[name]
        with act.Fori(0, units // 2) as i:
            for s in range(2):
                act.wait_ge(S["w_used"], i * 2 + (u0 + s + 1))
                split_hi(act, i * 2 + (u0 + s + 2), s)

    def gemm_split_dve(dve, name):
        u0, units = UNIT[name]
        with dve.Fori(0, units // 2) as i:
            for s in range(2):
                dve.wait_ge(S["w_used"], i * 2 + (u0 + s + 1))
                split_lo(dve, i * 2 + (u0 + s + 2), s)

    def gemm_add_dve(dve, name):
        u0, units = UNIT[name]
        with dve.Fori(0, units // 2) as i:
            for s in range(2):
                dve.wait_ge(S["w_used"], i * 2 + (u0 + s + 1))
                at = ds(i * 4 + 2 * s, 2)
                nc.vector.scalar_tensor_tensor(xT[:, at, :], ps[:, 2 * s:2 * s + 2, 0:T], 1 / WSCALE, xT[:, at, :],
                                               ALU.mult, ALU.add).then_inc(S["w_ev"], 1)
                split_lo(dve, i * 2 + (u0 + s + 2), s)

    def input_act(act, src, n=T, norm=None):
        for half in range(2):
            k = slice(4 * half, 4 * half + 4)
            if norm is not None:
                act.wait_ge(S["xn_ready"], 2 * norm + half + 1)
            nc.scalar.copy(xh[:, k, 0:n], src[:, k]).then_inc(S["in_hi"], 1)

    def input_dve(dve, g, src, n=T):
        for half in range(2):
            k = slice(4 * half, 4 * half + 4)
            dve.wait_ge(S["in_hi"], 2 * g + half + 1)
            nc.vector.tensor_sub(xl[:, k, 0:n], src[:, k], xh[:, k, 0:n]).then_inc(S["in_lo"], 1)

    def tr_pe(pe, g, srcs, n):
        if g >= 4:
            pe.wait_ge(S["tr_ev"], g - 3)
        for i, src in enumerate(srcs):
            m = src.shape[-1]
            last = nc.tensor.transpose(ps[0:m, 4 + g % 4, 128 * i:128 * i + n], src, ident[0:n, 0:n])
        last.then_inc(S["tr_ps"], 1)

    def tr_dve(dve, g, dst, m, n, cnt=4):
        dve.wait_ge(S["tr_ps"], g + 1)
        src = ps[0:m, 4 + g % 4, :].rearrange("p (a b) -> p a b", a=4)[:, 0:cnt, 0:n]
        nc.vector.tensor_copy(dst, src).then_inc(S["tr_ev"], 1)

    G_X, G_MEM, G_MKV, G_ML, G_DA, G_Y = 0, 6, 10, 26, 32, 44

    NVROW = {0: VEC["mix"], 1: VEC["mem"], 2: VEC["ffn"], 3: VEC["mix"] + 8, 4: VEC["mem"] + 8, 5: VEC["ffn"] + 8,
             6: VEC["final"]}

    def norm_act(act, n):
        nc.scalar.activation(sq[:], xT[:], ACT.Square).then_inc(S["sq_ready"], 1)
        act.wait_ge(S["sum_ready"], n + 1)
        nc.scalar.activation(rstd[:, 0, :], ps[:, 4, 0:T], ACT.Ln, bias=epsc[:, 0:1],
                             scale=1.0 / D).then_inc(S["std_ready"], 1)
        act.wait_ge(S["std_ready"], 2 * n + 1)
        nc.scalar.activation(rstd[:, 1, :], rstd[:, 0, :], ACT.Exp, scale=-0.5).then_inc(S["std_ready"], 1)

    def norm_pe(pe, n):
        pe.wait_ge(S["sq_ready"], n + 1)
        for k in range(KD):
            last = nc.tensor.matmul(ps[:, 4, 0:T], ones[:], sq[:, k, :], start=(k == 0), stop=(k == KD - 1))
        last.then_inc(S["sum_ready"], 1)

    def norm_dve(dve, link, n):
        dve.wait_ge(S["std_ready"], 2 * n + 2)
        for k in range(KD):
            v = NVROW[n] + k
            last = nc.vector.scalar_tensor_tensor(xn[:, k, :], xT[:, k, :], vec[:, v:v + 1], rstd[:, 1, :], ALU.mult,
                                                  ALU.mult)
            if k % 4 == 3:
                last.then_inc(S["xn_ready"], 1)
        dve.wait_ge(S["xn_ready"], 2 * n + 2)

    NPOOL = a["cache_k"].shape[1]
    SMALL = 16 * 3
    NVIN = 16 * (7 + 2 + 8 + 1)
    DGROUPS = ((0, 128, 0, 256), (1, 128, 256, 128), (2, 64, 384, 64))

    def mlstm_pool(pool):
        for h in range(2):
            pool.dma_start(c0[:, h], a["state_mlstm_C"][0, :, h].rearrange("b v k -> v b k")).then_inc(slot_in[h], 16)
        pool.dma_start(n0[0:32, :], a["state_mlstm_n"][0].rearrange("b h k -> (b h) k")).then_inc(S["small_in"], 16)
        pool.dma_start(m0row[0:4, :], a["state_mlstm_m"][0].rearrange("b h -> h b")).then_inc(S["small_in"], 16)
        pool.dma_start(cnat[0:16, :], a["state_conv"][0].rearrange("b w d -> (b w) d")).then_inc(S["small_in"], 16)

    def mlstm_pool_out(pool):
        pool.wait_ge(S["ml_ev"], 3)
        pool.dma_start(o["p_conv"][0, 0], cout[0:2, :]).then_inc(S["out_c"], 16)
        pool.dma_start(o["s_conv"][0].rearrange("b w d -> (b w) d"), cout[32:48, :]).then_inc(S["out_c"], 16)
        pool.wait_ge(S["rows_ready"], 1)
        pool.dma_start(o["p_m"][0].rearrange("b h -> h b"), mrow[0:4, NP - 1:NP]).then_inc(S["out_c"], 16)
        pool.dma_start(o["s_m"][0].rearrange("b h -> h b"), mrow[0:4, NP + NI - 1::NI]).then_inc(S["out_c"], 16)
        for h in range(HA):
            pool.wait_ge(S["c_ready"], h + 1)
            pool.dma_start(o["s_C"][0, :, h].rearrange("b v k -> v b k"), c0[:, h % 2]).then_inc(c_out[h % 2], 16)
            pool.dma_start(o["p_C"][0, 0, h], cp_out[:, h, :]).then_inc(S["out_c"], 16)
            if h + 2 < HA:
                pool.wait_ge(c_out[h % 2], 16)
                pool.dma_start(c0[:, h % 2], a["state_mlstm_C"][0, :, h + 2].rearrange("b v k -> v b k")
                               ).then_inc(slot_in[h % 2], 16)
        pool.wait_ge(S["n_ready"], 1)
        pool.dma_start(o["s_n"][0].rearrange("b h k -> (b h) k"), nout[0:32, :]).then_inc(S["out_c"], 16)
        pool.dma_start(o["p_n"][0, 0], nout[32:36, :]).then_inc(S["out_c"], 16)

    def mlstm_pe(pe):
        pe.wait_ge(S["gate_in"], 32)
        pe.wait_ge(S["cst_ready"], 1)
        for k in range(KD):
            last = nc.tensor.matmul(ps[0:36, 5, 0:T], wgate[:, k, :], xn[:, k, :], start=(k == 0),
                                    stop=(k == KD - 1))
        last.then_inc(S["gate_ps"], 1)
        gemm_pe(pe, "in_a", 1)
        gemm_pe(pe, "in_b", 1)
        pe.wait_ge(S["small_in"], SMALL)
        for c in range(4):
            nc.tensor.transpose(ps[:, 6, 16 * c:16 * c + 16], cnat[0:16, 128 * c:128 * c + 128], ident[0:16, 0:16])
        nc.tensor.transpose(ps[:, 6, 64:96], n0[0:32, :], ident[0:32, 0:32]).then_inc(S["ml_ps"], 1)
        pe.wait_ge(S["kscaled"], 1)
        pe.wait_ge(S["gneg_ready"], 1)
        pe.wait_ge(S["ml_ev"], 1)
        g = G_ML
        for src in (zk, zv):
            for t0, n in TILES:
                tr_pe(pe, g, [src[:, i, t0:t0 + n] for i in range(4)], 128)
                g += 1
        pe.wait_ge(S["rows_ready"], 1)
        pe.wait_ge(S["tr_ev"], G_ML + 6)
        for i, (t0, n) in enumerate(TILES):
            last = nc.tensor.transpose(ps[0:n, 3, 4 * i:4 * i + 4], r_out[:, 704 + t0:704 + t0 + n], ident[0:4, 0:4])
        last.then_inc(S["ml_ps"], 1)
        pe.wait_ge(S["u_ready"], 2)
        for c in range(4):
            nc.tensor.transpose(ps[0:2, 1, 128 * c:128 * c + 128], cvt[:, c, :], ident)
        for c in range(4):
            last = nc.tensor.transpose(ps[0:16, 2, 128 * c:128 * c + 128], cvs[:, c, :], ident)
        last.then_inc(S["ml_ps"], 1)
        pe.wait_ge(S["ml_ev"], 3)
        pe.wait_ge(S["ml_ev"], 2)
        for h in range(HA):
            if h:
                pe.wait_ge(S["ei_ready"], h)
            sel = ident[0:4, h:h + 1].to_broadcast([4, 128])
            for (tile, n, c, w) in DGROUPS:
                t0 = T - 64 if tile == 2 else 128 * tile
                mname, mw = ("m_samp", 64) if tile == 2 else ("m_tri", 128)
                nc.tensor.matmul(ps[0:n, 4, c:c + w], sel[:, 0:n], r_out[:, t0:t0 + w], start=True, stop=False)
                nc.tensor.matmul(ps[0:n, 4, c:c + mw], identb[0:n, 0:n], mask(mname, n), start=False, stop=True)
            nc.tensor.matmul(ps[:, 5, 0:384], sel, r_out[:, 320:704], start=True, stop=True).then_inc(S["bc_ps"], 1)
            if h:
                pe.wait_ge(S["s_ready"], h)
            for (tile, n, c, w) in DGROUPS:
                t0 = T - 64 if tile == 2 else 128 * tile
                last = nc.tensor.matmul(ps[0:n, 6, c:c + w], zk[:, h, t0:t0 + n], zq[:, h, t0:t0 + w], start=True,
                                        stop=True)
            last.then_inc(S["s_ps"], 1)
            pe.wait_ge(slot_in[h % 2], 16 * (h // 2 + 1))
            if h:
                pe.wait_ge(S["c_ready"], h)
            for b in range(NB):
                last = nc.tensor.transpose(ps[:, 1 + b // 4, 128 * (b % 4):128 * (b % 4) + 128], c0[:, h % 2, b, :],
                                           ident)
            last.then_inc(S["ct_ps"], 1)
            pe.wait_ge(S["s_ready"], h + 1)
            pe.wait_ge(S["ct_ev"], h + 1)
            pe.wait_ge(S["q_ready"], h + 1)
            if h:
                pe.wait_ge(S["h_ready"], h)
            for bank, left in ((7, None), (0, ones)):
                first = True
                for (tile, n, c, w) in DGROUPS:
                    t0 = T - 64 if tile == 2 else 128 * tile
                    lhs = vtok[0:n, tile, 128 * h:128 * h + 128] if left is None else ones[0:n, :]
                    nc.tensor.matmul(ps[:, bank, t0:t0 + w], lhs, smat[0:n, c:c + w], start=first, stop=False,
                                     skip_group_check=True)
                    first = False
                if left is None:
                    for b in range(NB):
                        last = nc.tensor.matmul(ps[:, bank, NP + NI * b:NP + NI * b + NI], c0T[:, b, :],
                                                qi[:, NI * b:NI * b + NI], start=False, stop=(b == NB - 1),
                                                skip_group_check=True)
                else:
                    last = nc.tensor.matmul(ps[:, bank, NP:T], ones[:], qn[:], start=False, stop=True,
                                            skip_group_check=True)
            last.then_inc(S["num_ps"], 1)
            pe.wait_ge(S["vw_ready"], h + 1)
            kt = ktok[:, :, 128 * h:128 * h + 128]
            for b in range(NB):
                nc.tensor.matmul(ps[:, 1 + b // 4, 128 * (b % 4):128 * (b % 4) + 128], vw[0:64, b, :],
                                 kt[0:64, 2, :], start=True, stop=True)
            for i in range(2):
                nc.tensor.matmul(ps[:, 3, 0:128], vwp[:, i, :], kt[:, i, :], start=(i == 0), stop=(i == 1))
            nc.tensor.matmul(ps[:, 3, 128:136], kt[0:64, 2, :], dmat[0:64, h, 384 + NI - 1:448:NI], start=True,
                             stop=True)
            for i in range(2):
                last = nc.tensor.matmul(ps[:, 3, 136:137], kt[:, i, :], dmat[:, h, 255 + 128 * i:256 + 128 * i],
                                        start=(i == 0), stop=(i == 1))
            last.then_inc(S["cn_ps"], 1)
        pe.wait_ge(S["c_ready"], HA)
        nc.tensor.transpose(ps[0:36, 3, 0:128], nT[:], ident).then_inc(S["ml_ps"], 1)
        pe.wait_ge(S["hsq_ready"], 1)
        pe.wait_ge(S["h_ready"], HA)
        pe.wait_ge(S["s_ready"], HA)
        for h in range(HA):
            last = nc.tensor.matmul(ps[:, 4 + h, 0:T], ones[:], hsq[:, h, :], start=True, stop=True)
        last.then_inc(S["hsum_ready"], 1)

    def mlstm_act(act, link):
        act.wait_ge(S["gneg_ready"], 1)
        link(nc.scalar.activation(g_t[32:36, :], g_t[32:36, :], ACT.Exp))
        nc.scalar.activation(g_t[32:36, :], g_t[32:36, :], ACT.Ln, bias=epsc[32:36, 1:2]).then_inc(S["gln_ready"], 1)
        for h in range(HA):
            act.wait_ge(S["bc_ps"], h + 1)
            if h == 0:
                act.wait_ge(S["ml_ev"], 2)
            for (tile, n, c, w) in DGROUPS:
                last = nc.scalar.activation(dmat[0:n, h, c:c + w], ps[0:n, 4, c:c + w], ACT.Exp,
                                            bias=acol[0:n, 4 * tile + h:4 * tile + h + 1])
            last.then_inc(S["d_ready"], 1)
            nc.scalar.activation(ei[:, h, :], ps[:, 5, 0:384], ACT.Exp).then_inc(S["ei_ready"], 1)
            act.wait_ge(S["ct_ps"], h + 1)
            if h:
                act.wait_ge(S["num_ps"], h)
            nc.scalar.copy(c0T.rearrange("p (a b) c -> p a (b c)", a=2), ps[:, 1:3, :]).then_inc(S["ct_ev"], 1)
        act.wait_ge(S["h_ready"], HA)
        nc.scalar.activation(hsq, xn[:, 0:4, :], ACT.Square).then_inc(S["hsq_ready"], 1)
        nc.scalar.activation(zo[:], zo[:], ACT.Tanh, scale=0.5).then_inc(S["osig_ready"], 1)
        act.wait_ge(S["hsum_ready"], 1)
        link(nc.scalar.activation(hstd, ps[:, 4:8, 0:T], ACT.Ln, bias=epsc[:, 0:1], scale=1.0 / 128))
        nc.scalar.activation(hstd, hstd, ACT.Exp, scale=-0.5).then_inc(S["hstd_ready"], 1)

    def mlstm_dve(dve, link):
        dve.wait_ge(S["w_ev"], UNIT["out_a"][0])
        nc.vector.tensor_scalar(zk[:], zk[:], 128 ** -0.5, None, ALU.mult).then_inc(S["kscaled"], 1)
        dve.wait_ge(S["gate_ps"], 1)
        nc.vector.tensor_scalar(g_ig, ps[0:4, 5, 0:T], gbias[0:4, :], None, ALU.add)
        link(nc.vector.tensor_scalar(g_f[32:36, :], ps[32:36, 5, 0:T], gbias[32:36, :], None, ALU.add))
        nc.vector.scalar_tensor_tensor(g_t[32:36, :], g_f[32:36, :], -1.0, g_f[32:36, :], ALU.mult, ALU.min
                                       ).then_inc(S["gneg_ready"], 1)
        dve.wait_ge(S["ml_ps"], 1)
        nc.vector.tensor_copy(u_s[:, :, :, 0:2], ps[:, 6, 0:64].rearrange("p (c b w) -> p c b w", c=4, w=2))
        link(nc.vector.tensor_copy(n0T[:], ps[:, 6, 64:96]))
        nc.vector.memset(u_p[:, :, 0:2], 0.0).then_inc(S["ml_ev"], 1)
        dve.wait_ge(S["ml_ev"], 1)
        nc.vector.tensor_tensor(u_p[:, :, 2:], zgc[:, :, 0:NP], zhb[:, :, 0:NP], ALU.mult)
        for c in range(4):
            last = nc.vector.tensor_tensor(u_s[:, c, :, 2:], zgc[:, c, NP:T].rearrange("p (b i) -> p b i", b=NB),
                                           zhb[:, c, NP:T].rearrange("p (b i) -> p b i", b=NB), ALU.mult)
        link(last)
        nc.vector.tensor_copy(cvt[:], u_p[:, :, NP:NP + 2]).then_inc(S["u_ready"], 1)
        nc.vector.tensor_copy(cvs.rearrange("p c (b w) -> p c b w", w=2), u_s[:, :, :, NI:NI + 2]
                              ).then_inc(S["u_ready"], 1)
        for i, (t0, n) in enumerate(TILES):
            tr_dve(dve, G_ML + i, ktok[0:n, i, :].rearrange("p (a b) -> p a b", a=4), n, 128)
        for i, (t0, n) in enumerate(TILES):
            tr_dve(dve, G_ML + 3 + i, vtok[0:n, i, :].rearrange("p (a b) -> p a b", a=4), n, 128)
        dve.wait_ge(S["gln_ready"], 1)
        link(nc.vector.scalar_tensor_tensor(g_lf, g_f[32:36, :], 0.0, g_t[32:36, :], ALU.min, ALU.subtract))
        link(nc.vector.tensor_tensor_scan(g_b, const("seg", 4), g_lf, 0.0, ALU.mult, ALU.add))
        ar = r_out[:, 704:1024]
        link(nc.vector.tensor_tensor(ar, g_ig, g_b, ALU.subtract))
        link(nc.vector.tensor_copy(g_lf, ar))
        nc.vector.tensor_scalar(g_lf[:, 0:1], ar[:, 0:1], 0.0, None, ALU.max)
        link(nc.vector.tensor_tensor(g_lf[:, NP::NI], ar[:, NP::NI], m0row[0:4, :], ALU.max))
        link(nc.vector.tensor_tensor_scan(g_ig, const("segneg", 4), g_lf, 0.0, ALU.add, ALU.max))
        link(nc.vector.tensor_tensor(mrow[0:4, :], g_b, g_ig, ALU.add))
        nc.vector.tensor_scalar(r_out[:, 0:320], g_ig, -1.0, None, ALU.mult)
        nc.vector.tensor_scalar(r_out[:, 320:640], mrow[0:4, :], -1.0, None, ALU.mult)
        nc.vector.tensor_tensor(r_out[:, 640:704].rearrange("p (b i) -> p b i", b=NB),
                                m0row[0:4, :].unsqueeze(2).to_broadcast([4, NB, NI]),
                                g_ig[:, NP:T].rearrange("p (b i) -> p b i", b=NB), ALU.subtract
                                ).then_inc(S["rows_ready"], 1)
        dve.wait_ge(S["ml_ps"], 2)
        nc.vector.tensor_copy(acol[:, 0:8], ps[:, 3, 0:8])
        nc.vector.tensor_copy(acol[0:64, 8:12], ps[0:64, 3, 8:12]).then_inc(S["ml_ev"], 1)
        dve.wait_ge(S["ml_ps"], 3)
        link(nc.vector.tensor_copy(cout[0:2, :], ps[0:2, 1, :]))
        nc.vector.tensor_copy(cout[32:48, :], ps[0:16, 2, :]).then_inc(S["ml_ev"], 1)
        dve.wait_ge(S["ml_ev"], 3)
        for h in range(HA):
            dve.wait_ge(S["s_ps"], h + 1)
            dve.wait_ge(S["d_ready"], h + 1)
            if h:
                dve.wait_ge(S["num_ps"], h)
            for (tile, n, c, w) in DGROUPS:
                last = nc.vector.tensor_tensor(smat[0:n, c:c + w], ps[0:n, 6, c:c + w], dmat[0:n, h, c:c + w],
                                               ALU.mult)
            last.then_inc(S["s_ready"], 1)
            dve.wait_ge(S["ei_ready"], h + 1)
            link(nc.vector.tensor_tensor(qi[:], zq[:, h, NP:T], ei[:, h, 320:384], ALU.mult))
            nc.vector.tensor_tensor(qn.rearrange("p (b i) -> p b i", b=NB), qi.rearrange("p (b i) -> p b i", b=NB),
                                    n0T[:, h::HA].unsqueeze(2).to_broadcast([128, NB, NI]), ALU.mult
                                    ).then_inc(S["q_ready"], 1)
            if h:
                dve.wait_ge(S["cn_ps"], h)
            hs = slice(128 * h, 128 * h + 128)
            nc.vector.tensor_tensor(vw[0:64], vtok[0:64, 2, hs].unsqueeze(1).to_broadcast([64, NB, 128]),
                                    dmat[0:64, h, 384 + NI - 1:448:NI].unsqueeze(2).to_broadcast([64, NB, 128]),
                                    ALU.mult)
            for i in range(2):
                last = nc.vector.tensor_scalar(vwp[:, i, :], vtok[:, i, hs], dmat[:, h, 255 + 128 * i:256 + 128 * i],
                                               None, ALU.mult)
            last.then_inc(S["vw_ready"], 1)
            y = xn[:, 4 + h, :]
            for j in range(3):
                v = VEC["conv"] + 4 * j + h
                for (dst, src) in ((y[:, 0:NP], u_p[:, h, j:j + NP]),
                                   (y[:, NP:T].rearrange("p (b i) -> p b i", b=NB), u_s[:, h, :, j:j + NI])):
                    if j == 0:
                        last = nc.vector.tensor_scalar(dst, src, vec[:, v:v + 1], None, ALU.mult)
                    else:
                        last = nc.vector.scalar_tensor_tensor(dst, src, vec[:, v:v + 1], dst, ALU.mult, ALU.add)
                link(last)
            link(nc.vector.tensor_tensor(y, y, zgb[:, h, :], ALU.mult))
            dve.wait_ge(S["num_ps"], h + 1)
            link(nc.vector.scalar_tensor_tensor(den[:, 0, :], ps[:, 0, 0:T], -1.0, ei[:, h, 0:T], ALU.mult, ALU.max))
            link(nc.vector.tensor_tensor(den[:, 0, :], ps[:, 0, 0:T], den[:, 0, :], ALU.max))
            link(nc.vector.reciprocal(den[:, 1, :], den[:, 0, :]))
            nc.vector.tensor_tensor(xn[:, h, :], ps[:, 7, 0:T], den[:, 1, :], ALU.mult).then_inc(S["h_ready"], 1)
            dve.wait_ge(S["cn_ps"], h + 1)
            dec = ei[:, h, 320 + NI - 1:384:NI]
            link(nc.vector.tensor_tensor(c0[:, h % 2], c0[:, h % 2], dec.unsqueeze(2).to_broadcast([128, NB, 128]),
                                         ALU.mult))
            nc.vector.tensor_tensor(c0[:, h % 2].rearrange("p (a b) c -> p a (b c)", a=2), ps[:, 1:3, :],
                                    c0[:, h % 2].rearrange("p (a b) c -> p a (b c)", a=2), ALU.add)
            nc.vector.tensor_copy(cp_out[:, h, :], ps[:, 3, 0:128])
            nc.vector.tensor_copy(nT[:, 32 + h:33 + h], ps[:, 3, 136:137])
            link(nc.vector.tensor_tensor(nT[:, h:32:HA], n0T[:, h::HA], dec, ALU.mult))
            nc.vector.tensor_tensor(nT[:, h:32:HA], nT[:, h:32:HA], ps[:, 3, 128:136], ALU.add
                                    ).then_inc(S["c_ready"], 1)
        dve.wait_ge(S["ml_ps"], 4)
        nc.vector.tensor_copy(nout[0:36, :], ps[0:36, 3, 0:128]).then_inc(S["n_ready"], 1)
        dve.wait_ge(S["osig_ready"], 1)
        link(nc.vector.tensor_scalar(zo[:], zo[:], 0.5, 0.5, ALU.mult, ALU.add))
        dve.wait_ge(S["hstd_ready"], 1)
        link(nc.vector.tensor_tensor(xn[:, 0:4, :], xn[:, 0:4, :], hstd, ALU.mult))
        for h in range(HA):
            v = VEC["head"] + h
            last = nc.vector.scalar_tensor_tensor(xn[:, h, :], xn[:, h, :], vec[:, v:v + 1], zo[:, h, :], ALU.mult,
                                                  ALU.mult)
        last.then_inc(S["y_ready"], 1)
        dve.wait_ge(S["y_ready"], 1)


    ATT = {"m0": dict(tile0=0, batch0=0, k0=32, v0=0, dma=16, layer=0),
           "d": dict(tile0=2, batch0=8, k0=96, v0=64, dma=32, layer=1),
           "m1": dict(tile0=6, batch0=16, k0=224, v0=192, dma=16, layer=1)}
    for _k, _c in ATT.items():
        diff = _k == "d"
        _c.update(diff=diff, nt=4 if diff else 2, nq=64 if diff else 128, nh=8 if diff else 4,
                  rows=128 if diff else 32, width=T if diff else 256, c=64 if diff else 32,
                  scale=64 ** -0.5 if diff else 256 ** -0.5)
    psf = ps.rearrange("p b k -> p (b k)")

    def head_of(c, blk):
        return blk if c["diff"] else blk // 2

    def prompt_pe(pe, kind):
        c = ATT[kind]
        nh, nq = c["nh"], c["nq"]

        def scores(t):
            n = c["tile0"] + t
            nk = 64 * (t + 1) if c["diff"] else 256
            if c["diff"]:
                pe.wait_ge(S["qp_tile"], t + 1)
            if n:
                pe.wait_ge(S["pexp_ready"], n)
            for h in range(nh):
                out = psf[:, 2048 + 256 * h:2048 + 256 * h + nk]
                if c["diff"]:
                    nc.tensor.matmul(out, qpad[:, h, :], zc[:, 8 + h, 0:nk], start=True, stop=False,
                                     skip_group_check=True)
                    last = nc.tensor.matmul(out[:, 64 * t:nk], identb[:], mask("m_pair"), start=False, stop=True,
                                            skip_group_check=True)
                else:
                    for dc in range(2):
                        last = nc.tensor.matmul(out, zc[:, 2 * h + dc, 128 * t:128 * t + 128],
                                                memkT[:, c["layer"], 2 * h + dc, :], start=(dc == 0), stop=(dc == 1))
            last.then_inc(S["psc_ps"], 1)

        scores(0)
        for t in range(c["nt"]):
            n = c["tile0"] + t
            nk = 64 * (t + 1) if c["diff"] else 256
            if t + 1 < c["nt"]:
                scores(t + 1)
            pe.wait_ge(S["pfr_ready"], n + 1)
            kts = [(kt, min(128, nk - 128 * kt)) for kt in range((nk + 127) // 128)]
            for kt, m in kts:
                for h in range(nh):
                    last = nc.tensor.matmul(ps[0:m, kt, nq * h:nq * h + nq], pp[:, h, 128 * kt:128 * kt + m],
                                            frp[:, nq * h:nq * h + nq], start=True, stop=True)
            last.then_inc(S["pat_ps"], 1)
            pe.wait_ge(S["pat_ev"], n + 1)
            if n:
                pe.wait_ge(S["ppv_ev"], n)
            for blk in range(8):
                h = head_of(c, blk)
                at = 1024 + nq * blk
                for kt, m in kts:
                    v = vtok3[0:m, kt, 128 * blk:128 * blk + 128] if c["diff"] else \
                        memv[0:m, c["layer"], kt, 128 * blk:128 * blk + 128]
                    last = nc.tensor.matmul(psf[:, at:at + nq], v, aTp[0:m, kt, nq * h:nq * h + nq], start=(kt == 0),
                                            stop=(kt == kts[-1][0]))
            last.then_inc(S["ppv_ps"], 1)

    def prompt_act(act, kind):
        c = ATT[kind]
        for t in range(c["nt"]):
            n = c["tile0"] + t
            nk = 64 * (t + 1) if c["diff"] else 256
            act.wait_ge(S["pmax_ready"], n + 1)
            if n:
                act.wait_ge(S["pat_ps"], n)
            for h in range(c["nh"]):
                last = nc.scalar.activation(pp[:, h, 0:nk], psf[:, 2048 + 256 * h:2048 + 256 * h + nk], ACT.Exp,
                                            bias=sst[:, 0, h:h + 1], scale=c["scale"], accum_out=sst[:, 1, h:h + 1])
            last.then_inc(S["pexp_ready"], 1)
            act.wait_ge(S["pat_ps"], n + 1)
            if n:
                act.wait_ge(S["ppv_ps"], n)
            for kt in range((nk + 127) // 128):
                m = min(128, nk - 128 * kt)
                last = nc.scalar.copy(aTp[0:m, kt, :], ps[0:m, kt, :])
            last.then_inc(S["pat_ev"], 1)

    def prompt_dve(dve, link, kind):
        c = ATT[kind]
        nh, nq = c["nh"], c["nq"]
        if c["diff"]:
            link(nc.vector.memset(qpad[:], 0.0))

        def queries(t):
            if t:
                dve.wait_ge(S["psc_ps"], c["tile0"] + t)
            for m in range(2):
                r = slice(64 * m, 64 * m + 64)
                last = nc.vector.tensor_copy(qpad[r, :, 64 * m:64 * m + 64], zc[r, 0:8, 64 * t:64 * t + 64])
            last.then_inc(S["qp_tile"], 1)

        def maxima(t):
            n = c["tile0"] + t
            nk = 64 * (t + 1) if c["diff"] else 256
            dve.wait_ge(S["psc_ps"], n + 1)
            sc = psf[:, 2048:2048 + 256 * nh].rearrange("p (h k) -> p h k", h=nh)[:, :, 0:nk]
            link(nc.vector.reduce_max(sst[:, 2, 0:nh], sc, AX.X))
            nc.vector.tensor_scalar(sst[:, 0, 0:nh], sst[:, 2, 0:nh], -c["scale"], None, ALU.mult
                                    ).then_inc(S["pmax_ready"], 1)

        if c["diff"]:
            queries(0)
        maxima(0)
        for t in range(c["nt"]):
            n = c["tile0"] + t
            if c["diff"] and t + 1 < c["nt"]:
                queries(t + 1)
            dve.wait_ge(S["pexp_ready"], n + 1)
            link(nc.vector.reciprocal(sst[:, 3, 0:nh], sst[:, 1, 0:nh]))
            if c["diff"]:
                link(nc.vector.tensor_scalar(sst[:, 3, 0:nh], sst[:, 3, 0:nh], lams[:, 5:6], None, ALU.mult))
            fold = const("fold_pair") if c["diff"] else ident
            nc.vector.tensor_tensor(frp.rearrange("p (h q) -> p h q", h=nh),
                                    fold.unsqueeze(1).to_broadcast([128, nh, nq]),
                                    sst[:, 3, 0:nh].unsqueeze(2).to_broadcast([128, nh, nq]), ALU.mult
                                    ).then_inc(S["pfr_ready"], 1)
            if t + 1 < c["nt"]:
                maxima(t + 1)
            dve.wait_ge(S["ppv_ps"], n + 1)
            nc.vector.tensor_copy(xn[:, :, nq * t:nq * t + nq],
                                  psf[:, 1024:1024 + 8 * nq].rearrange("p (b q) -> p b q", b=8)
                                  ).then_inc(S["ppv_ev"], 1)

    def batch_pool(pool, kind):
        c = ATT[kind]

        def load(b, s, cache, dst, arrived):
            if c["diff"]:
                v = cache[0].rearrange("g t h m d -> g t (h m d)") if len(cache.shape) == 6 else \
                    cache[0].rearrange("g t h d -> g t (h d)")
                for p in range(2):
                    page = pool.value_load(ptab[0:1, ds(b * 2 + p, 1)] if not isinstance(b, int) else
                                           ptab[0:1, 2 * b + p:2 * b + p + 1], min_val=0, max_val=NPOOL - 1)
                    pool.dma_start(dst[:, s, p, :], v[ds(page, 1), :, :].rearrange("g t d -> (g t) d")
                                   ).then_inc(arrived[s], 16)
            else:
                v = cache[c["layer"]].rearrange("b (t p) h d -> b p t (h d)", p=128)
                src = v[b] if isinstance(b, int) else v[ds(b, 1)].rearrange("g p t d -> (g p) t d")
                pool.dma_start(dst[:, s], src).then_inc(arrived[s], 16)

        def keys(b, s):
            load(b, s, a["cache_k"] if c["diff"] else a["cache_mem_k"], kpg, slot_in)

        def values(b, s):
            load(b, s, a["cache_v"] if c["diff"] else a["cache_mem_v"], vpg, v_in)

        for s in range(2):
            keys(s, s)
            values(s, s)
        pool.wait_ge(S["kt_ps"], 4 * c["batch0"] + 4)
        keys(2, 0)

        def step(i, s):
            pool.wait_ge(S["kt_ps"], i * 8 + 4 * (c["batch0"] + s + 2))
            keys(i * 2 + (s + 3), 1 - s)
            pool.wait_ge(S["v_lo"], i * 4 + 2 * (c["batch0"] + s + 1))
            values((i + 1) * 2 + s, s)

        with pool.Fori(0, NB // 2 - 2) as i:
            for s in range(2):
                step(i, s)
        step(NB // 2 - 2, 0)
        pool.wait_ge(S["v_lo"], 2 * (c["batch0"] + NB - 2))
        values(NB - 1, 1)

    ASCALE = 64.0

    def exact3(out, st, mv, start, stop):
        nc.tensor.matmul(out, st[0], mv[0], start=start, stop=False, skip_group_check=True)
        nc.tensor.matmul(out, st[0], mv[1], start=False, stop=False, skip_group_check=True)
        return nc.tensor.matmul(out, st[1], mv[0], start=False, stop=stop, skip_group_check=True)

    def batch_pe(pe, kind):
        c = ATT[kind]
        R, C, b0 = c["rows"], c["c"], c["batch0"]

        def turn(s, p):
            for half in range(2):
                for j in range(4):
                    at = 512 * half + 128 * j
                    last = nc.tensor.transpose(ps[:, 4 + 2 * p + half, 128 * j:128 * j + 128],
                                               kpg[:, s, p, at:at + 128], ident)
                last.then_inc(S["kt_ps"], 1)

        def step(i, s, first, final):
            n = i * 2 + (b0 + s)
            b = i * 2 + s
            nxt = 1 - s
            at = slice(8 * b, 8 * b + 8) if isinstance(b, int) else ds(b * 8, 8)
            pe.wait_ge(S["kt_ev"], n * 4 + 4)
            w = R // c["nh"]
            for h in range(c["nh"]):
                for kt in range(3 if c["diff"] else 2):
                    o = R * kt + w * h
                    keys = slice(128 * kt, 128 * kt + 128)
                    if c["diff"]:
                        q = [x[:, h, :].rearrange("p (m t) -> p m t", m=2)[:, :, at] for x in (qph, qpl)]
                        k = (kTh[:, h, keys], kTl[:, h, keys]) if kt < 2 else (sideh[:, h, :], sidel[:, h, :])
                        last = exact3(ps[0:128 if kt < 2 else 64, 3, o:o + w].rearrange("p (m t) -> p m t", m=2),
                                      k, q, True, True)
                    else:
                        for dc in range(2):
                            blk = 2 * h + dc
                            last = exact3(ps[:, 3, o:o + w], (kTh[:, blk, keys], kTl[:, blk, keys]),
                                          (sideh[:, blk, at], sidel[:, blk, at]), dc == 0, dc == 1)
            last.then_inc(S["bst_ps"], 1)
            if not final:
                pe.wait_ge(slot_in[nxt], (i + s) * c["dma"] + (c["k0"] + c["dma"]))
                turn(nxt, 0)
            pe.wait_ge(S["bst_ev"], n + 1)
            for kt in range(2):
                last = nc.tensor.transpose(ps[0:R, 0, 128 * kt:128 * kt + 128], sTb[:, kt, 0:R], ident)
            if c["diff"]:
                nc.tensor.matmul(ps[:, 0, 256:T], identb[:], mask("m_new")[:, ds(b * 64, 64)] if
                                 not isinstance(b, int) else mask("m_new")[:, 64 * b:64 * b + 64], start=True,
                                 stop=False, skip_group_check=True)
                last = nc.tensor.matmul(ps[:, 0, 256:T], sTb[0:64, 2, :], ident[0:64, 0:64], start=False, stop=True,
                                        skip_group_check=True)
            last.then_inc(S["bsc_ps"], 1)
            if not final:
                turn(nxt, 1)
            pe.wait_ge(S["bfr_ready"], n + 1)
            for kt in range(2):
                last = nc.tensor.matmul(ps[:, 1, 64 * kt:64 * kt + C], pb[0:R, 128 * kt:128 * kt + 128],
                                        fr[0:R, 0:C], start=True, stop=True)
            if c["diff"]:
                last = nc.tensor.matmul(ps[0:64, 1, 128:192], pb[:, 256:T], fr, start=True, stop=True)
            last.then_inc(S["bat_ps"], 1)
            pe.wait_ge(S["v_lo"], n * 2 + 2)
            pe.wait_ge(S["bat_ev"], n + 1)
            if not first:
                pe.wait_ge(S["bpv_ev"], n)
            for blk in range(8):
                q = slice(8 * head_of(c, blk), 8 * head_of(c, blk) + 8)
                f = slice(128 * blk, 128 * blk + 128)
                for kt in range(2):
                    last = exact3(ps[:, 2, 8 * blk:8 * blk + 8], (vh[:, kt, f], vl[:, kt, f]),
                                  (aTh[:, kt, q], aTl[:, kt, q]), kt == 0, kt == 1 and not c["diff"])
                if c["diff"]:
                    last = exact3(ps[:, 2, 8 * blk:8 * blk + 8], (vnh[:, f], vnl[:, f]),
                                  (aTh[0:64, 2, q], aTl[0:64, 2, q]), False, True)
            last.then_inc(S["bpv_ps"], 1)

        pe.wait_ge(S["bq_ready"], (0, 8, 16).index(b0) + 1)
        pe.wait_ge(slot_in[0], c["k0"] + c["dma"])
        turn(0, 0)
        turn(0, 1)
        start = 0
        if kind == "m0":
            step(0, 0, True, False)
            step(0, 1, False, False)
            start = 1
        with pe.Fori(start, NB // 2 - 1) as i:
            for s in range(2):
                step(i, s, False, False)
        step(NB // 2 - 1, 0, False, False)
        step(NB // 2 - 1, 1, False, True)

    def key_block(p, half):
        at = (slice(None), slice(4 * half, 4 * half + 4), slice(128 * p, 128 * p + 128))
        return at, ps[:, 4 + 2 * p + half, :].rearrange("p (a b) -> p a b", a=4)

    def batch_act(act, kind):
        c = ATT[kind]
        R, C, b0, W = c["rows"], c["c"], c["batch0"], c["width"]

        def keys_hi(n, p, half):
            at, src = key_block(p, half)
            act.wait_ge(S["kt_ps"], n * 4 + (2 * p + half + 1))
            nc.scalar.copy(kTh[at], src).then_inc(S["k_hi"], 1)

        def values_hi(s):
            for kt in range(2):
                nc.scalar.copy(vh[:, kt, :], vpg[:, s, kt, :]).then_inc(S["v_hi"], 1)

        def step(i, s, final):
            n = i * 2 + (b0 + s)
            if not final:
                keys_hi(n + 1, 0, 0)
                keys_hi(n + 1, 0, 1)
            act.wait_ge(S["bmax_ready"], n + 1)
            nc.scalar.activation(pb[0:R, 0:W], ps[0:R, 0, 0:W], ACT.Exp, bias=sst[0:R, 0, 0:1],
                                 scale=c["scale"], accum_out=sst[0:R, 1, 0:1]).then_inc(S["bexp_ready"], 1)
            if not final:
                keys_hi(n + 1, 1, 0)
                keys_hi(n + 1, 1, 1)
            act.wait_ge(S["bat_ps"], n + 1)
            if c["diff"]:
                nc.scalar.copy(aTh[0:64, 2, :], ps[0:64, 1, 128:192])
            nc.scalar.copy(aTh[:, 0:2, 0:C], ps[:, 1, 0:128].rearrange("p (t c) -> p t c", t=2)[:, :, 0:C]
                           ).then_inc(S["at_hi"], 1)
            if not final:
                act.wait_ge(v_in[1 - s], (i + s) * c["dma"] + (c["v0"] + c["dma"]))
                act.wait_ge(S["bpv_ps"], n + 1)
                values_hi(1 - s)

        act.wait_ge(v_in[0], c["v0"] + c["dma"])
        values_hi(0)
        for p in range(2):
            for half in range(2):
                keys_hi(b0, p, half)
        with act.Fori(0, NB // 2 - 1) as i:
            for s in range(2):
                step(i, s, False)
        step(NB // 2 - 1, 0, False)
        step(NB // 2 - 1, 1, True)

    def batch_dve(dve, link, kind):
        c = ATT[kind]
        V = nc.vector
        R, C, b0, W = c["rows"], c["c"], c["batch0"], c["width"]

        def keys_lo(n, p, half):
            at, src = key_block(p, half)
            dve.wait_ge(S["k_hi"], n * 4 + (2 * p + half + 1))
            V.tensor_tensor(kTl[at], src, kTh[at], ALU.subtract).then_inc(S["kt_ev"], 1)

        def values_lo(n, s, kt):
            dve.wait_ge(S["v_hi"], n * 2 + (kt + 1))
            V.tensor_tensor(vl[:, kt, :], vpg[:, s, kt, :], vh[:, kt, :], ALU.subtract).then_inc(S["v_lo"], 1)

        def step(i, s, final):
            n = i * 2 + (b0 + s)
            b = i * 2 + s
            dve.wait_ge(S["bst_ps"], n + 1)
            if c["diff"]:
                V.tensor_copy(sTb[0:64, 2, :], ps[0:64, 3, 256:384])
            V.tensor_copy(sTb[:, 0:2, 0:R], ps[:, 3, 0:2 * R].rearrange("p (a b) -> p a b", a=2)
                          ).then_inc(S["bst_ev"], 1)
            values_lo(n, s, 0)
            if not final:
                keys_lo(n + 1, 0, 0)
            dve.wait_ge(S["bsc_ps"], n + 1)
            link(V.reduce_max(sst[0:R, 2, 0:1], ps[0:R, 0, 0:W], AX.X))
            V.tensor_scalar(sst[0:R, 0, 0:1], sst[0:R, 2, 0:1], -c["scale"], None, ALU.mult
                            ).then_inc(S["bmax_ready"], 1)
            if not final:
                keys_lo(n + 1, 0, 1)
            dve.wait_ge(S["bexp_ready"], n + 1)
            link(V.reciprocal(sst[0:R, 3, 0:1], sst[0:R, 1, 0:1]))
            if c["diff"]:
                link(V.tensor_tensor(sst[:, 3, 0:1], sst[:, 3, 0:1], lams[:, 6:7], ALU.mult))
            fold = const("fold_heads") if c["diff"] else ident[0:32, 0:32]
            V.tensor_scalar(fr[0:R, 0:C], fold, sst[0:R, 3, 0:1], ASCALE, ALU.mult, ALU.mult
                            ).then_inc(S["bfr_ready"], 1)
            values_lo(n, s, 1)
            if not final:
                keys_lo(n + 1, 1, 0)
                keys_lo(n + 1, 1, 1)
            dve.wait_ge(S["at_hi"], n + 1)
            if c["diff"]:
                V.tensor_tensor(aTl[0:64, 2, :], ps[0:64, 1, 128:192], aTh[0:64, 2, :], ALU.subtract)
            V.tensor_tensor(aTl[:, 0:2, 0:C], ps[:, 1, 0:128].rearrange("p (t c) -> p t c", t=2)[:, :, 0:C],
                            aTh[:, 0:2, 0:C], ALU.subtract).then_inc(S["bat_ev"], 1)
            dve.wait_ge(S["bpv_ps"], n + 1)
            at = slice(NP + 8 * b, NP + 8 * b + 8) if isinstance(b, int) else ds(b * 8 + NP, 8)
            V.tensor_scalar(xn[:, :, at], ps[:, 2, 0:64].rearrange("p (b q) -> p b q", b=8), 1 / ASCALE, None,
                            ALU.mult).then_inc(S["bpv_ev"], 1)

        dve.wait_ge(S["ppv_ps"], c["tile0"] + c["nt"])
        side = zc[:, 8:16, NP:T] if c["diff"] else zc[:, 0:8, NP:T]
        link(V.tensor_copy(sideh, side))
        last = V.tensor_tensor(sidel, side, sideh, ALU.subtract)
        if c["diff"]:
            link(V.memset(qpad[:], 0.0))
            for m in range(2):
                r = slice(64 * m, 64 * m + 64)
                t = slice(64 * m, 64 * m + 64)
                link(V.tensor_copy(qph[r, :, t], zc[r, 0:8, NP:T]))
                V.tensor_tensor(qpl[r, :, t], zc[r, 0:8, NP:T], qph[r, :, t], ALU.subtract)
            dve.wait_ge(S["out_p"], 64)
            link(V.tensor_copy(vnh, vtok3[0:64, 2, :]))
            last = V.tensor_tensor(vnl, vtok3[0:64, 2, :], vnh, ALU.subtract)
        last.then_inc(S["bq_ready"], 1)
        for p in range(2):
            for half in range(2):
                keys_lo(b0, p, half)
        rounds = NB // 2 - 1
        with dve.Fori(0, rounds) as i:
            link.enter(i, 6 if c["diff"] else 4)
            for s in range(2):
                step(i, s, False)
        link.leave(rounds)
        step(rounds, 0, False)
        step(rounds, 1, True)

    def rope_pe(pe):
        pe.wait_ge(S["w_ev"], UNIT["out_c"][0])
        for blk in range(16):
            if blk >= 4:
                pe.wait_ge(S["rot_done"], blk - 3)
            nc.tensor.matmul(ps[:, blk % 4, 0:T], const("rot"), zc[:, blk, :], start=True, stop=True
                             ).then_inc(S["rot_ps"], 1)
        g = G_DA
        for src in (8, 16):
            for t0, n in TILES:
                for half in range(2):
                    if src == 8:
                        pe.wait_ge(S["rot_done"], 16)
                    tr_pe(pe, g, [zc[:, src + 4 * half + j, t0:t0 + n] for j in range(4)], 128)
                    g += 1

    def rope_pool(pool):
        for blk in range(16):
            pool.wait_ge(S["rot_ps"], blk + 1)
            nc.gpsimd.tensor_tensor(zc[:, blk, :], zc[:, blk, :], const("cos"), ALU.mult
                                    ).then_inc(S["rot_cos"], 1)

    def rope_dve(dve, link):
        for blk in range(16):
            dve.wait_ge(S["rot_ps"], blk + 1)
            link(nc.vector.tensor_tensor(rstd[:, blk % 2, :], ps[:, blk % 4, 0:T], const("sin"), ALU.mult))
            dve.wait_ge(S["rot_cos"], blk + 1)
            nc.vector.tensor_tensor(zc[:, blk, :], zc[:, blk, :], rstd[:, blk % 2, :], ALU.add
                                    ).then_inc(S["rot_done"], 1)
        lv = lamv.rearrange("p (a d) -> p a d", a=4)
        dve.wait_ge(S["rot_done"], 16)
        link(nc.vector.tensor_tensor(rstd[:, 0, 0:128].rearrange("p (a d) -> p a d", a=2), lv[:, 0::2, :],
                                     lv[:, 1::2, :], ALU.mult))
        nc.vector.reduce_sum(lams[:, 0:2], rstd[:, 0, 0:128].rearrange("p (a d) -> p a d", a=2), AX.X
                             ).then_inc(S["lam_arg"], 1)
        dve.wait_ge(S["lam_exp"], 1)
        lam_init = 0.8 - 0.6 * math.exp(-0.3)
        link(nc.vector.tensor_tensor(lams[:, 4:5], lams[:, 3:4], lams[:, 2:3], ALU.subtract))
        link(nc.vector.tensor_scalar(lams[:, 4:5], lams[:, 4:5], -(1.0 + lam_init), None, ALU.add))
        for col, name in ((5, "map_pair"), (6, "map_heads")):
            link(nc.vector.tensor_scalar(lams[:, col:col + 1], const(name), lams[:, 4:5], 1.0, ALU.mult, ALU.add))
        g = G_DA
        for dst in (ktok3, vtok3):
            for i, (t0, n) in enumerate(TILES):
                for half in range(2):
                    tr_dve(dve, g, dst[0:n, i, 512 * half:512 * half + 512].rearrange("p (a b) -> p a b", a=4), n,
                           128)
                    g += 1

    def subln_pe(pe):
        pe.wait_ge(S["osq_ready"], 1)
        pe.wait_ge(S["ppv_ev"], ATT["d"]["tile0"] + 4)
        pe.wait_ge(S["bpv_ev"], ATT["d"]["batch0"] + 8)
        for h in range(HC):
            last = nc.tensor.matmul(ps[:, h, 0:T], ones[:], sq[:, h, :], start=True, stop=True)
        last.then_inc(S["osum_ready"], 1)

    def subln_act(act, link):
        act.wait_ge(S["bpv_ev"], ATT["d"]["batch0"] + 8)
        nc.scalar.activation(sq[:], xn[:], ACT.Square).then_inc(S["osq_ready"], 1)
        act.wait_ge(S["osum_ready"], 1)
        for half in range(2):
            h = slice(4 * half, 4 * half + 4)
            link(nc.scalar.activation(sq[:, h], ps[:, h, 0:T], ACT.Ln, bias=epsc[:, 0:1], scale=1.0 / 128))
            nc.scalar.activation(sq[:, h], sq[:, h], ACT.Exp, scale=-0.5).then_inc(S["ostd_ready"], 1)

    def subln_dve(dve, link):
        lam_init = 0.8 - 0.6 * math.exp(-0.3)
        v = VEC["subln"]
        link(nc.vector.tensor_scalar(lams[:, 7:8], vec[:, v:v + 1], 1.0 - lam_init, None, ALU.mult))
        for half in range(2):
            h = slice(4 * half, 4 * half + 4)
            dve.wait_ge(S["ostd_ready"], half + 1)
            last = nc.vector.scalar_tensor_tensor(xn[:, h], xn[:, h], lams[:, 7:8], sq[:, h], ALU.mult, ALU.mult)
        last.then_inc(S["on_ready"], 1)
        dve.wait_ge(S["on_ready"], 1)

    def route_pe(pe, l):
        for i, (t0, n) in enumerate(TILES):
            for k in range(KD):
                last = nc.tensor.matmul(ps[0:n, 5, 36 * i:36 * i + 36], xn[:, k, t0:t0 + n], wrt[:, l, k, :],
                                        start=(k == 0), stop=(k == KD - 1))
        last.then_inc(S["lg_ps"], 1)
        pe.wait_ge(S["gate_ready"], l + 1)
        pe.wait_ge(S["rc_in"], 16 * (l + 1))
        for i, (t0, n) in enumerate(TILES):
            for j in range(i):
                nc.tensor.matmul(ps[0:n, 7, NE * i:NE * i + NE], ones[:, 0:n], amat[:, j, :], start=(j == 0),
                                 stop=False)
            nc.tensor.matmul(ps[0:n, 7, NE * i:NE * i + NE], before[0:n, 0:n], amat[0:n, i, :], start=(i == 0),
                             stop=True)
        for i, (t0, n) in enumerate(TILES):
            last = nc.tensor.matmul(ps[:, 7, 96:128], ones[0:n, :], amat[0:n, i, :], start=(i == 0), stop=(i == 2))
        last.then_inc(S["rank_ps"], 1)

    def route_act(act, l):
        act.wait_ge(S["gsel_ready"], l + 1)
        nc.scalar.activation(rt[:, 4, :, 0:4], rt[:, 3, :, 0:4], ACT.Exp).then_inc(S["gexp_ready"], 1)
        act.wait_ge(S["rexp_ready"], 2 * l + 1)
        nc.scalar.activation(rt[:, 15, :, 0:1], rt[:, 14, :, 0:1], ACT.Exp).then_inc(S["rexp_ready"], 1)

    def route_dve(dve, link, l):
        V = nc.vector

        def bc(x, w):
            return x.to_broadcast([128, 3, w])

        link(V.memset(lg[:, 2, :], 0.0))
        dve.wait_ge(S["lg_ps"], l + 1)
        V.tensor_tensor(lg[:, 0:2, :], ps[:, 5, 0:72].rearrange("p (t n) -> p t n", t=2),
                        brt[:, l, :].unsqueeze(1).to_broadcast([128, 2, 36]), ALU.add)
        link(V.tensor_tensor(lg[0:64, 2, :], ps[0:64, 5, 72:108], brt[0:64, l, :], ALU.add))
        gl, el = lg[:, :, 0:4], lg[:, :, 4:36].rearrange("p t (g e) -> p t g e", g=4)

        def first_max(x, w, rank, at, oh):
            link(V.reduce_max(rt[:, at, :, 0:1], x, AX.X))
            link(V.tensor_tensor(rt[:, at + 1, :, 0:w], x, bc(rt[:, at, :, 0:1], w), ALU.is_equal))
            link(V.tensor_tensor(rt[:, at + 1, :, 0:w], rt[:, at + 1, :, 0:w],
                                 const(rank).unsqueeze(1).to_broadcast([128, 3, w]), ALU.mult))
            link(V.reduce_max(rt[:, at, :, 1:2], rt[:, at + 1, :, 0:w], AX.X))
            link(V.tensor_tensor(oh, rt[:, at + 1, :, 0:w], bc(rt[:, at, :, 1:2], w), ALU.is_equal))

        ohg = rt[:, 2, :, 0:4]
        first_max(gl, 4, "rank_g", 0, ohg)
        V.tensor_tensor(rt[:, 3, :, 0:4], gl, bc(rt[:, 0, :, 0:1], 4), ALU.subtract).then_inc(S["gsel_ready"], 1)
        prod = rt[:, 16:20].rearrange("p a t e -> p (a t e)").rearrange("p (t g e) -> p t g e", t=3, g=4)
        link(V.tensor_tensor(prod, el, ohg.unsqueeze(3).to_broadcast([128, 3, 4, 8]), ALU.mult))
        es, oh1, es2, oh2 = rt[:, 5], rt[:, 8], rt[:, 9], rt[:, 12]
        link(V.tensor_tensor(es, prod[:, :, 0, :], prod[:, :, 1, :], ALU.add))
        link(V.tensor_tensor(es, es, prod[:, :, 2, :], ALU.add))
        link(V.tensor_tensor(es, es, prod[:, :, 3, :], ALU.add))
        first_max(es, 8, "rank_e", 6, oh1)
        link(V.tensor_scalar(es2, oh1, -BIG, None, ALU.mult))
        link(V.tensor_tensor(es2, es2, es, ALU.add))
        first_max(es2, 8, "rank_e", 10, oh2)
        V.tensor_tensor(rt[:, 14, :, 0:1], rt[:, 10, :, 0:1], rt[:, 6, :, 0:1], ALU.subtract
                        ).then_inc(S["rexp_ready"], 1)
        dve.wait_ge(S["gexp_ready"], l + 1)
        link(V.reduce_sum(rt[:, 13, :, 0:1], rt[:, 4, :, 0:4], AX.X))
        dve.wait_ge(S["rexp_ready"], 2 * l + 2)
        link(V.tensor_scalar(rt[:, 13, :, 1:2], rt[:, 15, :, 0:1], 1.0, None, ALU.add))
        link(V.tensor_tensor(rt[:, 13, :, 2:3], rt[:, 13, :, 0:1], rt[:, 13, :, 1:2], ALU.mult))
        link(V.reciprocal(rt[:, 13, :, 3:4], rt[:, 13, :, 2:3]))
        ew, both = rt[:, 20], rt[:, 21]
        link(V.tensor_tensor(ew, oh2, bc(rt[:, 15, :, 0:1], 8), ALU.mult))
        link(V.tensor_tensor(ew, ew, oh1, ALU.add))
        V.tensor_tensor(rt[:, 13, :, 4:5], rt[:, 13, :, 3:4], rt[:, 15, :, 0:1], ALU.mult)
        V.tensor_tensor(both, oh1, oh2, ALU.add)
        link(V.tensor_tensor(ew, ew, bc(rt[:, 13, :, 3:4], 8), ALU.mult))
        for dst, src in ((gate, ew), (amat, both)):
            for i in range(3):
                last = V.tensor_tensor(dst[:, i, :].rearrange("p (g e) -> p g e", g=4),
                                       ohg[:, i, :].unsqueeze(2).to_broadcast([128, 4, 8]),
                                       src[:, i, :].unsqueeze(1).to_broadcast([128, 4, 8]), ALU.mult)
        last.then_inc(S["gate_ready"], 1)
        dve.wait_ge(S["rank_ps"], l + 1)
        link(V.tensor_copy(cnt, ps[:, 7, 96:128]))
        link(V.tensor_tensor_scan(off, ones[:, 0:NE], cnt, 0.0, ALU.mult, ALU.add))
        link(V.tensor_tensor(off, off, cnt, ALU.subtract))
        pos = lg[:, :, 0:NE]
        link(V.memset(lg[:, 2, :], 0.0))
        V.tensor_tensor(pos[:, 0:2, :], ps[:, 7, 0:64].rearrange("p (t n) -> p t n", t=2),
                        off.unsqueeze(1).to_broadcast([128, 2, NE]), ALU.add)
        link(V.tensor_tensor(pos[0:64, 2, :], ps[0:64, 7, 64:96], off[0:64, :], ALU.add))
        pos4 = pos.rearrange("p t (g e) -> p t g e", g=4)
        link(V.tensor_tensor(prod, pos4, ohg.unsqueeze(3).to_broadcast([128, 3, 4, 8]), ALU.mult))
        for g in range(1, 4):
            link(V.tensor_tensor(es, prod[:, :, 0, :] if g == 1 else es, prod[:, :, g, :], ALU.add))
        for oh, at in ((oh1, 5), (oh2, 6)):
            link(V.tensor_tensor(both, es, oh, ALU.mult))
            link(V.reduce_sum(rt[:, 13, :, at:at + 1], both, AX.X))
        link(V.reduce_max(cmax, cnt, AX.X))
        V.tensor_copy(roff[0:1, 0:NE], off[0:1, :])
        V.tensor_scalar(roff[0:1, NE:NE + 1], cmax[0:1, :], CAP + 0.5, None, ALU.is_le).then_inc(S["off_ready"], 1)

    def moe_all_pe(pe, l):
        M = ML[l]
        u0 = UNIT[f"moe{l}"][0]
        for i, (t0, n) in enumerate(TILES):
            last = nc.tensor.transpose(ps[0:32, 6, t0:t0 + n], gate[0:n, i, :], ident[0:n, 0:n])
        last.then_inc(M["g_ps"], 1)
        pe.wait_ge(M["g_ev"], 1)
        for e in range(NE):
            if e >= 4:
                pe.wait_ge(M["gs_ready"], e - 3)
            nc.tensor.matmul(ps[:, 4 + e % 4, 0:T], ident[0:32, e:e + 1].to_broadcast([32, 128]), gT[0:32, :],
                             start=True, stop=True).then_inc(M["gs_ps"], 1)

        def up(u, s, bank):
            pe.wait_ge(S["w_lo"], u * 2 + 2)
            for j in range(2):
                for k in range(KD):
                    last = mm3(ps[:, bank + j, 0:T], s, k, 128 * j, xh[:, k, :], xl[:, k, :], k == 0, k == KD - 1)
            last.then_inc(S["w_used"], 1)

        def down(u, s, bank):
            pe.wait_ge(S["w_lo"], u * 2 + 2)
            for j in range(4):
                for k in range(4):
                    last = mm3(ps[:, bank + j, 0:T], s, k, 128 * j, hh[:, k, :], hl[:, k, :], k == 0, k == 3, 512)
            last.then_inc(S["w_used"], 1)

        pe.wait_ge(S["w_ev"], u0)
        up(u0, 0, 0)
        up(u0 + 1, 1, 2)
        pe.wait_ge(M["gs_ready"], NE)
        up(u0 + 2, 0, 4)
        up(u0 + 3, 1, 6)
        with pe.Fori(1, NE // 2) as i:
            u = i * 6 + (u0 - 2)
            pe.wait_ge(S["w_ev"], u - 2)
            up(u, 0, 0)
            up(u + 1, 1, 2)
            pe.wait_ge(S["w_ev"], u)
            pe.wait_ge(M["hl"], i * 2)
            down(u + 2, 0, 4)
            pe.wait_ge(S["w_ev"], u + 2)
            down(u + 3, 1, 0)
            pe.wait_ge(S["w_ev"], u + 3)
            up(u + 4, 0, 4)
            up(u + 5, 1, 6)
        u = u0 + 94
        pe.wait_ge(S["w_ev"], u)
        pe.wait_ge(M["hl"], NE)
        down(u, 0, 4)
        down(u + 1, 1, 0)

    def moe_all_act(act, l, last_layer):
        M = ML[l]
        u0 = UNIT[f"moe{l}"][0]

        def hi(u, s):
            act.wait_ge(S["w_used"], u + 1)
            split_hi(act, u + 2, s)

        def sig(u, bank, prev):
            if prev is not None:
                act.wait_ge(S["w_ev"], prev + 1)
            nc.scalar.activation(e_t, ps[:, bank:bank + 2, 0:T], ACT.Exp, scale=-1.0 / WSCALE
                                 ).then_inc(M["exp"], 1)

        def hid(n, j):
            act.wait_ge(M["c"], n + 1)
            nc.scalar.copy(hh[:, 2 * j:2 * j + 2, :], cg[:, j]).then_inc(M["hh"], 1)

        n0_ = 0
        for e in range(NE):
            act.wait_ge(M["gs_ps"], e + 1)
            nc.scalar.copy(gbc[:, e, :], ps[:, 4 + e % 4, 0:T]).then_inc(M["gs_ready"], 1)
        hi(u0, 0)
        sig(u0, 0, None)
        hi(u0 + 1, 1)
        hid(n0_, 0)
        hi(u0 + 2, 0)
        sig(u0 + 2, 4, u0 + 1)
        hi(u0 + 3, 1)
        hid(n0_ + 1, 1)
        with act.Fori(1, NE // 2) as i:
            u = i * 6 + (u0 - 2)
            n = i * 2 + n0_
            hi(u, 0)
            sig(u, 0, u - 1)
            hi(u + 1, 1)
            hi(u + 2, 0)
            hi(u + 3, 1)
            hid(n, 0)
            hi(u + 4, 0)
            sig(u + 4, 4, u + 1)
            hi(u + 5, 1)
            hid(n + 1, 1)
        if not last_layer:
            hi(u0 + 94, 0)
            hi(u0 + 95, 1)

    def moe_all_pool(pool, l):
        M = ML[l]
        def gated(u, n, e, j):
            pool.wait_ge(S["w_ev"], u + 1)
            if not isinstance(n, int) or n >= 2:
                pool.wait_ge(M["hl"], n - 1)
            for c in range(2):
                g = gbc[:, e, :] if isinstance(e, int) else gbc[:, ds(e, 1), :].rearrange("p a t -> p (a t)")
                last = nc.gpsimd.tensor_tensor(cg[:, j, c, :], b_t[:, c, :], g, ALU.mult)
            last.then_inc(M["c"], 1)

        u0 = UNIT[f"moe{l}"][0]
        pool.wait_ge(M["gs_ready"], NE)
        gated(u0 + 1, 0, 0, 0)
        gated(u0 + 3, 1, 1, 1)
        with pool.Fori(1, NE // 2) as i:
            u = i * 6 + (u0 - 2)
            gated(u + 1, i * 2, i * 2, 0)
            gated(u + 5, i * 2 + 1, i * 2 + 1, 1)

    def moe_all_dve(dve, l, last_layer):
        M = ML[l]
        link = Chain(dve, M["chain"], M["loop"])
        u0 = UNIT[f"moe{l}"][0]

        def lo(u, s):
            dve.wait_ge(S["w_used"], u + 1)
            split_lo(dve, u + 2, s)

        def act_fn(u, n, bank, nfirst=False):
            dve.wait_ge(M["exp"], n + 1)
            link(nc.vector.tensor_scalar(r_t, e_t, 1.0, None, ALU.add))
            link(nc.vector.reciprocal(r_t, r_t))
            nc.vector.scalar_tensor_tensor(a_t, ps[:, bank:bank + 2, 0:T], 1 / WSCALE, r_t, ALU.mult, ALU.mult
                                           ).then_inc(S["w_ev"], 1)
            dve.wait_ge(S["w_ev"], u + 1)
            if not nfirst:
                dve.wait_ge(M["c"], n)
            nc.vector.scalar_tensor_tensor(b_t, ps[:, bank + 2:bank + 4, 0:T], 1 / WSCALE, a_t, ALU.mult, ALU.mult
                                           ).then_inc(S["w_ev"], 1)

        def low(n, j):
            dve.wait_ge(M["hh"], n + 1)
            nc.vector.tensor_tensor(hl[:, 2 * j:2 * j + 2, :], cg[:, j], hh[:, 2 * j:2 * j + 2, :], ALU.subtract
                                    ).then_inc(M["hl"], 1)

        def add(half, bank):
            x = xT[:, 4 * half:4 * half + 4, :]
            nc.vector.scalar_tensor_tensor(x, ps[:, bank:bank + 4, 0:T], 1 / WSCALE, x, ALU.mult, ALU.add
                                           ).then_inc(S["w_ev"], 1)

        n0_ = 0
        dve.wait_ge(M["g_ps"], 1)
        nc.vector.tensor_copy(gT[0:32, :], ps[0:32, 6, 0:T]).then_inc(M["g_ev"], 1)
        lo(u0, 0)
        lo(u0 + 1, 1)
        act_fn(u0, n0_, 0, nfirst=True)
        low(n0_, 0)
        lo(u0 + 2, 0)
        lo(u0 + 3, 1)
        act_fn(u0 + 2, n0_ + 1, 4)
        low(n0_ + 1, 1)
        with dve.Fori(1, NE // 2) as i:
            link.enter(i - 1, 4)
            u = i * 6 + (u0 - 2)
            n = i * 2 + n0_
            lo(u, 0)
            lo(u + 1, 1)
            act_fn(u, n, 0)
            lo(u + 2, 0)
            add(0, 4)
            lo(u + 3, 1)
            add(1, 0)
            low(n, 0)
            lo(u + 4, 0)
            lo(u + 5, 1)
            act_fn(u + 4, n + 1, 4)
            low(n + 1, 1)
        link.leave(NE // 2 - 1)
        if last_layer:
            dve.wait_ge(S["w_used"], u0 + 95)
            add(0, 4)
            dve.wait_ge(S["w_used"], u0 + 96)
            add(1, 0)
        else:
            lo(u0 + 94, 0)
            add(0, 4)
            lo(u0 + 95, 1)
            add(1, 0)
        dve.wait_ge(S["w_ev"], u0 + 96)
        nc.vector.memset(gT[0:1, 0:1], 0.0).then_inc(S["moe_done"], 1)

    def pack_pe(pe, l):
        M = ML[l]
        pe.wait_ge(S["xn_ready"], 6 * l + 6)
        for g in range(6):
            i, half = g // 2, g % 2
            t0, n = TILES[i]
            if g >= 4:
                pe.wait_ge(M["xt_ev"], g - 3)
            for j in range(4):
                last = nc.tensor.transpose(ps[0:n, g % 4, 128 * j:128 * j + 128], xn[:, 4 * half + j, t0:t0 + n],
                                           ident)
            last.then_inc(M["xt_ps"], 1)
        pe.wait_ge(M["p_ready"], 1)
        for st in range(5):
            for i, (t0, n) in enumerate(TILES):
                last = nc.tensor.matmul(ps[:, 4, st:st + 1], pw[0:n, i, 128 * st:128 * st + 128], ones[0:n, 0:1],
                                        start=(i == 0), stop=(i == 2))
        last.then_inc(M["gs_ps"], 1)
        for st in range(5):
            if st >= 2:
                pe.wait_ge(M["g_ev"], st - 1)
            for i, (t0, n) in enumerate(TILES):
                last = nc.tensor.matmul(ps[:, 6 + st % 2, t0:t0 + n], pk[0:n, i, 128 * st:128 * st + 128],
                                        identb[0:n, 0:n], start=True, stop=True)
            last.then_inc(M["g_ps"], 1)
        pe.wait_ge(M["xt_ev"], 6)
        pe.wait_ge(M["g_ev"], 5)
        pe.wait_ge(M["gs_ready"], 1)
        for g in range(32):
            k, half, part = g // 4, (g // 2) % 2, g % 2
            if g >= 8:
                pe.wait_ge(M["xg_hi"] if part == 0 else M["xg_lo"], (g - 8) // 2 + 1)
            src = (xth, xtl)[part]
            for i, (t0, n) in enumerate(TILES):
                last = nc.tensor.matmul(ps[:, g % 8, 0:SH], src[0:n, i, 128 * k:128 * k + 128],
                                        pk[0:n, i, SH * half:SH * half + SH], start=(i == 0), stop=(i == 2))
            last.then_inc(M["xg_ps"], 1)

    def pack_act(act, l):
        M = ML[l]
        for g in range(6):
            i, half = g // 2, g % 2
            n = TILES[i][1]
            act.wait_ge(M["xt_ps"], g + 1)
            nc.scalar.copy(xth[0:n, i, 512 * half:512 * half + 512], ps[0:n, g % 4, :]).then_inc(M["xt_hi"], 1)
        for st in range(5):
            act.wait_ge(M["g_ps"], st + 1)
            nc.scalar.copy(gk[:, st, :], ps[:, 6 + st % 2, 0:T]).then_inc(M["g_ev"], 1)
        for g in range(0, 32, 2):
            k, half = g // 4, (g // 2) % 2
            act.wait_ge(M["xg_ps"], g + 1)
            nc.scalar.copy(xgh[:, k, SH * half:SH * half + SH], ps[:, g % 8, 0:SH]).then_inc(M["xg_hi"], 1)

    def pack_dve(dve, l, link):
        M = ML[l]
        dve.wait_ge(S["rc_in"], 16 * (l + 1))
        for i in range(3):
            p1, p2, w1, w2 = (rt[:, 13, i, c:c + 1] for c in (5, 6, 3, 4))
            nc.vector.tensor_scalar(pk[:, i, :], iota, p1, None, ALU.is_equal)
            nc.vector.tensor_scalar(pw[:, i, :], iota, p1, w1, ALU.is_equal, ALU.mult)
            link(nc.vector.tensor_scalar(gslot, iota, p2, w2, ALU.is_equal, ALU.mult))
            nc.vector.scalar_tensor_tensor(pk[:, i, :], iota, p2, pk[:, i, :], ALU.is_equal, ALU.add)
            last = nc.vector.tensor_tensor(pw[:, i, :], pw[:, i, :], gslot, ALU.add)
            if i < 2:
                link(last)
        last.then_inc(M["p_ready"], 1)
        for g in range(6):
            i, half = g // 2, g % 2
            n = TILES[i][1]
            dve.wait_ge(M["xt_hi"], g + 1)
            nc.vector.tensor_tensor(xtl[0:n, i, 512 * half:512 * half + 512], ps[0:n, g % 4, :],
                                    xth[0:n, i, 512 * half:512 * half + 512], ALU.subtract).then_inc(M["xt_ev"], 1)
        dve.wait_ge(M["gs_ps"], 1)
        nc.vector.tensor_copy(gcol, ps[:, 4, 0:5]).then_inc(M["gs_ready"], 1)
        for g in range(1, 32, 2):
            k, half = g // 4, (g // 2) % 2
            dve.wait_ge(M["xg_ps"], g + 1)
            nc.vector.tensor_copy(xgl[:, k, SH * half:SH * half + SH], ps[:, g % 8, 0:SH]).then_inc(M["xg_lo"], 1)

    def offset(eng, e):
        at = roff[0:1, e:e + 1] if isinstance(e, int) else roff[0:1, ds(e, 1)]
        return eng.value_load(at, min_val=0, max_val=2 * T)

    def moe_pack_pe(pe, l):
        M = ML[l]
        u0 = UNIT[f"moe{l}"][0]
        pack_pe(pe, l)
        pe.wait_ge(M["xg_hi"], 16)
        pe.wait_ge(M["xg_lo"], 16)

        def up(u, s, bank, at):
            pe.wait_ge(S["w_lo"], u * 2 + 2)
            for j in range(2):
                for k in range(KD):
                    last = mm3(ps[:, bank, CAP * j:CAP * j + CAP], s, k, 128 * j, xgh[:, k, ds(at, CAP)],
                               xgl[:, k, ds(at, CAP)], k == 0, k == KD - 1)
            last.then_inc(S["w_used"], 1)

        def down(u, s, bank):
            pe.wait_ge(S["w_lo"], u * 2 + 2)
            for e in range(2):
                for j in range(4):
                    for k in range(2):
                        c = CAP * (4 * e + j)
                        last = mm3(ps[:, bank, c:c + CAP], s, 2 * e + k, 128 * j, hh[:, 2 * e + k, 0:CAP],
                                   hl[:, 2 * e + k, 0:CAP], k == 0, k == 1, 512)
            last.then_inc(S["w_used"], 1)

        at = offset(pe, 0)
        up(u0, 0, 0, at)
        up(u0 + 1, 1, 1, at)
        at = offset(pe, 1)
        up(u0 + 2, 0, 2, at)
        up(u0 + 3, 1, 3, at)
        with pe.Fori(1, NE // 2) as i:
            u = i * 6 + (u0 - 2)
            at = offset(pe, i * 2)
            pe.wait_ge(M["b"], i * 2 - 1)
            up(u, 0, 0, at)
            up(u + 1, 1, 1, at)
            pe.wait_ge(M["hl"], i * 2)
            down(u + 2, 0, 4)
            down(u + 3, 1, 5)
            at = offset(pe, i * 2 + 1)
            pe.wait_ge(M["b"], i * 2)
            up(u + 4, 0, 2, at)
            pe.wait_ge(M["y"], i * 4)
            up(u + 5, 1, 3, at)
        pe.wait_ge(M["hl"], NE)
        down(u0 + 94, 0, 4)
        down(u0 + 95, 1, 5)
        pe.wait_ge(M["y"], 2 * NE)
        for g in range(10):
            st, half = g // 2, g % 2
            if g >= 4:
                pe.wait_ge(M["ys_lo"], g - 3)
            for j in range(4):
                last = nc.tensor.transpose(ps[:, g % 4, 128 * j:128 * j + 128],
                                           yc[:, 4 * half + j, 128 * st:128 * st + 128], ident)
            last.then_inc(M["ys_ps"], 1)
        pe.wait_ge(M["ys_lo"], 10)
        for k in range(KD):
            for st in range(5):
                for part in (ysh, ysl):
                    last = nc.tensor.matmul(ps[:, k, 0:T], part[:, st, 128 * k:128 * k + 128], gk[:, st, :],
                                            start=(st == 0 and part is ysh), stop=(st == 4 and part is ysl))
            last.then_inc(M["z_ps"], 1)

    def moe_pack_act(act, l, last_layer):
        M = ML[l]
        u0 = UNIT[f"moe{l}"][0]
        pack_act(act, l)

        def hi(u, s):
            act.wait_ge(S["w_used"], u + 1)
            split_hi(act, u + 2, s)

        def sig(n, bank):
            if not isinstance(n, int) or n >= 1:
                act.wait_ge(M["b"], n)
            nc.scalar.activation(e_t[:, :, 0:CAP], ps[:, bank, 0:2 * CAP].rearrange("p (a b) -> p a b", a=2),
                                 ACT.Tanh, scale=0.5 / WSCALE).then_inc(M["exp"], 1)

        def hid(n, j):
            act.wait_ge(M["b"], n + 1)
            nc.scalar.copy(hh[:, 2 * j:2 * j + 2, 0:CAP], cg[:, j, :, 0:CAP]).then_inc(M["hh"], 1)

        def out(p, half, at):
            for e in range(2):
                nc.scalar.mul(yc[:, 4 * half:4 * half + 4, ds(at[e], CAP)],
                              ps[:, 4 + half, 256 * e:256 * e + 256].rearrange("p (a b) -> p a b", a=4),
                              1 / WSCALE).then_inc(M["y"], 1)
                if e == 0:
                    act.wait_ge(M["y"], p * 4 + (2 * half + 1))

        hi(u0, 0)
        sig(0, 0)
        hi(u0 + 1, 1)
        hi(u0 + 2, 0)
        hid(0, 0)
        sig(1, 2)
        hi(u0 + 3, 1)
        with act.Fori(1, NE // 2) as i:
            u = i * 6 + (u0 - 2)
            n = i * 2
            at = [offset(act, i * 2 - 2), offset(act, i * 2 - 1)]
            hi(u, 0)
            hid(n - 1, 1)
            sig(n, 0)
            hi(u + 1, 1)
            hi(u + 2, 0)
            out(i - 1, 0, at)
            hi(u + 3, 1)
            out(i - 1, 1, at)
            hid(n, 0)
            hi(u + 4, 0)
            sig(n + 1, 2)
            hi(u + 5, 1)
        hid(NE - 1, 1)
        at = [offset(act, NE - 2), offset(act, NE - 1)]
        for half in range(2):
            if last_layer:
                act.wait_ge(S["w_used"], u0 + 95 + half)
            else:
                hi(u0 + 94 + half, half)
            out(NE // 2 - 1, half, at)
        for g in range(10):
            st, half = g // 2, g % 2
            act.wait_ge(M["ys_ps"], g + 1)
            nc.scalar.activation(ysh[:, st, 512 * half:512 * half + 512], ps[:, g % 4, :], ACT.Copy,
                                 scale=gcol[:, st:st + 1]).then_inc(M["ys_hi"], 1)

    def moe_pack_dve(dve, l, last_layer):
        M = ML[l]
        u0 = UNIT[f"moe{l}"][0]
        link = Chain(dve, M["chain"], M["loop"])
        pack_dve(dve, l, link)

        def lo(u, s):
            dve.wait_ge(S["w_used"], u + 1)
            split_lo(dve, u + 2, s)

        def act_fn(n, bank):
            dve.wait_ge(M["exp"], n + 1)
            ab = a_t[:, :, 0:CAP]
            g, u = (ps[:, bank + c, 0:2 * CAP].rearrange("p (a b) -> p a b", a=2) for c in range(2))
            link(nc.vector.scalar_tensor_tensor(ab, e_t[:, :, 0:CAP], 1.0, g, ALU.add, ALU.mult))
            nc.vector.scalar_tensor_tensor(cg[:, bank // 2, :, 0:CAP], u, 0.5 / WSCALE ** 2, ab, ALU.mult,
                                           ALU.mult).then_inc(M["b"], 1)

        def low(n, j):
            dve.wait_ge(M["hh"], n + 1)
            nc.vector.tensor_tensor(hl[:, 2 * j:2 * j + 2, 0:CAP], cg[:, j, :, 0:CAP],
                                    hh[:, 2 * j:2 * j + 2, 0:CAP], ALU.subtract).then_inc(M["hl"], 1)

        lo(u0, 0)
        lo(u0 + 1, 1)
        act_fn(0, 0)
        lo(u0 + 2, 0)
        low(0, 0)
        lo(u0 + 3, 1)
        act_fn(1, 2)
        with dve.Fori(1, NE // 2) as i:
            link.enter(i - 1, 2)
            u = i * 6 + (u0 - 2)
            n = i * 2
            lo(u, 0)
            low(n - 1, 1)
            lo(u + 1, 1)
            act_fn(n, 0)
            lo(u + 2, 0)
            lo(u + 3, 1)
            low(n, 0)
            lo(u + 4, 0)
            lo(u + 5, 1)
            act_fn(n + 1, 2)
        link.leave(NE // 2 - 1)
        low(NE - 1, 1)
        if not last_layer:
            lo(u0 + 94, 0)
            lo(u0 + 95, 1)
        for g in range(10):
            st, half = g // 2, g % 2
            dve.wait_ge(M["ys_hi"], g + 1)
            nc.vector.scalar_tensor_tensor(ysl[:, st, 512 * half:512 * half + 512], ps[:, g % 4, :],
                                           gcol[:, st:st + 1], ysh[:, st, 512 * half:512 * half + 512], ALU.mult,
                                           ALU.subtract).then_inc(M["ys_lo"], 1)
        for k in range(KD):
            dve.wait_ge(M["z_ps"], k + 1)
            last = nc.vector.tensor_tensor(xT[:, k, :], xT[:, k, :], ps[:, k, 0:T], ALU.add)
        last.then_inc(S["w_ev"], 96)
        dve.wait_ge(S["w_ev"], u0 + 96)
        nc.vector.memset(gslot[0:1, 0:1], 0.0).then_inc(S["moe_done"], 1)

    def moe(eng, l, packed, general, *args):
        eng.wait_ge(S["off_ready"], l + 1)
        fits = eng.value_load(roff[0:1, NE:NE + 1], min_val=0, max_val=1)
        with eng.If(fits > 0):
            packed(eng, l, *args)
        with eng.Else():
            general(eng, l, *args)

    def moe_pool(pool, l):
        pool.wait_ge(S["off_ready"], l + 1)
        fits = pool.value_load(roff[0:1, NE:NE + 1], min_val=0, max_val=1)
        with pool.If(fits < 1):
            moe_all_pool(pool, l)

    def pe_memory(pe, l):
        n = 1 + 3 * l
        norm_pe(pe, n)
        gemm_pe(pe, f"memq{l}", (3, 8)[l])
        pe.wait_ge(S["w_ev"], sum(UNIT[f"memq{l}"]))
        prompt_pe(pe, f"m{l}")
        batch_pe(pe, f"m{l}")
        pe.wait_ge(S["bpv_ev"], ATT[f"m{l}"]["batch0"] + 8)
        gemm_pe(pe, f"memo{l}", (4, 9)[l])
        norm_pe(pe, n + 1)
        pe.wait_ge(S["xn_ready"], 2 * n + 4)
        route_pe(pe, l)
        moe(pe, l, moe_pack_pe, moe_all_pe)

    def pe_rest(pe):
        pe.wait_ge(S["vec_in"], NVIN)
        pe_memory(pe, 0)
        norm_pe(pe, 3)
        gemm_pe(pe, "qkv", 6)
        rope_pe(pe)
        pe.wait_ge(S["tr_ev"], G_Y)
        prompt_pe(pe, "d")
        batch_pe(pe, "d")
        subln_pe(pe)
        pe.wait_ge(S["ostd_ready"], 2)
        gemm_pe(pe, "out_c", 7)
        pe_memory(pe, 1)
        norm_pe(pe, 6)
        pe.wait_ge(S["xn_ready"], 14)
        g = G_Y
        for i, (t0, n) in enumerate(TILES):
            for half in range(2):
                tr_pe(pe, g, [xn[:, 4 * half + j, t0:t0 + n] for j in range(4)], 128)
                g += 1

    def act_memory(act, link, l):
        n = 1 + 3 * l
        norm_act(act, n)
        input_act(act, xn[:], norm=n)
        gemm_copy_act(act, f"memq{l}", z[:, 0:8])
        prompt_act(act, f"m{l}")
        batch_act(act, f"m{l}")
        act.wait_ge(S["bpv_ev"], ATT[f"m{l}"]["batch0"] + 8)
        input_act(act, xn[:])
        gemm_split_act(act, f"memo{l}")
        act.wait_ge(S["w_ev"], sum(UNIT[f"memo{l}"]))
        norm_act(act, n + 1)
        input_act(act, xn[:], norm=n + 1)
        route_act(act, l)
        moe(act, l, moe_pack_act, moe_all_act, l == 1)

    def act_rest(act, link):
        act.wait_ge(S["w_ev"], sum(UNIT["out_a"]))
        act.wait_ge(S["out_c"], 16 * 10)
        act.wait_ge(c_out[0], 32)
        act.wait_ge(c_out[1], 32)
        act_memory(act, link, 0)
        act.wait_ge(S["moe_done"], 1)
        norm_act(act, 3)
        input_act(act, xn[:], norm=3)
        gemm_copy_act(act, "qkv", zc[:])
        act.wait_ge(S["lam_arg"], 1)
        nc.scalar.activation(lams[:, 2:4], lams[:, 0:2], ACT.Exp).then_inc(S["lam_exp"], 1)
        prompt_act(act, "d")
        batch_act(act, "d")
        subln_act(act, link)
        act.wait_ge(S["on_ready"], 1)
        input_act(act, xn[:])
        gemm_split_act(act, "out_c")
        act.wait_ge(S["w_ev"], sum(UNIT["out_c"]))
        act_memory(act, link, 1)
        act.wait_ge(S["moe_done"], 2)
        norm_act(act, 6)

    def dve_memory(dve, link, l):
        n = 1 + 3 * l
        norm_dve(dve, link, n)
        input_dve(dve, (3, 8)[l], xn[:])
        gemm_split_dve(dve, f"memq{l}")
        dve.wait_ge(S["w_ev"], sum(UNIT[f"memq{l}"]))
        prompt_dve(dve, link, f"m{l}")
        batch_dve(dve, link, f"m{l}")
        dve.wait_ge(S["bpv_ev"], ATT[f"m{l}"]["batch0"] + 8)
        input_dve(dve, (4, 9)[l], xn[:])
        gemm_add_dve(dve, f"memo{l}")
        norm_dve(dve, link, n + 1)
        input_dve(dve, (5, 10)[l], xn[:])
        route_dve(dve, link, l)
        moe(dve, l, moe_pack_dve, moe_all_dve, l == 1)
        dve.wait_ge(S["moe_done"], l + 1)

    def dve_rest(dve, link):
        dve_memory(dve, link, 0)
        norm_dve(dve, link, 3)
        input_dve(dve, 6, xn[:])
        gemm_split_dve(dve, "qkv")
        rope_dve(dve, link)
        prompt_dve(dve, link, "d")
        batch_dve(dve, link, "d")
        subln_dve(dve, link)
        input_dve(dve, 7, xn[:])
        gemm_add_dve(dve, "out_c")
        dve_memory(dve, link, 1)
        norm_dve(dve, link, 6)
        g = G_Y
        for i, (t0, n) in enumerate(TILES):
            for half in range(2):
                tr_dve(dve, g, x_nat[0:n, i, 512 * half:512 * half + 512].rearrange("p (a b) -> p a b", a=4), n, 128)
                g += 1

    def pool_rest(pool):
        pool.wait_ge(S["out_c"], 16 * 10)
        pool.wait_ge(c_out[0], 32)
        pool.wait_ge(c_out[1], 32)
        pool.wait_ge(S["in_lo"], 6)
        batch_pool(pool, "m0")
        pool.wait_ge(S["in_lo"], 10)
        pool.dma_start(rc, a["slots"]).then_inc(S["rc_in"], 16)
        moe_pool(pool, 0)
        rope_pool(pool)
        pool.wait_ge(S["tr_ev"], G_Y)
        pool.dma_start(o["p_k"][0, 0].rearrange("(t p) h m d -> p t (h m d)", p=128), ktok3[:, 0:2, :]
                       ).then_inc(S["out_p"], 16)
        pool.dma_start(o["s_k"][0].rearrange("b i h m d -> (b i) (h m d)"), ktok3[0:64, 2, :]).then_inc(S["out_p"], 16)
        pool.dma_start(o["p_v"][0, 0].rearrange("(t p) h d -> p t (h d)", p=128), vtok3[:, 0:2, :]
                       ).then_inc(S["out_p"], 16)
        pool.dma_start(o["s_v"][0].rearrange("b i h d -> (b i) (h d)"), vtok3[0:64, 2, :]).then_inc(S["out_p"], 16)
        pool.wait_ge(S["out_p"], 64)
        batch_pool(pool, "d")
        pool.wait_ge(S["in_lo"], 16)
        batch_pool(pool, "m1")
        pool.wait_ge(S["in_lo"], 20)
        pool.dma_start(rc, a["slots"]).then_inc(S["rc_in"], 16)
        moe_pool(pool, 1)
        pool.wait_ge(S["tr_ev"], G_Y + 6)
        pool.dma_start(o["y_prompt"][0].rearrange("(t p) d -> p t d", p=128), x_nat[:, 0:2, :]).then_inc(S["out_y"], 16)
        pool.dma_start(o["y_sample"].rearrange("b i d -> (b i) d"), x_nat[0:64, 2, :]).then_inc(S["out_y"], 16)
        pool.wait_ge(S["out_y"], 32)

    @block.gpsimd
    def _(pool):
        nc.gpsimd.memset(ones[:], 1.0)
        nc.gpsimd.memset(wgate[:], 0.0)
        nc.gpsimd.memset(epsc[:, 0:1], EPS)
        nc.gpsimd.memset(epsc[:, 1:2], 1.0).then_inc(S["cst_ready"], 1)
        pool.dma_start(cst[:], a["consts"]).then_inc(S["const_in"], 16)
        pool.dma_start(mem_nat, a["mem_prompt"][0].rearrange("(t p) d -> p t d", p=128)).then_inc(S["mem_in"], 16)
        pool.dma_start(x_nat[:, 0:2, :], a["x_prompt"][0].rearrange("(t p) d -> p t d", p=128)
                       ).then_inc(S["x_in"], 16)
        pool.dma_start(x_nat[0:64, 2, :], a["x_sample"].rearrange("b i d -> (b i) d")).then_inc(S["x_in"], 16)
        r = 0
        for name in ("norm_mix_g", "norm_mem_g", "norm_ffn_g"):
            pool.dma_start(vecs[r:r + 16, :], a[name].rearrange("l (k p) -> (l k) p", p=128)
                           ).then_inc(S["vec_in"], 16)
            r += 16
        pool.dma_start(vecs[r:r + 8, :], a["final_norm_g"].rearrange("(k p) -> k p", p=128)
                       ).then_inc(S["vec_in"], 16)
        pool.dma_start(vecs[r + 8:r + 12, :], a["head_norm_g_a"][0].rearrange("(k p) -> k p", p=128)
                       ).then_inc(S["vec_in"], 16)
        pool.dma_start(vecs[r + 12:r + 13, :], a["subln_g_c"]).then_inc(S["vec_in"], 16)
        pool.dma_start(vecs[r + 13:r + 25, :], a["conv_w_b"][0].rearrange("j (k p) -> (j k) p", p=128)
                       ).then_inc(S["vec_in"], 16)
        pool.dma_start(ptab[:], a["page_table"].rearrange("b n -> (b n)").unsqueeze(0)).then_inc(S["tab_in"], 16)
        pool.wait_ge(S["tab_in"], 16)
        pool.wait_ge(S["cst_ready"], 1)
        wg = a["w_in_a"][0].rearrange("(k p) n -> p k n", p=128)
        pool.dma_start(wgate[:, :, 0:4], wg[:, :, 2048:2052]).then_inc(S["gate_in"], 16)
        pool.dma_start(wgate[:, :, 32:36], wg[:, :, 2052:2056]).then_inc(S["gate_in"], 16)
        pool.dma_start(gbias[0:4, :], a["gate_b_a"][0, 0].rearrange("(h o) -> h o", o=1)).then_inc(S["vec_in"], 16)
        pool.dma_start(gbias[32:36, :], a["gate_b_a"][0, 1].rearrange("(h o) -> h o", o=1)
                       ).then_inc(S["vec_in"], 16)
        for l in range(2):
            pool.dma_start(wrt[:, l, :, 0:4], a["w_router_g"][l].rearrange("(k p) n -> p k n", p=128)
                           ).then_inc(S["vec_in"], 16)
            pool.dma_start(wrt[:, l, :, 4:36], a["w_router_e"][l].rearrange("(k p) n -> p k n", p=128)
                           ).then_inc(S["vec_in"], 16)
            pool.dma_start(brt[:, l, 0:4], a["b_router_g"][l].partition_broadcast(128)).then_inc(S["vec_in"], 16)
            pool.dma_start(brt[:, l, 4:36], a["b_router_e"][l].partition_broadcast(128)).then_inc(S["vec_in"], 16)
        pool.dma_start(lamv[:], a["lambda_c"][0].rearrange("a b -> (a b)").partition_broadcast(128)
                       ).then_inc(S["vec_in"], 16)
        for l in range(2):
            pool.wait_ge(S["tr_ev"], G_MKV + 8 * l + 4)
            pool.dma_start(o["p_mem_k"][l, 0].rearrange("(t p) h d -> p t (h d)", p=128), mk_out
                           ).then_inc(S["out_mem"], 16)
            pool.wait_ge(S["tr_ev"], G_MKV + 8 * l + 8)
            pool.dma_start(o["p_mem_v"][l, 0].rearrange("(t p) h d -> p t (h d)", p=128), memv[:, l]
                           ).then_inc(S["out_mem"], 16)
        pool.wait_ge(S["out_mem"], 64)
        pool.wait_ge(S["in_lo"], 4)
        mlstm_pool(pool)
        mlstm_pool_out(pool)
        pool_rest(pool)

    @block.tensor
    def _(pe):
        pe.wait_ge(S["const_in"], 16)
        pe.wait_ge(S["cst_ready"], 1)
        g = G_X
        pe.wait_ge(S["x_in"], 32)
        for i, (t0, n) in enumerate(TILES):
            for half in range(2):
                tr_pe(pe, g, [x_nat[0:n, i, 512 * half + 128 * j:512 * half + 128 * j + 128] for j in range(4)], n)
                g += 1
        pe.wait_ge(S["mem_in"], 16)
        for i in range(2):
            for half in range(2):
                tr_pe(pe, g, [mem_nat[:, i, 512 * half + 128 * j:512 * half + 128 * j + 128] for j in range(4)], 128)
                g += 1
        pe.wait_ge(S["vec_in"], NVIN)
        pe.wait_ge(S["tr_ev"], G_MKV)
        nc.tensor.transpose(ps[:, 4, 0:NVEC], vecs[:], ident[0:NVEC, 0:NVEC]).then_inc(S["vec_ps"], 1)
        pe.wait_ge(S["vec_ev"], 1)
        for l in range(2):
            for kv in range(2):
                name = ("memk", "memv")[kv] + str(l)
                gemm_pe(pe, name, 0, 256)
                pe.wait_ge(S["w_ev"], sum(UNIT[name]))
                src = memkT[:, l] if kv == 0 else mvT
                for i in range(2):
                    for half in range(2):
                        tr_pe(pe, g, [src[:, 4 * half + j, 128 * i:128 * i + 128] for j in range(4)], 128)
                        g += 1
        pe.wait_ge(S["tr_ev"], g)
        norm_pe(pe, 0)
        pe.wait_ge(S["xn_ready"], 2)
        mlstm_pe(pe)
        gemm_pe(pe, "out_a", 2)
        pe_rest(pe)

    @block.scalar
    def _(act):
        link = Chain(act, S["act_chain"], None)
        for s in range(2):
            split_hi(act, s, s)
        act.wait_ge(S["tr_ev"], G_MKV)
        input_act(act, sq[:, :, 0:256], 256)
        for l in range(2):
            gemm_copy_act(act, f"memk{l}", memkT[:, l], 256)
            if l:
                act.wait_ge(S["tr_ps"], G_MKV + 8)
            gemm_copy_act(act, f"memv{l}", mvT, 256)
        act.wait_ge(S["in_lo"], 2)
        norm_act(act, 0)
        input_act(act, xn[:], norm=0)
        act.wait_ge(S["out_mem"], 64)
        gemm_copy_act(act, "in_a", z[:, 0:16])
        gemm_copy_act(act, "in_b", z[:, 16:28])
        mlstm_act(act, link)
        act.wait_ge(S["y_ready"], 1)
        input_act(act, xn[:])
        gemm_split_act(act, "out_a")
        act_rest(act, link)

    @block.vector
    def _(dve):
        link = Chain(dve, S["dve_chain"], S["dve_loop"])
        dve.wait_ge(S["const_in"], 16)
        nc.vector.tensor_copy(maskb[:], cst[:, m0:m0 + 768])
        link(nc.vector.tensor_copy(identb[:], ident))
        for s in range(2):
            split_lo(dve, s, s)
        g = G_X
        for i, (t0, n) in enumerate(TILES):
            for half in range(2):
                tr_dve(dve, g, xT[:, 4 * half:4 * half + 4, t0:t0 + n], 128, n)
                g += 1
        for i in range(2):
            for half in range(2):
                tr_dve(dve, g, sq[:, 4 * half:4 * half + 4, 128 * i:128 * i + 128], 128, 128)
                g += 1
        dve.wait_ge(S["vec_ps"], 1)
        nc.vector.tensor_copy(vec[:], ps[:, 4, 0:NVEC]).then_inc(S["vec_ev"], 1)
        dve.wait_ge(S["tr_ev"], G_MKV)
        input_dve(dve, 0, sq[:, :, 0:256], 256)
        for l in range(2):
            for kv in range(2):
                gemm_split_dve(dve, ("memk", "memv")[kv] + str(l))
                if kv == 0 and l == 1:
                    dve.wait_ge(S["out_mem"], 32)
                for i in range(2):
                    for half in range(2):
                        dst = mk_out if kv == 0 else memv[:, l]
                        tr_dve(dve, g, dst[:, i, 512 * half:512 * half + 512].rearrange("p (a b) -> p a b", a=4),
                               128, 128)
                        g += 1
        norm_dve(dve, link, 0)
        input_dve(dve, 1, xn[:])
        gemm_split_dve(dve, "in_a")
        gemm_split_dve(dve, "in_b")
        mlstm_dve(dve, link)
        input_dve(dve, 2, xn[:])
        gemm_add_dve(dve, "out_a")
        dve_rest(dve, link)



_INS = ['x_prompt', 'x_sample', 'state_mlstm_C', 'state_mlstm_n', 'state_mlstm_m', 'state_conv', 'cache_k', 'cache_v',
        'page_table', 'cache_mem_k', 'cache_mem_v', 'mem_prompt', 'norm_mix_g', 'norm_mem_g', 'norm_ffn_g',
        'final_norm_g', 'w_in_a', 'gate_b_a', 'head_norm_g_a', 'conv_w_b', 'w_out_a', 'w_qkv_c', 'lambda_c',
        'subln_g_c', 'w_out_c', 'w_mem_q', 'w_mem_k', 'w_mem_v', 'w_mem_o', 'w_router_g', 'b_router_g', 'w_router_e',
        'b_router_e', 'w_exp_gate', 'w_exp_up', 'w_exp_down']
_OUTS = [("y_prompt", (1, 256, 1024)), ("y_sample", (8, 8, 1024)), ("p_C", (1, 1, 4, 128, 128)),
         ("p_n", (1, 1, 4, 128)), ("p_m", (1, 1, 4)), ("p_conv", (1, 1, 2, 512)), ("p_k", (1, 1, 256, 8, 2, 64)),
         ("p_v", (1, 1, 256, 8, 128)), ("p_mem_k", (2, 1, 256, 4, 256)), ("p_mem_v", (2, 1, 256, 4, 256)),
         ("s_C", (1, 8, 4, 128, 128)), ("s_n", (1, 8, 4, 128)), ("s_m", (1, 8, 4)), ("s_conv", (1, 8, 2, 512)),
         ("s_k", (1, 8, 8, 8, 2, 64)), ("s_v", (1, 8, 8, 8, 128))]


def kernel(**inputs):
    import concourse.bacc as bacc
    from concourse import mybir
    from concourse.bass_utils import run_bass_kernel_spmd

    nc = bacc.Bacc("TRN2", target_bir_lowering=False, num_devices=1)
    arrays = {f"in_{n}": np.ascontiguousarray(inputs[n]) for n in _INS}
    arrays["in_consts"] = constants()
    arrays["in_slots"] = slot_constants()
    a = {n[3:]: nc.dram_tensor(n, v.shape, mybir.dt.from_np(v.dtype), kind="ExternalInput").ap()
         for n, v in arrays.items()}
    o = {n: nc.dram_tensor(f"out_{n}", s, mybir.dt.float32, kind="ExternalOutput").ap() for n, s in _OUTS}
    build(nc, a, o)
    r = run_bass_kernel_spmd(nc, [arrays], core_ids=[0])
    return tuple(r.results[0][f"out_{n}"] for n, _ in _OUTS)
```
